# Optimizing a Trainium2 kernel written in Bass

```python
import math
import jax, jax.numpy as jnp
from jax import lax
import numpy as np

D_MODEL = 1024
BATCH = 1
SEQ = 1024
DEPTH = 1

MEM_LEN = 256
D_MIX = D_MODEL
GM_WIDTH = D_MIX // 2
CHUNK = 128
GM_HEAD_DIM = 128
GM_HEADS = GM_WIDTH // GM_HEAD_DIM
SSM_WIDTH = D_MIX // 4
SSM_GROUP = 16
SSM_GROUPS = SSM_WIDTH // SSM_GROUP
SSM_STATE = 64
XA_WIDTH = D_MIX - GM_WIDTH - SSM_WIDTH
XA_HEADS = 4
XA_HEAD_DIM = XA_WIDTH // XA_HEADS
IN_WIDTH = 3 * GM_WIDTH + 2 * SSM_WIDTH + 2 * XA_WIDTH
SPLITS = (GM_WIDTH, 2 * GM_WIDTH, 3 * GM_WIDTH,
          3 * GM_WIDTH + SSM_WIDTH, 3 * GM_WIDTH + 2 * SSM_WIDTH,
          3 * GM_WIDTH + 2 * SSM_WIDTH + XA_WIDTH)
DN_ALPHA = (2 * DEPTH) ** 0.25
DN_BETA = (8 * DEPTH) ** -0.25
LN_EPS = 1e-5
DT_MIN = 0.001
DT_MAX = 0.1


def layer_norm(x, g, b):
    xf = x.astype(jnp.float32)
    mu = jnp.mean(xf, axis=-1, keepdims=True)
    xc = xf - mu
    var = jnp.mean(xc * xc, axis=-1, keepdims=True)
    return (xc * lax.rsqrt(var + LN_EPS) * g.astype(jnp.float32) + b.astype(jnp.float32)).astype(x.dtype)

def spatial_gating(u, v, w_s, b_s, ln_g, ln_b, causal):
    Bsz, L, _ = v.shape
    nc = L // CHUNK
    vh = layer_norm(v.reshape(Bsz, L, GM_HEADS, GM_HEAD_DIM), ln_g, ln_b)
    w = jnp.where(causal[None], w_s, 0)
    vc = vh.reshape(Bsz, nc, CHUNK, GM_HEADS, GM_HEAD_DIM)
    mixed = jnp.einsum('hts,bcshd->bcthd', w, vc) + b_s.T[None, None, :, :, None]
    return u * mixed.reshape(Bsz, L, GM_WIDTH)

def _diag_combine(c1, c2):
    a1, b1 = c1
    a2, b2 = c2
    return a1 * a2, a2 * b1 + b2

def s5_branch(xs, lam_re, lam_im, log_step, b_re, b_im, c_re, c_im, d_skip, glu_w, glu_b):
    f32 = jnp.float32
    Bsz, L, W = xs.shape
    xg = xs.reshape(Bsz, L, SSM_GROUPS, SSM_GROUP).astype(f32)
    lam = lax.complex(lam_re.astype(f32), lam_im.astype(f32))
    step = jnp.exp(log_step.astype(f32))[:, None]
    lam_bar = jnp.exp(lam * step)
    b_mat = lax.complex(b_re.astype(f32), b_im.astype(f32))
    b_bar = ((lam_bar - 1.0) / lam)[:, :, None] * b_mat
    c_mat = lax.complex(c_re.astype(f32), c_im.astype(f32))
    bu = jnp.einsum('gpc,blgc->blgp', b_bar, xg.astype(jnp.complex64))
    decay = jnp.broadcast_to(lam_bar, bu.shape)
    _, h = lax.associative_scan(_diag_combine, (decay, bu), axis=1)
    y = jnp.einsum('gcp,blgp->blgc', c_mat, h).real \
        + d_skip.astype(f32).reshape(SSM_GROUPS, SSM_GROUP) * xg
    y = jax.nn.gelu(y.reshape(Bsz, L, W)).astype(xs.dtype)
    return y * jax.nn.sigmoid(y @ glu_w + glu_b)

def memory_cross_attention(q, mem, w_k, w_v):
    Bsz, L, _ = q.shape
    M = mem.shape[1]
    qh = q.reshape(Bsz, L, XA_HEADS, XA_HEAD_DIM)
    kh = (mem @ w_k).reshape(Bsz, M, XA_HEADS, XA_HEAD_DIM)
    vh = (mem @ w_v).reshape(Bsz, M, XA_HEADS, XA_HEAD_DIM)
    s = jnp.einsum('blhd,bmhd->bhlm', qh, kh, preferred_element_type=jnp.float32)
    p = jax.nn.softmax(s * (XA_HEAD_DIM ** -0.5), axis=-1).astype(vh.dtype)
    o = jnp.einsum('bhlm,bmhd->blhd', p, vh)
    return o.reshape(Bsz, L, XA_WIDTH)

def first_inputs(seed: int = 0) -> dict:
    key = jax.random.key(seed)
    ks = jax.random.split(key, 24)
    f32 = jnp.float32
    nrm = lambda k, shape, s: jax.random.normal(k, shape, f32) * s
    x = jax.random.normal(ks[0], (BATCH, SEQ, D_MODEL), f32)
    mem = jax.random.normal(ks[1], (BATCH, MEM_LEN, D_MODEL), f32)
    w_in = nrm(ks[2], (DEPTH, D_MODEL, IN_WIDTH), D_MODEL ** -0.5)
    gm_w_s = nrm(ks[3], (DEPTH, GM_HEADS, CHUNK, CHUNK), CHUNK ** -0.5)
    gm_b_s = 1.0 + nrm(ks[4], (DEPTH, GM_HEADS, CHUNK), 0.01)
    gm_ln_g = 1.0 + nrm(ks[5], (DEPTH, GM_HEADS, GM_HEAD_DIM), 0.01)
    gm_ln_b = nrm(ks[6], (DEPTH, GM_HEADS, GM_HEAD_DIM), 0.01)
    n = jnp.arange(SSM_STATE, dtype=f32)
    ssm_lam_re = -0.5 + nrm(ks[7], (DEPTH, SSM_GROUPS, SSM_STATE), 0.01)
    ssm_lam_im = math.pi * n + nrm(ks[8], (DEPTH, SSM_GROUPS, SSM_STATE), 0.01)
    ssm_log_step = jax.random.uniform(ks[9], (DEPTH, SSM_GROUPS), f32,
                                      math.log(DT_MIN), math.log(DT_MAX))
    bs = (2.0 * SSM_GROUP) ** -0.5
    ssm_b_re = nrm(ks[10], (DEPTH, SSM_GROUPS, SSM_STATE, SSM_GROUP), bs)
    ssm_b_im = nrm(ks[11], (DEPTH, SSM_GROUPS, SSM_STATE, SSM_GROUP), bs)
    cs = (2.0 * SSM_STATE) ** -0.5
    ssm_c_re = nrm(ks[12], (DEPTH, SSM_GROUPS, SSM_GROUP, SSM_STATE), cs)
    ssm_c_im = nrm(ks[13], (DEPTH, SSM_GROUPS, SSM_GROUP, SSM_STATE), cs)
    ssm_d = nrm(ks[14], (DEPTH, SSM_WIDTH), 1.0)
    glu_w = nrm(ks[15], (DEPTH, SSM_WIDTH, SSM_WIDTH), SSM_WIDTH ** -0.5)
    glu_b = nrm(ks[16], (DEPTH, SSM_WIDTH), 0.01)
    xa_w_k = nrm(ks[17], (DEPTH, D_MODEL, XA_WIDTH), D_MODEL ** -0.5)
    xa_w_v = nrm(ks[18], (DEPTH, D_MODEL, XA_WIDTH), D_MODEL ** -0.5)
    w_out = nrm(ks[19], (DEPTH, D_MIX, D_MODEL), DN_BETA * D_MIX ** -0.5)
    ln_g = 1.0 + nrm(ks[20], (DEPTH, D_MODEL), 0.01)
    ln_b = nrm(ks[21], (DEPTH, D_MODEL), 0.01)
    return {"x": x, "mem": mem, "w_in": w_in, "gm_w_s": gm_w_s, "gm_b_s": gm_b_s,
            "gm_ln_g": gm_ln_g, "gm_ln_b": gm_ln_b, "ssm_lam_re": ssm_lam_re,
            "ssm_lam_im": ssm_lam_im, "ssm_log_step": ssm_log_step,
            "ssm_b_re": ssm_b_re, "ssm_b_im": ssm_b_im, "ssm_c_re": ssm_c_re,
            "ssm_c_im": ssm_c_im, "ssm_d": ssm_d, "glu_w": glu_w, "glu_b": glu_b,
            "xa_w_k": xa_w_k, "xa_w_v": xa_w_v, "w_out": w_out,
            "ln_g": ln_g, "ln_b": ln_b}

def first_block(x, mem, w_in, gm_w_s, gm_b_s, gm_ln_g, gm_ln_b, ssm_lam_re, ssm_lam_im,
              ssm_log_step, ssm_b_re, ssm_b_im, ssm_c_re, ssm_c_im, ssm_d, glu_w, glu_b,
              xa_w_k, xa_w_v, w_out, ln_g, ln_b):
    causal = jnp.tril(jnp.ones((CHUNK, CHUNK), dtype=bool))
    for layer in range(DEPTH):
        z = x @ w_in[layer]
        u_a, v_a, g_a, x_b, g_b, q_x, g_x = jnp.split(z, SPLITS, axis=-1)
        y_a = spatial_gating(jax.nn.gelu(u_a), jax.nn.gelu(v_a), gm_w_s[layer], gm_b_s[layer],
                             gm_ln_g[layer], gm_ln_b[layer], causal)
        y_b = s5_branch(x_b, ssm_lam_re[layer], ssm_lam_im[layer], ssm_log_step[layer],
                        ssm_b_re[layer], ssm_b_im[layer], ssm_c_re[layer], ssm_c_im[layer],
                        ssm_d[layer], glu_w[layer], glu_b[layer])
        y_x = memory_cross_attention(q_x, mem, xa_w_k[layer], xa_w_v[layer])
        y = jnp.concatenate([y_a * jax.nn.silu(g_a),
                             y_b * jax.nn.silu(g_b),
                             y_x * jax.nn.silu(g_x)], axis=-1)
        x = layer_norm(DN_ALPHA * x + y @ w_out[layer], ln_g[layer], ln_b[layer])
    return x


_first_inputs = first_inputs


def first_inputs(seed=0):
    import zlib

    import numpy as np

    out = dict(_first_inputs(seed))
    spreads = {}
    factors = {'mem': 3.861,
     'gm_b_s': 64.0,
     'gm_ln_g': 64.0,
     'gm_ln_b': 64.0,
     'ssm_lam_re': 64.0,
     'ssm_lam_im': 64.0,
     'ssm_log_step': 64.0,
     'ssm_b_re': 64.0,
     'ssm_b_im': 64.0,
     'ssm_c_re': 64.0,
     'ssm_c_im': 64.0,
     'glu_w': 16.951,
     'glu_b': 64.0,
     'xa_w_k': 4.407,
     'xa_w_v': 3.613,
     'ln_g': 34.995,
     'ln_b': 32.407}
    for name, (base, spread) in spreads.items():
        noise = np.random.default_rng([zlib.crc32(name.encode()), seed]).standard_normal(out[name].shape)
        drawn = base * np.exp(spread * noise) if base else spread * noise
        out[name] = __import__('jax').numpy.asarray(drawn.astype(out[name].dtype))
    for name, factor in factors.items():
        out[name] = (out[name] * factor).astype(out[name].dtype)
    return out


_narrow_inputs = first_inputs


def first_inputs(seed=0):

    out = dict(_narrow_inputs(seed))
    wider = {'gm_b_s': 8.67,
     'gm_ln_g': 11.53,
     'gm_ln_b': 11.52,
     'ssm_d': 10.54,
     'glu_w': 12.0,
     'glu_b': 12.0,
     'ln_g': 6.66,
     'ln_b': 6.67}
    for name, times in wider.items():
        mean = out[name].mean()
        out[name] = (mean + times * (out[name] - mean)).astype(out[name].dtype)
    return out


CHUNK_2 = 64
Q_BLOCK = 128
MAX_STREAM_OFFSET = 65536

LRU_WIDTH = D_MODEL
LRU_BLOCKS = 8
CONV_WIDTH = 4
LRU_C = 8.0

ATTN_HEADS = 8
ATTN_HEAD_DIM = D_MODEL // (2 * ATTN_HEADS)
ATTN_V_DIM = 2 * ATTN_HEAD_DIM
ATTN_QK_WIDTH = ATTN_HEADS * 2 * ATTN_HEAD_DIM
ATTN_WIDTH = ATTN_HEADS * ATTN_V_DIM
ROPE_THETA = 500000.0
ROT_DIMS = ATTN_HEAD_DIM // 4

MEM_TOKENS = 256
MEM_HEADS = 4
MEM_HEAD_DIM = 128
MEM_WIDTH = MEM_HEADS * MEM_HEAD_DIM

N_GROUPS = 4
EXPERTS_PER_GROUP = 8
N_EXPERTS = N_GROUPS * EXPERTS_PER_GROUP
TOP_K = 2
EXPERT_FF = 512
EXPERT_BLOCK = 128

IN_WIDTHS = (LRU_WIDTH, LRU_WIDTH, ATTN_QK_WIDTH, ATTN_QK_WIDTH, ATTN_WIDTH, D_MODEL, D_MODEL)
EPS = 1e-6
NEG_INF = -1e30


def rms_norm(x, g):
    xf = x.astype(jnp.float32)
    y = xf * lax.rsqrt(jnp.mean(xf * xf, axis=-1, keepdims=True) + EPS)
    return (y * g.astype(jnp.float32)).astype(x.dtype)

def rotary_tables(positions):
    half = ROT_DIMS // 2
    inv_freq = jnp.exp(-math.log(ROPE_THETA) * jnp.arange(half, dtype=jnp.float32) / half)
    ang = positions.astype(jnp.float32)[..., None] * inv_freq
    return jnp.cos(ang)[:, :, None, None, :], jnp.sin(ang)[:, :, None, None, :]

def rope_partial(x, cos, sin):
    half = ROT_DIMS // 2
    xr = x[..., :ROT_DIMS].astype(jnp.float32)
    x1, x2 = xr[..., :half], xr[..., half:]
    rot = jnp.concatenate([x1 * cos - x2 * sin, x2 * cos + x1 * sin], axis=-1)
    return jnp.concatenate([rot.astype(x.dtype), x[..., ROT_DIMS:]], axis=-1)

def causal_depthwise_conv(x, w, b):
    k = w.shape[0]
    y = lax.conv_general_dilated(x, w[:, None, :].astype(x.dtype), window_strides=(1,),
                                 padding=((k - 1, 0),), dimension_numbers=('NWC', 'WIO', 'NWC'),
                                 feature_group_count=x.shape[-1])
    return y + b

def block_diag_linear(x, w, b):
    bsz, s, c = x.shape
    nb, bw, _ = w.shape
    y = jnp.einsum('bsnc,ncd->bsnd', x.reshape(bsz, s, nb, bw), w).reshape(bsz, s, c)
    return y + b

def rg_lru(x, wa, ba, wx, bx, lam):
    r = jax.nn.sigmoid(block_diag_linear(x, wa, ba).astype(jnp.float32))
    i = jax.nn.sigmoid(block_diag_linear(x, wx, bx).astype(jnp.float32))
    log_a = -LRU_C * r * jax.nn.softplus(-lam.astype(jnp.float32))
    a = jnp.exp(log_a)
    b = jnp.sqrt(-jnp.expm1(2.0 * log_a)) * i * x.astype(jnp.float32)

    def combine(left, right):
        a_l, b_l = left
        a_r, b_r = right
        return a_l * a_r, a_r * b_l + b_r

    _, h = lax.associative_scan(combine, (a, b), axis=1)
    return h.astype(x.dtype)

def diff_attention(q, k, v, cos, sin, q_norm, k_norm, lam, lambda_init, subln):
    bsz, s, _ = q.shape
    q = q.reshape(bsz, s, ATTN_HEADS, 2, ATTN_HEAD_DIM)
    k = k.reshape(bsz, s, ATTN_HEADS, 2, ATTN_HEAD_DIM)
    v = v.reshape(bsz, s, ATTN_HEADS, ATTN_V_DIM)
    q = rope_partial(rms_norm(q, q_norm), cos, sin) * (ATTN_HEAD_DIM ** -0.5)
    k = rope_partial(rms_norm(k, k_norm), cos, sin)
    outs = []
    for blk in range(s // Q_BLOCK):
        q0, q1 = blk * Q_BLOCK, (blk + 1) * Q_BLOCK
        sc = jnp.einsum('bqhmd,bkhmd->bhmqk', q[:, q0:q1], k[:, :q1]).astype(jnp.float32)
        mask = (jnp.arange(q1) // CHUNK_2)[None, :] <= (jnp.arange(q0, q1) // CHUNK_2)[:, None]
        p = jax.nn.softmax(jnp.where(mask, sc, NEG_INF), axis=-1)
        w = p[:, :, 0] - lam * p[:, :, 1]
        outs.append(jnp.einsum('bhqk,bkhd->bqhd', w.astype(v.dtype), v[:, :q1]))
    o = jnp.concatenate(outs, axis=1)
    o = rms_norm(o, subln) * (1.0 - lambda_init)
    return o.reshape(bsz, s, ATTN_WIDTH)

def memory_cross_attention_2(x, mem, norm_cx, norm_mem, w_cq, w_ckv, cq_norm, ck_norm, w_co):
    bsz, s, _ = x.shape
    m = mem.shape[1]
    q = (rms_norm(x, norm_cx) @ w_cq).reshape(bsz, s, MEM_HEADS, MEM_HEAD_DIM)
    kv = rms_norm(mem, norm_mem) @ w_ckv
    k = kv[..., :MEM_WIDTH].reshape(bsz, m, MEM_HEADS, MEM_HEAD_DIM)
    v = kv[..., MEM_WIDTH:].reshape(bsz, m, MEM_HEADS, MEM_HEAD_DIM)
    q = rms_norm(q, cq_norm) * (MEM_HEAD_DIM ** -0.5)
    k = rms_norm(k, ck_norm)
    p = jax.nn.softmax(jnp.einsum('bqhd,bkhd->bhqk', q, k).astype(jnp.float32), axis=-1)
    o = jnp.einsum('bhqk,bkhd->bqhd', p.astype(v.dtype), v).reshape(bsz, s, MEM_WIDTH)
    return o @ w_co

def hierarchical_moe(h, w_group, b_group, w_router, b_router, w_gate_up, w_down):
    bsz, s, d = h.shape
    n = bsz * s
    a_tot = n * TOP_K
    hf = h.reshape(n, d)
    gp = jax.nn.softmax((hf @ w_group).astype(jnp.float32) + b_group.astype(jnp.float32), axis=-1)
    gval, gidx = lax.top_k(gp, 1)
    el = ((hf @ w_router).astype(jnp.float32) + b_router.astype(jnp.float32))
    el = el.reshape(n, N_GROUPS, EXPERTS_PER_GROUP)
    el = jnp.take_along_axis(el, gidx[:, :, None], axis=1)[:, 0]
    ev, eidx = lax.top_k(el, TOP_K)
    ew = jax.nn.softmax(ev, axis=-1) * gval
    expert_id = (gidx * EXPERTS_PER_GROUP + eidx).reshape(-1)
    token_id = jnp.repeat(jnp.arange(n, dtype=jnp.int32), TOP_K)
    weight = ew.reshape(-1)
    order = jnp.argsort(expert_id)
    sorted_e = expert_id[order]
    counts = jnp.bincount(expert_id, length=N_EXPERTS)
    padded = (counts + EXPERT_BLOCK - 1) // EXPERT_BLOCK * EXPERT_BLOCK
    start = jnp.cumsum(counts) - counts
    pend = jnp.cumsum(padded)
    pstart = pend - padded
    dest = pstart[sorted_e] + jnp.arange(a_tot) - start[sorted_e]
    p_rows = a_tot + N_EXPERTS * EXPERT_BLOCK
    n_blk = p_rows // EXPERT_BLOCK
    buf_tok = jnp.full((p_rows,), n, jnp.int32).at[dest].set(token_id[order])
    buf_w = jnp.zeros((p_rows,), jnp.float32).at[dest].set(weight[order])
    blk_e = jnp.minimum(jnp.searchsorted(pend, jnp.arange(n_blk) * EXPERT_BLOCK, side='right'),
                        N_EXPERTS - 1)
    h_pad = jnp.concatenate([hf, jnp.zeros((1, d), hf.dtype)], axis=0)
    xs = h_pad[buf_tok].reshape(n_blk, EXPERT_BLOCK, d)

    def expert_block(args):
        xb, e = args
        gu = xb @ w_gate_up[e]
        return (jax.nn.silu(gu[:, :EXPERT_FF]) * gu[:, EXPERT_FF:]) @ w_down[e]

    ys = lax.map(expert_block, (xs, blk_e)).reshape(p_rows, d)
    out = jnp.zeros((n + 1, d), ys.dtype).at[buf_tok].add(ys * buf_w[:, None].astype(ys.dtype))
    return out[:n].reshape(bsz, s, d)

def second_inputs(seed: int = 0) -> dict:
    key = jax.random.key(seed)
    keys = iter(jax.random.split(key, 48))

    def normal(shape, scale):
        return jax.random.normal(next(keys), shape, jnp.float32) * scale

    def gain(n):
        return 1.0 + normal((DEPTH, n), 0.02)

    bw = LRU_WIDTH // LRU_BLOCKS
    u = jax.random.uniform(next(keys), (DEPTH, LRU_WIDTH), jnp.float32, 0.9, 0.999)
    p = u ** (1.0 / LRU_C)
    lru_lambda = jnp.log(p) - jnp.log1p(-p)
    offset = jax.random.randint(next(keys), (BATCH, 1), 0, MAX_STREAM_OFFSET, jnp.int32)
    positions = offset + jnp.arange(SEQ, dtype=jnp.int32)[None, :]
    return {
        "x": normal((BATCH, SEQ, D_MODEL), 1.0),
        "mem": normal((BATCH, MEM_TOKENS, D_MODEL), 1.0),
        "positions": positions,
        "norm_mix": gain(D_MODEL),
        "w_in": normal((DEPTH, D_MODEL, sum(IN_WIDTHS)), D_MODEL ** -0.5),
        "conv_w": normal((DEPTH, CONV_WIDTH, LRU_WIDTH), CONV_WIDTH ** -0.5),
        "conv_b": normal((DEPTH, LRU_WIDTH), 0.01),
        "lru_wa": normal((DEPTH, LRU_BLOCKS, bw, bw), bw ** -0.5),
        "lru_ba": normal((DEPTH, LRU_WIDTH), 0.01),
        "lru_wx": normal((DEPTH, LRU_BLOCKS, bw, bw), bw ** -0.5),
        "lru_bx": normal((DEPTH, LRU_WIDTH), 0.01),
        "lru_lambda": lru_lambda,
        "w_lru_o": normal((DEPTH, LRU_WIDTH, D_MODEL), LRU_WIDTH ** -0.5),
        "q_norm": gain(ATTN_HEAD_DIM),
        "k_norm": gain(ATTN_HEAD_DIM),
        "lambda_q1": normal((DEPTH, ATTN_HEAD_DIM), 0.1),
        "lambda_k1": normal((DEPTH, ATTN_HEAD_DIM), 0.1),
        "lambda_q2": normal((DEPTH, ATTN_HEAD_DIM), 0.1),
        "lambda_k2": normal((DEPTH, ATTN_HEAD_DIM), 0.1),
        "subln": gain(ATTN_V_DIM),
        "w_attn_o": normal((DEPTH, ATTN_WIDTH, D_MODEL), ATTN_WIDTH ** -0.5),
        "w_out": normal((DEPTH, D_MODEL, D_MODEL), D_MODEL ** -0.5),
        "norm_cx": gain(D_MODEL),
        "norm_mem": gain(D_MODEL),
        "w_cq": normal((DEPTH, D_MODEL, MEM_WIDTH), D_MODEL ** -0.5),
        "w_ckv": normal((DEPTH, D_MODEL, 2 * MEM_WIDTH), D_MODEL ** -0.5),
        "cq_norm": gain(MEM_HEAD_DIM),
        "ck_norm": gain(MEM_HEAD_DIM),
        "w_co": normal((DEPTH, MEM_WIDTH, D_MODEL), MEM_WIDTH ** -0.5),
        "norm_ffn": gain(D_MODEL),
        "w_group": normal((DEPTH, D_MODEL, N_GROUPS), D_MODEL ** -0.5),
        "b_group": normal((DEPTH, N_GROUPS), 0.01),
        "w_router": normal((DEPTH, D_MODEL, N_EXPERTS), D_MODEL ** -0.5),
        "b_router": normal((DEPTH, N_EXPERTS), 0.01),
        "w_gate_up": normal((DEPTH, N_EXPERTS, D_MODEL, 2 * EXPERT_FF), D_MODEL ** -0.5),
        "w_down": normal((DEPTH, N_EXPERTS, EXPERT_FF, D_MODEL), EXPERT_FF ** -0.5),
    }

def second_block(x, mem, positions, norm_mix, w_in, conv_w, conv_b, lru_wa, lru_ba, lru_wx, lru_bx,
              lru_lambda, w_lru_o, q_norm, k_norm, lambda_q1, lambda_k1, lambda_q2, lambda_k2,
              subln, w_attn_o, w_out, norm_cx, norm_mem, w_cq, w_ckv, cq_norm, ck_norm, w_co,
              norm_ffn, w_group, b_group, w_router, b_router, w_gate_up, w_down):
    cos, sin = rotary_tables(positions)
    splits = np.cumsum(IN_WIDTHS)[:-1].tolist()
    for layer in range(DEPTH):
        lambda_init = 0.8 - 0.6 * math.exp(-0.3 * layer)
        h = rms_norm(x, norm_mix[layer])
        proj = h @ w_in[layer]
        lru_in, lru_gate, q, k, v, g_lru, g_attn = jnp.split(proj, splits, axis=-1)
        xc = causal_depthwise_conv(lru_in, conv_w[layer], conv_b[layer])
        hr = rg_lru(xc, lru_wa[layer], lru_ba[layer], lru_wx[layer], lru_bx[layer], lru_lambda[layer])
        y_lru = (jax.nn.gelu(lru_gate) * hr) @ w_lru_o[layer]
        lam = (jnp.exp(jnp.sum(lambda_q1[layer].astype(jnp.float32) * lambda_k1[layer].astype(jnp.float32)))
               - jnp.exp(jnp.sum(lambda_q2[layer].astype(jnp.float32) * lambda_k2[layer].astype(jnp.float32)))
               + lambda_init)
        o_attn = diff_attention(q, k, v, cos, sin, q_norm[layer], k_norm[layer], lam, lambda_init,
                                subln[layer])
        y_attn = o_attn @ w_attn_o[layer]
        mixed = jax.nn.sigmoid(g_lru) * y_lru + jax.nn.sigmoid(g_attn) * y_attn
        x = x + mixed @ w_out[layer]
        x = x + memory_cross_attention_2(x, mem, norm_cx[layer], norm_mem[layer], w_cq[layer],
                                       w_ckv[layer], cq_norm[layer], ck_norm[layer], w_co[layer])
        x = x + hierarchical_moe(rms_norm(x, norm_ffn[layer]), w_group[layer], b_group[layer],
                                 w_router[layer], b_router[layer], w_gate_up[layer], w_down[layer])
    return x


def setup_inputs(seed=0):
    out = dict(first_inputs(seed))
    for name, value in second_inputs(seed + 1).items():
        if name != "x":
            out[name + "_2"] = value
    return out


def reference(
    x, mem, w_in, gm_w_s, gm_b_s, gm_ln_g, gm_ln_b, ssm_lam_re, ssm_lam_im, ssm_log_step,
    ssm_b_re, ssm_b_im, ssm_c_re, ssm_c_im, ssm_d, glu_w, glu_b, xa_w_k, xa_w_v, w_out, ln_g,
    ln_b, mem_2, positions_2, norm_mix_2, w_in_2, conv_w_2, conv_b_2, lru_wa_2, lru_ba_2,
    lru_wx_2, lru_bx_2, lru_lambda_2, w_lru_o_2, q_norm_2, k_norm_2, lambda_q1_2, lambda_k1_2,
    lambda_q2_2, lambda_k2_2, subln_2, w_attn_o_2, w_out_2, norm_cx_2, norm_mem_2, w_cq_2,
    w_ckv_2, cq_norm_2, ck_norm_2, w_co_2, norm_ffn_2, w_group_2, b_group_2, w_router_2,
    b_router_2, w_gate_up_2, w_down_2,
):
    x = first_block(
        x, mem, w_in, gm_w_s, gm_b_s, gm_ln_g, gm_ln_b, ssm_lam_re, ssm_lam_im, ssm_log_step,
        ssm_b_re, ssm_b_im, ssm_c_re, ssm_c_im, ssm_d, glu_w, glu_b, xa_w_k, xa_w_v, w_out,
        ln_g, ln_b,
    )
    return second_block(
        x, mem_2, positions_2, norm_mix_2, w_in_2, conv_w_2, conv_b_2, lru_wa_2, lru_ba_2,
        lru_wx_2, lru_bx_2, lru_lambda_2, w_lru_o_2, q_norm_2, k_norm_2, lambda_q1_2,
        lambda_k1_2, lambda_q2_2, lambda_k2_2, subln_2, w_attn_o_2, w_out_2, norm_cx_2,
        norm_mem_2, w_cq_2, w_ckv_2, cq_norm_2, ck_norm_2, w_co_2, norm_ffn_2, w_group_2,
        b_group_2, w_router_2, b_router_2, w_gate_up_2, w_down_2,
    )


_drawn_inputs = setup_inputs


def setup_inputs(seed=0):
    import zlib

    import numpy as np

    out = dict(_drawn_inputs(seed))
    spreads = {}
    factors = {'glu_b': 8.0,
     'mem_2': 8.0,
     'norm_mix_2': 8.0,
     'w_in_2': 3.687,
     'conv_w_2': 6.476,
     'conv_b_2': 64.0,
     'lru_wa_2': 8.0,
     'lru_ba_2': 64.0,
     'lru_wx_2': 8.0,
     'lru_bx_2': 64.0,
     'lru_lambda_2': 8.0,
     'w_lru_o_2': 6.166,
     'q_norm_2': 8.0,
     'k_norm_2': 8.0,
     'lambda_q1_2': 8.0,
     'lambda_k1_2': 8.0,
     'lambda_q2_2': 8.0,
     'lambda_k2_2': 8.0,
     'subln_2': 8.0,
     'w_attn_o_2': 4.442,
     'w_out_2': 3.635,
     'norm_cx_2': 8.0,
     'norm_mem_2': 8.0,
     'w_cq_2': 8.0,
     'w_ckv_2': 8.0,
     'cq_norm_2': 8.0,
     'ck_norm_2': 8.0,
     'w_co_2': 8.0,
     'norm_ffn_2': 8.0,
     'w_group_2': 8.0,
     'b_group_2': 8.0,
     'w_router_2': 8.0,
     'b_router_2': 55.861,
     'w_gate_up_2': 8.0,
     'w_down_2': 8.0}
    for name, (base, spread) in spreads.items():
        noise = np.random.default_rng([zlib.crc32(name.encode()), seed]).standard_normal(out[name].shape)
        drawn = base * np.exp(spread * noise) if base else spread * noise
        out[name] = __import__('jax').numpy.asarray(drawn.astype(out[name].dtype))
    for name, factor in factors.items():
        out[name] = (out[name] * factor).astype(out[name].dtype)
    return out
```

```python
from contextlib import ExitStack

import numpy as np
import concourse.bass as bass
from concourse import mybir

F32 = mybir.dt.float32
I32 = mybir.dt.int32
U32 = mybir.dt.uint32
ALU = mybir.AluOpType
ACT = mybir.ActivationFunctionType
AX = mybir.AxisListType

P = 128
SEQ = 1024
D = 1024
NT = SEQ // P
KT = D // P
HALF = 512
SLOT = KT * HALF
SLOTS = 4
LOADED = 48
LN_EPS = 1e-5
EPS = 1e-6
MEM = 256
GM = 512
GM_HEADS = 4
SSM = 256
ST = 8
XA = 256
XA_HEADS = 4
XA_DIM = 64
DN_ALPHA = 2.0 ** 0.25

ROW = {"norm_mix": 0, "conv_b": 8, "conv_w": 16, "lru_ba": 48, "lru_bx": 56, "lru_lambda": 64, "norm_cx": 72,
       "norm_mem": 80, "norm_ffn": 88, "positions": 96, "lam_re": 104, "lam_im": 112, "glu_b": 120, "ssm_d": 122,
       "cq_norm": 124, "ck_norm": 125, "subln": 126, "zero": 127}
MH = 4
EXPERTS = 32
GROUPS = 4
FF = 512
OVER = 2 * SEQ // P - 1
BLOCKS = EXPERTS + OVER
TWO_PI = 2.0 * np.pi
PI_A = 6.28125
PI_B = float(np.float32(np.round((TWO_PI - PI_A) * 2 ** 19) / 2 ** 19))
PI_C = float(TWO_PI - PI_A - PI_B)
LN2_A = 0.693359375
LN2_B = float(np.log(2.0) - 0.693359375)
INV_FREQ = [float(np.exp(np.float32(-np.log(500000.0)) * np.float32(n) / np.float32(8), dtype=np.float32)) for n in range(8)]
ROUND = 1.5 * 2 ** 23


def program(nc, I, out):
    ctx = ExitStack()
    base = 16512
    TOP = 229344
    RING = base
    A0 = RING + SLOTS * SLOT * 4
    B0 = A0 + KT * SEQ * 4
    C0 = B0 + KT * SEQ * 4
    K0 = C0 + KT * SEQ * 4
    top = {"K": K0}

    def at(name, shape, offset, dt=F32):
        size = int(np.prod(shape[1:])) * 4
        assert offset + size <= TOP, name
        return nc.alloc_sbuf_tensor_at(name, shape, dt, offset=offset)[:]

    def keep(name, shape, dt=F32):
        o = top["K"]
        top["K"] = o + (int(np.prod(shape[1:])) * 4 + 31) // 32 * 32
        return at(name, shape, o, dt)

    def sem(name):
        return ctx.enter_context(nc.semaphore(name))

    def area(start):
        pos = [start]

        def put(name, shape, dt=F32):
            o = pos[0]
            pos[0] = o + (int(np.prod(shape[1:])) * 4 + 31) // 32 * 32
            return at(name, shape, o, dt)
        put.pos = pos
        return put

    with ctx:
        ring = at("ring", [P, SLOTS, KT, HALF], RING)
        ring_flat = ring.rearrange("p s k n -> p (s k n)")
        regA = at("regA", [P, KT, SEQ], A0)
        regB = at("regB", [P, KT, SEQ], B0)
        regC = at("regC", [P, KT, SEQ], C0)
        ident = keep("ident", [P, P])
        ones = keep("ones", [P, P])
        cols = keep("cols", [P, P])
        psum = ctx.enter_context(nc.psum_tensor("psum", [P, 4, 2 * HALF], F32))[:]
        pair = [psum[:, n] for n in range(4)]

        def col(name, n=8):
            return cols[:, ROW[name]:ROW[name] + n]

        rope_c = keep("rope_c", [P, NT, 8])
        rope_s = keep("rope_s", [P, NT, 8])
        tiny = {n: keep("tiny_" + n, [P, NT * 8]) for n in ("a", "b", "c", "d", "e", "f", "g")}
        gm_st = keep("gm_st", [P, 32, 6])
        gm_mv = keep("gm_mv", [P, 32, 2])
        gm_r = keep("gm_r", [P, 32])
        sm = {n: keep("sm_" + n, [P, 8]) for n in ("mx", "sum", "rc", "mean", "r1", "r2", "ss", "v1")}
        xa_nm = [keep(f"xa_nm{n}", [P, 4]) for n in range(2)]
        xa_sum = [keep(f"xa_sum{n}", [P, 4]) for n in range(2)]
        tab8 = keep("tab8", [P, 8, KT])
        pcol = [keep(f"pcol{n}", [P, 8]) for n in range(2)]
        neg_lam = keep("neg_lam", [P, 1])
        subln = keep("subln", [P, 1])
        rs = (keep("rs_a", [P, 32]), keep("rs_b", [P, 32]), keep("rs_i", [P, 32], I32))

        gate_w = keep("gate_w", [P, NT, 2])
        dest_i = [keep(f"dest_i{n}", [P, NT], I32) for n in range(2)]
        slot_tok = keep("slot_tok", [P, BLOCKS], I32)
        over_i = keep("over_i", [P, 32], I32)
        S0 = top["K"]
        x3_dram = nc.dram_tensor("x3_scratch", [SEQ, D], F32).ap()
        h3_dram = nc.dram_tensor("h3_scratch", [SEQ, D], F32).ap()
        tok_dram = nc.dram_tensor("tok_scratch", [BLOCKS * P, 1], I32).ap()
        y_dram = nc.dram_tensor("y_scratch", [BLOCKS * P, D], F32).ap()
        x1_dram = nc.dram_tensor("x1_scratch", [SEQ, D], F32).ap()
        x2_dram = nc.dram_tensor("x2_scratch", [SEQ, D], F32).ap()

        slot_full = [sem(f"slot_full{n}") for n in range(SLOTS)]
        slot_free = [sem(f"slot_free{n}") for n in range(SLOTS)]
        loads = [0] * SLOTS
        used = [0] * SLOTS

        def slot_wait(sp, s, more=0):
            n = loads[s] + more
            if not isinstance(n, int) or n > 0:
                sp.wait_ge(slot_free[s], n)

        def slot_load(sp, s, w_rows, c0, width=HALF):
            slot_wait(sp, s)
            k = w_rows.shape[0] // P
            dst = ring[:, s].rearrange("p k n -> p (k n)")[:, 0:k * width].rearrange("p (k n) -> p k n", n=width)
            sp.dma_start(dst, w_rows[:, c0:c0 + width].rearrange("(k p) n -> p k n", p=P)).then_inc(slot_full[s], LOADED)
            loads[s] += 1

        def slot_ready(pe, s):
            pe.wait_ge(slot_full[s], LOADED * (used[s] + 1))

        def slot_done(pe, s):
            used[s] += 1
            pe.drain()
            pe.sem_inc(slot_free[s], 1)

        def products(o, terms):
            last = None
            for n, (l, r) in enumerate(terms):
                last = nc.tensor.matmul(o, l, r, start=(n == 0), stop=(n == len(terms) - 1))
            return last


        sems = {}

        def S(name):
            if name not in sems:
                sems[name] = sem(name)
            return sems[name]

        def wait_unless_first(engine, semaphore, count):
            if not isinstance(count, int) or count > 0:
                engine.wait_ge(semaphore, count)

        ONCE = {
            "pe": ("cols_turned", "kv_ready", "wgm_turned", "ct_turned", "ct_turned", "bt_turned", "bt_turned",
                   "k2_turned", "router_done", "ranked"),
            "dve": ("rows_filled", "cols_ready", "bbar_placed", "half_glu_b", "xp_zeroed", "lam_sums", "heads_done",
                    "k2_normed", "group_less_max", "second_less_first", "chosen", "dest_ready", "over_ready"),
            "act": ("kv_taken", "wt_taken", "ct_ready", "ct_ready", "bt_ready", "bt_ready", "lam_exp", "mrow_squared",
                    "k2_squared", "k2_squared", "k2t_taken", "group_exp", "second_exp"),
            "pool": ("zeroed", "ident_ready", "wgm_masked", "route_consts"),
        }

        def once(name):
            return S([e + "_steps" for e in ONCE if name in ONCE[e]][0])

        def nth(name, n):
            steps = [names for names in ONCE.values() if name in names][0]
            return [i + 1 for i, s in enumerate(steps) if s == name][n - 1]

        p0 = area(S0)
        rows = p0("rows", [P, P])
        irows = p0("irows", [P, P], I32)
        wgm = p0("wgm", [P, GM_HEADS, P])
        lstep = p0("lstep", [P, ST])
        ssmp = {n: p0("ssmp_" + n, [P, ST]) for n in
                ("step", "ang", "k", "r", "c", "s", "h", "lr", "li", "br", "bi", "den", "t1", "t2", "t3", "t4")}
        phase = {n: (p0(f"phase_c{n}", [P, ST]), p0(f"phase_s{n}", [P, ST])) for n in (1, 2, 4, 8, 16, 32, 64, 128, 256, 512)}
        b_raw = p0("b_raw", [P, 2, ST, 16])
        b_bar = p0("b_bar", [P, 2, ST, 16])
        b_tmp = p0("b_tmp", [P, ST, 16])
        wT = p0("wT", [P, GM_HEADS, P])
        gm_bs = p0("gm_bs", [P, GM_HEADS, P])
        glu_w = p0("glu_w", [P, 2, SSM])
        MT0 = p0.pos[0]
        memT = p0("memT", [P, KT, MEM])
        kF = p0("kF", [P, 2, MEM])
        vM = p0("vM", [P, 2, XA])
        W0 = p0.pos[0]
        xin = [at(f"xin{n}", [P, D], W0 + n * 4096) for n in range(2)]
        pc = area(C0)
        xb = pc("xb", [P, 2, SEQ])
        gb = pc("gb", [P, 2, SEQ])
        tabc = pc("tabc", [P, ST, P])
        tabs = pc("tabs", [P, ST, P])
        wcos = pc("wcos", [P, SEQ])
        wsin = pc("wsin", [P, SEQ])
        pb = area(B0)
        blockB = pb("blockB", [P, ST, 2, P])
        blockC = pb("blockC", [P, ST, 2, P])
        CT = pb("CT", [P, ST, 3, P])
        pw = area(RING + 2 * SLOT * 4)
        rot = [pw(f"rot{n}", [P, SEQ]) for n in range(4)]
        gr = pw("gr", [P, SEQ])
        gi = pw("gi", [P, SEQ])
        BT = pw("BT", [P, ST, 2, P])
        yb = at("yb", [P, 2, SEQ], W0)
        hbuf = [at(f"hbuf{n}", [P, SEQ], RING + SLOT * 4 + n * 4096) for n in range(4)]
        vh = at("vh", [P, NT, GM], C0)
        vg = at("vg", [P, NT, GM], C0 + 16384)
        pg = area(W0)
        gu = [at(f"gu{n}", [P, SEQ], MT0 + 4096 * n) for n in range(2)]
        th = [pg(f"th{n}", [P, SEQ]) for n in range(2)]
        mb = pg("mb", [P, SEQ])
        gm_g, gm_b = pg("gm_g", [P, GM]), pg("gm_b", [P, GM])
        ptiny = area(pg.pos[0])
        qF = at("qF", [P, 2, SEQ], C0)
        pT = at("pT", [P, 8, HALF], C0 + 8192)
        ex = [at(f"ex{n}", [P, SEQ], C0 + 24576 + 4096 * n) for n in range(2)]
        xr = [at(f"xr{n}", [P, D], C0 + 4096 * n) for n in range(2)]
        hx = [at(f"hx{n}", [P, D], C0 + 8192 + 4096 * n) for n in range(2)]
        ln_g = at("ln_g", [P, D], C0 + 16384)
        ln_b = at("ln_b", [P, D], C0 + 20480)
        sqj = at("sqj", [P, D], C0 + 24576)
        xf = [at(f"xf{n}", [P, D], C0 + 22528 + 4096 * n) for n in range(2)]
        pl = area(C0)
        xp = [pl(f"xp{n}", [P, SEQ + 4]) for n in range(2)]
        xc = [pl(f"xc{n}", [P, SEQ]) for n in range(2)]
        gg = at("gg", [P, SEQ], pl.pos[0])
        pl = area(S0)
        thr, thi, av, tl, sq = (pl(n, [P, SEQ]) for n in ("thr", "thi", "av", "tl", "sq"))
        mth = [at(f"mth{n}", [P, SEQ], S0 + 4096 * n) for n in range(2)]
        mtmp = at("mtmp", [P, SEQ], S0 + 8192)
        ph = area(RING + 2 * SLOT * 4)
        e2 = ph("e2", [P, 2, SEQ])
        wmix = [ph(f"wmix{n}", [P, SEQ]) for n in range(2)]
        wmT = ph("wmT", [P, SEQ])
        obuf = ph("obuf", [P, NT, P])
        qT = ph("qT", [P, SEQ])
        kT = ph("kT", [P, SEQ])
        ph = area(S0)
        qkv = ph("qkv", [P, NT, 384])
        vv = ph("vv", [P, NT, P])
        qk_gain = ph("qk_gain", [P, 4, 64])
        lam4 = ph("lam4", [P, 4, 64])
        junk = ph("junk", [P, P])
        hs = {n: ph("hs_" + n, [P, 32]) for n in ("ss", "r", "v1")}
        ho = {n: ph("ho_" + n, [P, 8]) for n in ("ss", "r", "v1", "mx", "nm", "sum", "rc", "rl")}
        sq8 = e2.rearrange("p m n -> p (m n)").rearrange("p (t n) -> p t n", n=256)
        rope_t = [wmix[n // 2][:, 256 * (n % 2):256 * (n % 2) + 256].rearrange("p (t m d) -> p t m d", m=4, d=8)
                  for n in range(4)]
        xr2 = [at(f"xr2{n}", [P, D], B0 + 4096 * n) for n in range(2)]
        hx2 = [at(f"hx2{n}", [P, D], B0 + 8192 + 4096 * n) for n in range(2)]
        sqj2 = at("sqj2", [P, D], B0 + 16384)
        LRU_O, GATE_L, GATE_A = 0, 5 * D, 6 * D
        HEADS = 8
        px = area(S0)
        mrow = [px(f"mrow{n}", [P, D]) for n in range(2)]
        mT2 = px("mT2", [P, KT, MEM])
        kvM = [px(f"kvM{n}", [P, D]) for n in range(2)]
        kF2 = px("kF2", [P, MH, MEM])
        ex2 = [px(f"ex2{n}", [P, SEQ]) for n in range(2)]
        jk = px("jk", [P, P])
        cs = {n: px("cs_" + n, [P, 32]) for n in ("ss", "v1", "r")}
        zeros = at("zeros", [P, 256], TOP - 1024)
        assert px.pos[0] <= TOP - 1024
        qM = at("qM", [P, NT, HALF], B0)
        oF2 = at("oF2", [P, MH, SEQ], B0 + 16384)
        qF2 = at("qF2", [P, MH, SEQ], C0)
        pT2 = at("pT2", [P, 8, HALF], C0 + 16384)
        xr3 = [at(f"xr3{n}", [P, D], C0 + 4096 * n) for n in range(2)]
        hx3 = [at(f"hx3{n}", [P, D], C0 + 8192 + 4096 * n) for n in range(2)]
        sqj3 = at("sqj3", [P, D], C0 + 16384)
        pr = area(C0 + 20480)
        w_r = pr("w_r", [P, KT, 36])
        b_r = pr("b_r", [P, 36])
        logit = pr("logit", [P, NT, 36])
        iota_i = pr("iota_i", [P, EXPERTS], I32)
        iota_f = pr("iota_f", [P, EXPERTS])
        tok_i = pr("tok_i", [P, NT], I32)
        tri = pr("tri", [P, P])
        zero_i = pr("zero_i", [P, BLOCKS], I32)
        pr = area(S0)
        grp = {n: pr("grp_" + n, [P, NT, 4]) for n in ("eq", "sel", "e")}
        el = {n: pr("el_" + n, [P, NT, 8]) for n in ("v", "v2", "eq", "one", "two")}
        r8 = {n: pr("r8_" + n, [P, NT]) for n in ("gm", "gi", "gv", "m1", "m2", "i1", "e2", "w1", "t")}
        big = pr("big", [P, NT, GROUPS, 8])
        M = [pr(f"M{n}", [P, NT, EXPERTS]) for n in range(2)]
        Mb = pr("Mb", [P, NT, EXPERTS])
        rank = pr("rank", [P, NT, EXPERTS])
        rt = pr("rt", [P, NT, EXPERTS])
        ce = {n: pr("ce_" + n, [P, EXPERTS]) for n in ("n", "ov", "end", "off", "t")}
        oj = pr("oj", [P, OVER + 1, EXPERTS])
        of = pr("of", [P, 32])
        assert pr.pos[0] <= TOP - 1024
        slots6 = at("slots6", [P, 2, 3, SLOT], RING)
        pe_ = area(C0)
        xg = [pe_(f"xg{n}", [P, D]) for n in range(2)]
        xgT = [pe_(f"xgT{n}", [P, KT, P]) for n in range(2)]
        ga = pe_("ga", [P, FF])
        aa = pe_("aa", [P, FF])
        aT = pe_("aT", [P, 4, P])
        pe_ = area(B0)
        ys = [pe_(f"ys{n}", [P, D]) for n in range(2)]
        gidx = [pe_(f"gidx{n}", [P, 8], I32) for n in range(2)]
        yg = [[pe_(f"yg{m}{n}", [P, D]) for n in range(2)] for m in range(2)]

        PARAMS = 16 * 17

        def flat(a):
            return a.rearrange("(r c) -> r c", c=P)

        block = ctx.enter_context(nc.Block())

        @block.sync
        def _(sp):
            for t in range(NT + 2):
                if t >= 2:
                    sp.wait_ge(S("xin_turned"), t - 1)
                src = I["x"][0, t * P:(t + 1) * P, :] if t < NT else I["mem"][0, (t - NT) * P:(t - NT + 1) * P, :]
                sp.dma_start(xin[t % 2], src).then_inc(S(f"xin_full{t % 2}"), 16)
                if t == 3:
                    slot_load(sp, 0, I["w_in"][0], 3 * GM)
            slot_wait(sp, 1)
            for m, key in enumerate(("xa_w_k", "xa_w_v")):
                sp.dma_start(ring[:, 1, :, XA * m:XA * (m + 1)], I[key][0].rearrange("(k p) n -> p k n", p=P)
                             ).then_inc(slot_full[1], 16 + 16 * m)
            loads[1] += 1
            slot_load(sp, 0, I["w_in"][0], GM)
            sp.wait_ge(S("branch_b"), 2)
            slot_load(sp, 1, I["w_in"][0], 0)
            slot_load(sp, 2, I["w_in"][0], 2 * GM)
            slot_load(sp, 3, I["w_in"][0], 3 * GM + 2 * SSM)
            for m, key in enumerate(("gm_ln_g", "gm_ln_b")):
                sp.dma_start((gm_g, gm_b)[m], I[key][0].rearrange("h d -> (h d)").partition_broadcast(P)
                             ).then_inc(S("vectors_in"), 16)
            slot_load(sp, 0, I["w_out"][0], 0)
            slot_load(sp, 1, I["w_out"][0], HALF)
            sp.wait_ge(S("yx_ready"), 4)
            for m, key in enumerate(("ln_g", "ln_b")):
                sp.dma_start((ln_g, ln_b)[m], I[key][0].partition_broadcast(P)).then_inc(S("vectors_in"), 16)
            for t in range(NT + 1):
                if t < NT:
                    if t >= 2:
                        sp.wait_ge(S(f"rows_stored{t % 2}"), 16 * (t // 2))
                        sp.wait_ge(S("rows_normed"), t - 1)
                    sp.dma_start(xr[t % 2], I["x"][0, t * P:(t + 1) * P, :]).then_inc(S(f"rows_full{t % 2}"), 16)
                if t >= 1:
                    sp.wait_ge(S("rows_ready"), t)
                    sp.dma_start(x1_dram[(t - 1) * P:t * P, :], xr[(t - 1) % 2]).then_inc(S(f"rows_stored{(t - 1) % 2}"), 16)
            w2 = I["w_in_2"][0]
            with sp.Fori(0, KT // 2) as i:
                for par in range(2):
                    c0 = sp.snap((i * 2 + par) * P)
                    c1 = sp.snap(c0 + D)
                    uses = sp.snap(i + loads[2 + par])
                    sp.wait_ge(slot_free[2 + par], uses)
                    flat_slot = ring[:, 2 + par].rearrange("p k n -> p (k n)")
                    for m in range(2):
                        sp.dma_start(flat_slot[:, m * 1024:(m + 1) * 1024].rearrange("p (k n) -> p k n", n=P),
                                     w2[:, bass.ds((c0, c1)[m], P)].rearrange("(k p) n -> p k n", p=P)
                                     ).then_inc(slot_full[2 + par], 16 + 16 * m)
                    for m, key in enumerate(("lru_wa_2", "lru_wx_2")):
                        sp.dma_start(flat_slot[:, 2048 + m * P:2048 + (m + 1) * P],
                                     I[key][0].rearrange("b i o -> (b i) o")[bass.ds(c0, P), :]
                                     ).then_inc(S("lru_w_full%d" % par), 16)
            for par in range(2):
                loads[2 + par] += KT // 2
            for c in range(2):
                slot_load(sp, 2 * c, I["w_lru_o_2"][0], c * HALF)
                slot_load(sp, 2 * c + 1, w2, GATE_L + c * HALF)
            sp.wait_ge(S("merged"), KT)
            for n, key in enumerate(("q_norm_2", "q_norm_2", "k_norm_2", "k_norm_2")):
                sp.dma_start(qk_gain[:, n], I[key][0].partition_broadcast(P)).then_inc(S("vectors_in"), 16)
            for n, key in enumerate(("lambda_q1_2", "lambda_k1_2", "lambda_q2_2", "lambda_k2_2")):
                sp.dma_start(lam4[:, n], I[key][0].partition_broadcast(P)).then_inc(S("vectors_in"), 16)

            def head_load(cols0, at0):
                dst = ring_flat[:, bass.ds(at0, KT * 384)].rearrange("p (k n) -> p k n", n=384)
                for m in range(3):
                    sp.dma_start(dst[:, :, m * P:(m + 1) * P],
                                 w2[:, bass.ds(cols0[m], P)].rearrange("(k p) n -> p k n", p=P)
                                 ).then_inc(S("head_full"), 16)

            slot_wait(sp, 0)
            slot_wait(sp, 1)
            head_load([2 * D, 3 * D, 4 * D], 0)
            sp.sem_inc(S("head_free"), 48)
            with sp.Fori(1, HEADS) as h:
                cols0, at0 = [sp.snap(h * P + (2 + m) * D) for m in range(3)], sp.snap((h % 2) * SLOT)
                before = sp.snap(h * 48)
                sp.wait_ge(S("head_free"), before)
                sp.wait_ge(S("head_full"), before)
                head_load(cols0, at0)
            slot_wait(sp, 2)
            slot_wait(sp, 3)
            sp.wait_ge(once("heads_done"), nth("heads_done", 1))
            slot_load(sp, 2, I["w_attn_o_2"][0], 0)
            slot_load(sp, 3, w2, GATE_A)
            sp.wait_ge(S("head_free"), 48 * HEADS + 48)
            slot_load(sp, 0, I["w_attn_o_2"][0], HALF)
            slot_load(sp, 1, w2, GATE_A + HALF)
            slot_load(sp, 2, I["w_out_2"][0], 0)
            slot_load(sp, 3, I["w_out_2"][0], HALF)
            sp.wait_ge(S("merged"), KT + KT)
            for t in range(NT + 1):
                if t < NT:
                    if t >= 2:
                        sp.wait_ge(S(f"rows_stored{t % 2}"), 16 * (t // 2) + 8 * NT)
                        sp.wait_ge(S("rows_normed"), t - 1 + NT)
                    else:
                        for par in range(2):
                            sp.wait_ge(S(f"rows_stored{par}"), 16 * NT // 2)
                    sp.dma_start(xr2[t % 2], x1_dram[t * P:(t + 1) * P, :]).then_inc(S(f"rows_full{t % 2}"), 16)
                if t >= 1:
                    sp.wait_ge(S("rows_ready"), t + NT)
                    sp.dma_start(x2_dram[(t - 1) * P:t * P, :], xr2[(t - 1) % 2]
                                 ).then_inc(S(f"rows_stored{(t - 1) % 2}"), 16)
            slot_load(sp, 0, I["w_ckv_2"][0], 0)
            slot_load(sp, 1, I["w_ckv_2"][0], HALF)
            for t in range(2):
                sp.dma_start(mrow[t], I["mem_2"][0, t * P:(t + 1) * P, :]).then_inc(S("vectors_in"), 16)
            slot_load(sp, 2, I["w_cq_2"][0], 0)
            slot_wait(sp, 3)
            sp.dma_start(ring[:, 3].rearrange("p k n -> p (k n)").rearrange("p (k n) -> p k n", n=D),
                         I["w_co_2"][0].rearrange("(k p) n -> p k n", p=P)).then_inc(slot_full[3], LOADED)
            loads[3] += 1
            sp.wait_ge(S("co_taken"), 8)
            sp.dma_start(w_r[:, :, 0:4], I["w_group_2"][0].rearrange("(k p) n -> p k n", p=P)).then_inc(S("vectors_in"), 16)
            sp.dma_start(w_r[:, :, 4:36], I["w_router_2"][0].rearrange("(k p) n -> p k n", p=P)).then_inc(S("vectors_in"), 16)
            sp.dma_start(b_r[:, 0:4], I["b_group_2"][0].partition_broadcast(P)).then_inc(S("vectors_in"), 16)
            sp.dma_start(b_r[:, 4:36], I["b_router_2"][0].partition_broadcast(P)).then_inc(S("vectors_in"), 16)
            for t in range(NT + 1):
                if t < NT:
                    if t >= 2:
                        sp.wait_ge(S(f"rows_stored{t % 2}"), 16 * (t // 2) + 16 * NT)
                        sp.wait_ge(S("rows_normed"), t - 1 + 2 * NT)
                    else:
                        for par in range(2):
                            sp.wait_ge(S(f"rows_stored{par}"), 16 * NT // 2 + 8 * NT)
                    sp.dma_start(xr3[t % 2], x2_dram[t * P:(t + 1) * P, :]).then_inc(S(f"rows_full{t % 2}"), 16)
                if t >= 1:
                    sp.wait_ge(S("rows_ready"), t + 2 * NT)
                    sp.dma_start(x3_dram[(t - 1) * P:t * P, :], xr3[(t - 1) % 2]
                                 ).then_inc(S(f"rows_stored{(t - 1) % 2}"), 16)
                    sp.wait_ge(S("rows_normed"), t + 2 * NT)
                    sp.dma_start(h3_dram[(t - 1) * P:t * P, :], hx3[(t - 1) % 2]
                                 ).then_inc(S(f"h3_stored{(t - 1) % 2}"), 16)
            def expert_load(e, par, waits):
                gu_, dn = I["w_gate_up_2"][0], I["w_down_2"][0]
                rows_gu = gu_.rearrange("e k n -> (e k) n")
                rows_dn = dn.rearrange("e k n -> (e k) n")
                r_gu, r_dn = (e * D, e * FF) if isinstance(e, int) else (sp.snap(e * D), sp.snap(e * FF))
                freed = sp.snap(e - 1) if waits else None
                for c in range(2):
                    if waits:
                        sp.wait_ge(S(("gate_done", "up_done")[c]), freed)
                    sp.dma_start(slots6[:, par, c].rearrange("p (k n) -> p k n", n=HALF),
                                 rows_gu[bass.ds(r_gu, D), c * FF:(c + 1) * FF].rearrange("(k p) n -> p k n", p=P)
                                 ).then_inc(S(f"w_full{par}{c}"), 16)
                if waits:
                    sp.wait_ge(S("down_done"), freed)
                sp.dma_start(slots6[:, par, 2].rearrange("p (k n) -> p k n", n=D),
                             rows_dn[bass.ds(r_dn, FF), :].rearrange("(k p) n -> p k n", p=P)
                             ).then_inc(S(f"w_full{par}2"), 16)

            slot_wait(sp, 0)
            slot_wait(sp, 1)
            slot_wait(sp, 2)
            expert_load(0, 0, False)
            slot_wait(sp, 3)
            sp.wait_ge(once("router_done"), nth("router_done", 1))
            expert_load(1, 1, False)
            with sp.Fori(1, EXPERTS // 2) as i:
                for par in range(2):
                    expert_load(sp.snap(i * 2 + par), par, True)
            sp.wait_ge(S("down_done"), EXPERTS)
            sp.wait_ge(once("over_ready"), nth("over_ready", 1))
            n_over = sp.value_load(over_i[0:1, 16:17], min_val=0, max_val=OVER)
            with sp.Fori(0, OVER) as j:
                with sp.If(j < n_over):
                    e = sp.value_load(over_i[0:1, bass.ds(j, 1)], min_val=0, max_val=EXPERTS - 1)
                    r_gu, r_dn, row0 = sp.snap(e * D), sp.snap(e * FF), sp.snap(j * P + EXPERTS * P)
                    before, made = sp.snap(j + EXPERTS), sp.snap(j + 1 + EXPERTS)
                    sp.wait_ge(S("down_done"), before)
                    for c in range(2):
                        sp.dma_start(slots6[:, 0, c].rearrange("p (k n) -> p k n", n=HALF),
                                     I["w_gate_up_2"][0].rearrange("e k n -> (e k) n")[bass.ds(r_gu, D), c * FF:(c + 1) * FF]
                                     .rearrange("(k p) n -> p k n", p=P)).then_inc(S("o_w_full"), 16)
                    sp.dma_start(slots6[:, 0, 2].rearrange("p (k n) -> p k n", n=D),
                                 I["w_down_2"][0].rearrange("e k n -> (e k) n")[bass.ds(r_dn, FF), :]
                                 .rearrange("(k p) n -> p k n", p=P)).then_inc(S("o_w_full"), 16)
                    sp.wait_ge(S("y_taken"), made + 1)
                    sp.dma_start(y_dram[bass.ds(row0, P), :], ys[0]).then_inc(S("y_stored0"), 16)
            sp.wait_ge(S("y_stored0"), n_over * 16 + 8 * EXPERTS)
            sp.sem_inc(S("over_stored"), 1)
            for t in range(NT + 1):
                if t < NT:
                    if t >= 2:
                        sp.wait_ge(S(f"rows_stored{t % 2}"), 16 * (t // 2) + 24 * NT)
                    sp.dma_start(xf[t % 2], x3_dram[t * P:(t + 1) * P, :]).then_inc(S(f"rows_full{t % 2}"), 16)
                if t >= 1:
                    sp.wait_ge(S("out_ready"), t)
                    sp.dma_start(out[0, (t - 1) * P:t * P, :], xf[(t - 1) % 2]).then_inc(S(f"rows_stored{(t - 1) % 2}"), 16)
            for par in range(2):
                sp.wait_ge(S(f"rows_stored{par}"), 16 * NT // 2 + 24 * NT)
                sp.wait_ge(S(f"rows_stored{par}"), 16 * NT // 2 + 8 * NT)
                sp.wait_ge(S(f"rows_stored{par}"), 16 * NT // 2 + 16 * NT)
                sp.wait_ge(S(f"h3_stored{par}"), 16 * NT // 2)

        @block.gpsimd
        def _(pool):
            nc.gpsimd.memset(ident, 0.0)
            nc.gpsimd.memset(ones, 1.0)
            nc.gpsimd.memset(rows, 0.0)
            nc.gpsimd.memset(irows, 0)
            nc.gpsimd.memset(blockB.rearrange("p a b c -> p (a b c)"), 0.0)
            nc.gpsimd.memset(blockC.rearrange("p a b c -> p (a b c)"), 0.0).then_inc(once("zeroed"), 1)
            pool.wait_ge(once("zeroed"), nth("zeroed", 1))
            nc.gpsimd.affine_select(out=ident, in_=ident, compare_op=ALU.not_equal, fill=1.0, base=0,
                                    pattern=[[-1, P]], channel_multiplier=1).then_inc(once("ident_ready"), 1)
            for name, key in (("norm_mix", "norm_mix_2"), ("conv_b", "conv_b_2"), ("lru_ba", "lru_ba_2"),
                              ("lru_bx", "lru_bx_2"), ("lru_lambda", "lru_lambda_2"), ("norm_cx", "norm_cx_2"),
                              ("norm_mem", "norm_mem_2"), ("norm_ffn", "norm_ffn_2"), ("glu_b", "glu_b"),
                              ("ssm_d", "ssm_d"), ("cq_norm", "cq_norm_2"), ("ck_norm", "ck_norm_2"),
                              ("subln", "subln_2")):
                src = flat(I[key][0])
                pool.dma_start(rows[ROW[name]:ROW[name] + src.shape[0], :], src).then_inc(S("params_in"), 16)
            for name, key in (("lam_re", "ssm_lam_re"), ("lam_im", "ssm_lam_im")):
                pool.dma_start(rows[ROW[name]:ROW[name] + 8, :], I[key][0].rearrange("(s a) q -> s (a q)", a=2)
                               ).then_inc(S("params_in"), 16)
            pool.dma_start(rows[16:48, :], I["conv_w_2"][0].rearrange("j (r c) -> (j r) c", c=P)
                           ).then_inc(S("params_in"), 16)
            pool.dma_start(irows[96:104, :], flat(I["positions_2"][0])).then_inc(S("params_in"), 16)
            ls = I["ssm_log_step"][0].rearrange("(s a) -> a s", a=2)
            for a in range(2):
                pool.dma_start(lstep[64 * a:64 * a + 64, :], ls[a].partition_broadcast(64), allow_slow_non_contiguous=True).then_inc(S("ssm_in"), 16)
            for m, key in enumerate(("ssm_b_re", "ssm_b_im")):
                pool.dma_start(b_raw[:, m], I[key][0].rearrange("(s a) q c -> (a q) s c", a=2)).then_inc(S("ssm_in"), 16)
            for m, key in enumerate(("ssm_c_re", "ssm_c_im")):
                src = I[key][0].rearrange("(f j a) c q -> j a c f q", j=4, a=2)
                for j in range(4):
                    for a in range(2):
                        pool.dma_start(blockC[32 * j + 16 * a:32 * j + 16 * a + 16, j:ST:4, m, 64 * a:64 * a + 64],
                                       src[j, a]).then_inc(S("ssm_c_in"), 16)
            pool.dma_start(wgm, I["gm_w_s"][0].rearrange("h t s -> t h s")).then_inc(S("wgm_in"), 16)
            pool.dma_start(gm_bs.rearrange("p h t -> p (h t)"), I["gm_b_s"][0].rearrange("h t -> (h t)").partition_broadcast(P)
                           ).then_inc(S("gm_in"), 16)
            pool.dma_start(glu_w, I["glu_w"][0].rearrange("(k p) n -> p k n", p=P)).then_inc(S("gm_in"), 16)
            pool.wait_ge(S("wgm_in"), 16)
            nc.gpsimd.affine_select(out=wgm, in_=wgm, compare_op=ALU.is_ge, fill=0.0, base=0,
                                    pattern=[[0, GM_HEADS], [-1, P]], channel_multiplier=1).then_inc(once("wgm_masked"), 1)
            pool.wait_ge(once("kv_ready"), nth("kv_ready", 1))
            for s in range(ST):
                pool.wait_ge(S("scanned"), s + 1)
                if s:
                    pool.wait_ge(S("h_used"), s)
                for n, (tab, gg) in enumerate(((wcos, gr), (wsin, gi), (wsin, gr), (wcos, gi))):
                    last = nc.gpsimd.tensor_tensor(hbuf[n], tab, gg, ALU.mult)
                last.then_inc(S("h_ready"), 1)

            pool.wait_ge(S("vectors_in"), 32 + 32)
            for t in range(NT):
                pool.wait_ge(S("xr_normed"), t + 1)
                nc.gpsimd.tensor_tensor(xr[t % 2], xr[t % 2], ln_g, ALU.mult)
                pool.drain()
                nc.gpsimd.tensor_tensor(xr[t % 2], xr[t % 2], ln_b, ALU.add).then_inc(S("rows_ready"), 1)

            pool.wait_ge(once("heads_done"), nth("heads_done", 1))
            nc.gpsimd.memset(zeros, 0.0)
            pool.drain()
            pool.dma_start(y_dram[EXPERTS * P:].rearrange("(p b) (q n) -> p (b q) n", p=P, n=256),
                           zeros.unsqueeze(1).broadcast_to([P, OVER * D // 256, 256])).then_inc(S("tok_moved"), 16)
            pool.wait_ge(S("co_taken"), 8)
            nc.gpsimd.iota(iota_i, pattern=[[1, EXPERTS]], base=0, channel_multiplier=0)
            nc.gpsimd.iota(tok_i, pattern=[[P, NT]], base=0, channel_multiplier=1)
            nc.gpsimd.memset(zero_i, 0)
            pool.drain()
            nc.gpsimd.tensor_copy(iota_f, iota_i)
            nc.gpsimd.affine_select(out=tri, in_=ones, compare_op=ALU.is_gt, fill=0.0, base=0,
                                    pattern=[[1, P]], channel_multiplier=-1).then_inc(once("route_consts"), 1)
            pool.wait_ge(once("route_consts"), nth("route_consts", 1))
            pool.dma_start(tok_dram.rearrange("(p b) o -> p (b o)", b=BLOCKS), zero_i).then_inc(S("tok_moved"), 16)
            pool.wait_ge(S("tok_moved"), 32)
            pool.wait_ge(once("dest_ready"), nth("dest_ready", 1))
            for t in range(NT):
                for n in range(2):
                    nc.gpsimd.indirect_dma_start(
                        out=tok_dram, out_offset=bass.IndirectOffsetOnAxis(ap=dest_i[n][:, t:t + 1], axis=0),
                        in_=tok_i[:, t:t + 1], in_offset=None).then_inc(S("tok_moved"), 16)
            pool.wait_ge(S("tok_moved"), 32 + 32 * NT)
            pool.dma_start(slot_tok, tok_dram.rearrange("(b p) o -> p (b o)", p=P), allow_slow_non_contiguous=True
                           ).then_inc(S("tok_moved"), 16)
            pool.wait_ge(S("tok_moved"), 48 + 32 * NT)
            for par in range(2):
                pool.wait_ge(S(f"h3_stored{par}"), 16 * NT // 2)
                pool.wait_ge(S(f"rows_stored{par}"), 16 * NT // 2 + 16 * NT)

            def gather_rows(e, par, waits):
                if waits:
                    pool.wait_ge(S("xg_turned"), e - 1)
                nc.gpsimd.tensor_copy(gidx[par][:, 0:1], slot_tok[:, bass.ds(e, 1)])
                pool.drain()
                nc.gpsimd.indirect_dma_start(
                    out=xg[par], out_offset=None, in_=h3_dram,
                    in_offset=bass.IndirectOffsetOnAxis(ap=gidx[par][:, 0:1], axis=0)).then_inc(S(f"xg_full{par}"), 16)

            gather_rows(0, 0, False)
            gather_rows(1, 1, False)
            with pool.Fori(1, EXPERTS // 2) as i:
                for par in range(2):
                    gather_rows(pool.snap(i * 2 + par), par, True)
            pool.wait_ge(S("xg_turned"), EXPERTS)
            pool.wait_ge(once("over_ready"), nth("over_ready", 1))
            n_over = pool.value_load(over_i[0:1, 16:17], min_val=0, max_val=OVER)
            with pool.Fori(0, OVER) as j:
                with pool.If(j < n_over):
                    pool.wait_ge(S("xg_turned"), j + EXPERTS)
                    nc.gpsimd.tensor_copy(gidx[0][:, 0:1], slot_tok[:, bass.ds(j + EXPERTS, 1)])
                    pool.drain()
                    nc.gpsimd.indirect_dma_start(
                        out=xg[0], out_offset=None, in_=h3_dram,
                        in_offset=bass.IndirectOffsetOnAxis(ap=gidx[0][:, 0:1], axis=0)).then_inc(S("xg_full0"), 16)
            pool.wait_ge(S("over_stored"), 1)
            for par in range(2):
                pool.wait_ge(S(f"y_stored{par}"), 16 * EXPERTS // 2)
            for t in range(NT):
                if t >= 2:
                    pool.wait_ge(S("out_ready"), t - 1)
                for n in range(2):
                    nc.gpsimd.indirect_dma_start(
                        out=yg[n][t % 2], out_offset=None, in_=y_dram,
                        in_offset=bass.IndirectOffsetOnAxis(ap=dest_i[n][:, t:t + 1], axis=0)
                    ).then_inc(S(f"yg_full{t % 2}"), 16)

        @block.tensor
        def _(pe):
            for name in ("o_ready", "ot_turned"):
                pe.sem_inc(S(name), 1)
            pe.wait_ge(once("ident_ready"), nth("ident_ready", 1))
            pe.wait_ge(once("rows_filled"), nth("rows_filled", 1))
            nc.tensor.transpose(pair[3][:, 0:P], rows, ident).then_inc(once("cols_turned"), 1)
            for t in range(NT + 2):
                pe.wait_ge(S(f"xin_full{t % 2}"), 16 * (t // 2 + 1))
                if t >= 2:
                    pe.wait_ge(S("xt_copied_v"), t - 1)
                    pe.wait_ge(S("xt_copied_a"), t - 1)
                for k in range(KT):
                    last = nc.tensor.transpose(pair[t % 2][:, k * P:(k + 1) * P], xin[t % 2][:, k * P:(k + 1) * P], ident)
                last.then_inc(S("xin_turned"), 1)
            slot_ready(pe, 0)
            pe.wait_ge(once("cols_ready"), nth("cols_ready", 1))
            pe.wait_ge(S("xt_copied_v"), NT + 2)
            pe.wait_ge(S("xt_copied_a"), NT + 2)
            for f in range(4):
                for c in range(2):
                    last = products(pair[f][:, c * HALF:(c + 1) * HALF],
                                    [(ring[:, 0, k, f * P:(f + 1) * P], regA[:, k, c * HALF:(c + 1) * HALF])
                                     for k in range(KT)])
                last.then_inc(S("xs_ready"), 1)
            slot_done(pe, 0)
            slot_ready(pe, 1)
            pe.wait_ge(S("xs_taken"), 1)
            for f in range(2):
                last = products(pair[0][:, f * MEM:(f + 1) * MEM],
                                [(ring[:, 1, k, f * P:(f + 1) * P], memT[:, k]) for k in range(KT)])
            for f in range(2):
                last = products(pair[0][:, HALF + f * XA:HALF + (f + 1) * XA],
                                [(memT[:, k, f * P:(f + 1) * P], ring[:, 1, k, XA:2 * XA]) for k in range(KT)])
            last.then_inc(once("kv_ready"), 1)
            slot_done(pe, 1)
            pe.wait_ge(once("wgm_masked"), nth("wgm_masked", 1))
            pe.wait_ge(S("xs_taken"), 2)
            for h in range(GM_HEADS):
                last = nc.tensor.transpose(pair[1][:, h * P:(h + 1) * P], wgm[:, h], ident)
            last.then_inc(once("wgm_turned"), 1)
            pe.wait_ge(S("ssm_c_in"), 16 * 16)
            for m in range(2):
                pe.wait_ge(S("xs_taken"), 3 + m)
                for s in range(ST):
                    last = nc.tensor.transpose(pair[2 + m][:, s * P:(s + 1) * P], blockC[:, s, m], ident)
                last.then_inc(once("ct_turned"), 1)
            pe.wait_ge(once("bbar_placed"), nth("bbar_placed", 1))
            for m in range(2):
                pe.wait_ge(once("wt_taken"), nth("wt_taken", 1))
                for s in range(ST):
                    last = nc.tensor.transpose(pair[m][:, s * P:(s + 1) * P], blockB[:, s, m], ident)
                last.then_inc(once("bt_turned"), 1)
            for s in range(ST):
                f = s // 4
                if s == 0:
                    pe.wait_ge(once("bt_ready"), nth("bt_ready", 2))
                    pe.wait_ge(once("ct_ready"), nth("ct_ready", 2))
                else:
                    pe.wait_ge(S("bx_taken"), s)
                for m in range(2):
                    for c in range(2):
                        last = nc.tensor.matmul(pair[m][:, c * HALF:(c + 1) * HALF], BT[:, s, m],
                                                xb[:, f, c * HALF:(c + 1) * HALF], start=True, stop=True)
                last.then_inc(S("bx_ready"), 1)
                pe.wait_ge(S("h_ready"), s + 1)
                for n, w in enumerate((0, 1, 2, 2)):
                    for c in range(2):
                        last = nc.tensor.matmul(pair[2 + f][:, c * HALF:(c + 1) * HALF], CT[:, s, w],
                                                hbuf[n][:, c * HALF:(c + 1) * HALF],
                                                start=(s % 4 == 0 and n == 0), stop=(s % 4 == 3 and n == 3))
                last.then_inc(S("h_used"), 1)
            pe.wait_ge(S("yb_ready"), 2)
            pe.wait_ge(S("gm_in"), 32)
            for f in range(2):
                for c in range(2):
                    last = products(pair[f][:, c * HALF:(c + 1) * HALF],
                                    [(glu_w[:, k, f * P:(f + 1) * P], yb[:, k, c * HALF:(c + 1) * HALF]) for k in range(2)])
                last.then_inc(S("glu_ready"), 1)

            slot_ready(pe, 0)
            for t in range(NT):
                if t >= 2:
                    pe.wait_ge(S("vg_ready"), t - 1)
                else:
                    pe.wait_ge(S("glu_tanh"), t + 1)
                products(pair[t % 2][:, 0:HALF], [(regA[:, k, t * P:(t + 1) * P], ring[:, 0, k]) for k in range(KT)]
                         ).then_inc(S("v_ready"), 1)
            slot_done(pe, 0)
            slot_ready(pe, 1)
            slot_ready(pe, 2)
            for h in range(GM_HEADS):
                for j in range(3):
                    n = 3 * h + j
                    if n >= 4:
                        pe.wait_ge(S(("u_taken", "g_taken", "mix_taken")[(n - 4) % 3]), (n - 4) // 3 + 1)
                    elif n < 2:
                        pe.wait_ge(S("vg_ready"), NT)
                    elif n == 2:
                        pe.wait_ge(S("yd_ready"), 2)
                    o = pair[n % 4]
                    if j < 2:
                        for c in range(2):
                            last = products(o[:, c * HALF:(c + 1) * HALF],
                                            [(ring[:, 1 + j, k, h * P:(h + 1) * P], regA[:, k, c * HALF:(c + 1) * HALF])
                                             for k in range(KT)])
                    else:
                        pe.wait_ge(S("vh_ready"), NT)
                        for c in range(NT):
                            last = nc.tensor.matmul(o[:, c * P:(c + 1) * P], vh[:, c, h * P:(h + 1) * P], wT[:, h],
                                                    start=True, stop=True)
                    last.then_inc(S(("u_ready", "g_ready", "mix_ready")[j]), 1)
            slot_done(pe, 1)
            slot_done(pe, 2)
            slot_ready(pe, 3)
            pe.wait_ge(S("mix_taken"), GM_HEADS)
            for f in range(4):
                for c in range(2):
                    last = products(pair[f][:, c * HALF:(c + 1) * HALF],
                                    [(ring[:, 3, k, f * P:(f + 1) * P], regA[:, k, c * HALF:(c + 1) * HALF])
                                     for k in range(KT)])
                last.then_inc(S("qx_ready"), 1)
            slot_done(pe, 3)
            pe.wait_ge(S("qx_taken"), 4)

            def xa_scores(t):
                if t >= 2:
                    pe.wait_ge(S("mem_exp"), t - 1)
                for h in range(XA_HEADS):
                    r = XA_DIM * (h % 2)
                    b = 2 * (h % 2) + h // 2
                    last = nc.tensor.matmul(pair[t % 2][:, b * MEM:(b + 1) * MEM],
                                            qF[r:r + XA_DIM, h // 2, t * P:(t + 1) * P], kF[r:r + XA_DIM, h // 2],
                                            start=True, stop=True)
                last.then_inc(S("mem_scores"), 1)

            xa_scores(0)
            for t in range(NT):
                if t + 1 < NT:
                    xa_scores(t + 1)
                pe.wait_ge(S("mem_probs"), t + 1)
                if t >= 1:
                    pe.wait_ge(S("probs_t_taken"), t)
                for n in range(8):
                    last = nc.tensor.transpose(pair[2][:, n * P:(n + 1) * P], ex[t % 2][:, n * P:(n + 1) * P], ident)
                last.then_inc(S("mem_turned"), 1)
                if t % 4 == 3:
                    pe.wait_ge(S("probs_t_taken"), t + 1)
                    if t == 7:
                        pe.wait_ge(S("yx_ready"), 2)
                    for f in range(2):
                        for a in range(2):
                            h = 2 * f + a
                            for m in range(2):
                                last = nc.tensor.matmul(pair[3][XA_DIM * a:XA_DIM * a + XA_DIM, f * HALF:(f + 1) * HALF],
                                                        vM[:, m, h * XA_DIM:(h + 1) * XA_DIM], pT[:, 2 * (2 * a + f) + m],
                                                        start=(m == 0), stop=(m == 1))
                        last.then_inc(S("xa_out"), 1)
            slot_ready(pe, 0)
            slot_ready(pe, 1)
            pe.wait_ge(S("yx_ready"), 4)
            for t in range(NT + 1):
                if t < NT:
                    if t >= 2:
                        pe.wait_ge(S("xr_added"), t - 1)
                    for c in range(2):
                        last = products(pair[t % 2][:, c * HALF:(c + 1) * HALF],
                                        [(regB[:, k, t * P:(t + 1) * P], ring[:, c, k]) for k in range(KT)])
                    last.then_inc(S("o_rows_ready"), 1)
                if t >= 1:
                    pe.wait_ge(S("rows_normed"), t)
                    if t >= 3:
                        pe.wait_ge(S("rows_taken"), t - 2)
                    for k in range(KT):
                        last = nc.tensor.transpose(pair[2 + (t - 1) % 2][:, k * P:(k + 1) * P],
                                                   hx[(t - 1) % 2][:, k * P:(k + 1) * P], ident)
                    last.then_inc(S("rows_turned"), 1)
            slot_done(pe, 0)
            slot_done(pe, 1)

            with pe.Fori(0, KT // 2) as i:
                for par in range(2):
                    b = i * 2 + par
                    w = ring[:, 2 + par].rearrange("p k n -> p (k n)")
                    pe.wait_ge(slot_full[2 + par], LOADED * (used[2 + par] + 1) + i * LOADED)
                    pe.wait_ge(S("lru_w_full%d" % par), i * 32 + 32)
                    pe.wait_ge(S("rows_taken"), NT)
                    pe.wait_ge(S("lin_taken"), b + 1)
                    for m in range(2):
                        if m == 1:
                            pe.wait_ge(S("gate_taken"), b + 1)
                        for c in range(2):
                            last = products(pair[m][:, c * HALF:(c + 1) * HALF],
                                            [(w[:, m * 1024 + k * P:m * 1024 + (k + 1) * P],
                                              regA[:, k, c * HALF:(c + 1) * HALF]) for k in range(KT)])
                        last.then_inc(S(("lin_ready", "gate_ready")[m]), 1)
                    pe.wait_ge(S("xc_ready"), b + 2)
                    for m in range(2):
                        pe.wait_ge(S(("r_taken", "i_taken")[m]), b + 1)
                        for c in range(2):
                            last = nc.tensor.matmul(pair[2 + m][:, c * HALF:(c + 1) * HALF],
                                                    w[:, 2048 + m * P:2048 + (m + 1) * P],
                                                    xc[par][:, c * HALF:(c + 1) * HALF], start=True, stop=True)
                        last.then_inc(S(("r_ready", "i_ready")[m]), 1)
                    pe.drain()
                    pe.sem_inc(slot_free[2 + par], 1)
            for par in range(2):
                used[2 + par] += KT // 2

            def merge(count0, slots, before):
                for m in range(KT):
                    if m % 4 == 0:
                        sw, sg = slots[m // 4]
                        slot_ready(pe, sw)
                        slot_ready(pe, sg)
                    for j, src in enumerate((regB, regA)):
                        if m >= 2:
                            pe.wait_ge(S("merged"), count0 + m - 1)
                        elif m == 0 and j == 0:
                            before()
                        for c in range(2):
                            last = products(pair[2 * (m % 2) + j][:, c * HALF:(c + 1) * HALF],
                                            [(ring[:, (sw, sg)[j], k, (m % 4) * P:(m % 4 + 1) * P],
                                              src[:, k, c * HALF:(c + 1) * HALF]) for k in range(KT)])
                        last.then_inc(S(("merge_y", "merge_g")[j]), 1)
                    if m % 4 == 3:
                        slot_done(pe, sw)
                        slot_done(pe, sg)

            merge(0, ((0, 1), (2, 3)), lambda: (pe.wait_ge(S("lru_done"), KT + 1), pe.wait_ge(S("i_taken"), KT + 1)))

            def project(h, t, par):
                if t == 0:
                    pe.wait_ge(S("head_full"), h * 48 + 48)
                pe.wait_ge(S("qkv_taken"), h * 8 + t + 1)
                products(pair[2][:, 0:384],
                         [(regA[:, k, t * P:(t + 1) * P], ring_flat[:, bass.ds(par * SLOT + k * 384, 384)])
                          for k in range(KT)]).then_inc(S("qkv_ready"), 1)
                if t == NT - 1:
                    pe.drain()
                    pe.sem_inc(S("head_free"), 48)

            def turn_qk(h):
                pe.wait_ge(S("qk_normed"), h + 1)
                for m in range(2):
                    for t in range(NT):
                        last = nc.tensor.transpose(pair[3 * (1 - m)][:, t * P:(t + 1) * P],
                                                   qkv[:, t, m * P:(m + 1) * P], ident)
                    last.then_inc(S(("qt_turned", "kt_turned")[m]), 1)

            def scores(h, j):
                if j == 0:
                    pe.wait_ge(S("qt_ready"), h + 1)
                    pe.wait_ge(S("kt_ready"), h + 1)
                    pe.wait_ge(S("ot_taken"), h + 1)
                pe.wait_ge(S("exp_done"), h * 8 + j + 1)
                n = (j + 1) * P
                for m in range(2):
                    for c in range(0, n, HALF):
                        e = min(n, c + HALF)
                        last = nc.tensor.matmul(pair[m][:, c:e], qT[64 * m:64 * m + 64, j * P:(j + 1) * P],
                                                kT[64 * m:64 * m + 64, c:e], start=True, stop=True)
                last.then_inc(S("s_ready"), 1)

            def values(h, j):
                pe.wait_ge(S("w_ready"), h * 8 + j + 2)
                pe.wait_ge(S("wt_taken2"), h * 8 + j + 1)
                for kb in range(j + 1):
                    last = nc.tensor.transpose(pair[3][:, kb * P:(kb + 1) * P], wmix[j % 2][:, kb * P:(kb + 1) * P], ident)
                last.then_inc(S("wt_turned"), 1)
                pe.wait_ge(S("wt_taken2"), h * 8 + j + 2)
                pe.wait_ge(S("o_taken"), h * 8 + j + 1)
                if j == 0:
                    pe.wait_ge(S("v_copied"), h + 1)
                products(pair[2][:, HALF:HALF + P],
                         [(wmT[:, kb * P:(kb + 1) * P], vv[:, kb]) for kb in range(j + 1)]).then_inc(S("o_ready"), 1)

            def turn_o(h):
                pe.wait_ge(S("o_normed"), h + 1)
                for t in range(NT):
                    last = nc.tensor.transpose(pair[1][:, t * P:(t + 1) * P], obuf[:, t], ident)
                last.then_inc(S("ot_turned"), 1)

            def attend(h, then):
                for j in range(NT):
                    scores(h, j)
                    then(j)
                    if j:
                        values(h, j - 1)
                values(h, NT - 1)

            pe.wait_ge(S("merged"), KT)
            for t in range(NT):
                project(0, t, 0)
            turn_qk(0)
            with pe.Fori(0, HEADS - 1) as h:
                attend(h, lambda j: project(h + 1, j, (h + 1) % 2))
                turn_qk(h + 1)
                turn_o(h)
            attend(HEADS - 1, lambda j: None)
            turn_o(HEADS - 1)
            merge(KT, ((2, 3), (0, 1)), lambda: pe.wait_ge(S("ot_taken"), HEADS + 1))
            slot_ready(pe, 2)
            slot_ready(pe, 3)
            pe.wait_ge(S("merged"), KT + KT)
            for t in range(NT + 1):
                if t < NT:
                    if t >= 2:
                        pe.wait_ge(S("rows_ready"), t - 1 + NT)
                    for c in range(2):
                        last = products(pair[t % 2][:, c * HALF:(c + 1) * HALF],
                                        [(regC[:, k, t * P:(t + 1) * P], ring[:, 2 + c, k]) for k in range(KT)])
                    last.then_inc(S("o_rows_ready"), 1)
                if t >= 1:
                    pe.wait_ge(S("rows_normed"), t + NT)
                    if t >= 3:
                        pe.wait_ge(S("rows_taken"), t - 2 + NT)
                    for k in range(KT):
                        last = nc.tensor.transpose(pair[2 + (t - 1) % 2][:, k * P:(k + 1) * P],
                                                   hx2[(t - 1) % 2][:, k * P:(k + 1) * P], ident)
                    last.then_inc(S("rows_turned"), 1)
            slot_done(pe, 2)
            slot_done(pe, 3)

            for t in range(2):
                pe.wait_ge(S("mrow_normed"), t + 1)
                pe.wait_ge(S("rows_taken"), NT + NT)
                for k in range(KT):
                    last = nc.tensor.transpose(pair[2 + t][:, k * P:(k + 1) * P], mrow[t][:, k * P:(k + 1) * P], ident)
                last.then_inc(S("m2_turned"), 1)
            slot_ready(pe, 0)
            slot_ready(pe, 1)
            pe.wait_ge(S("m2_taken"), 2)
            for t in range(2):
                for c in range(2):
                    last = products(pair[t][:, c * HALF:(c + 1) * HALF],
                                    [(mT2[:, k, t * P:(t + 1) * P], ring[:, c, k]) for k in range(KT)])
                last.then_inc(S("kv2_ready"), 1)
            slot_done(pe, 0)
            slot_done(pe, 1)
            slot_ready(pe, 2)
            for t in range(NT):
                if t >= 2:
                    pe.wait_ge(S("q2_taken"), t - 1)
                products(pair[2 + t % 2][:, 0:HALF], [(regA[:, k, t * P:(t + 1) * P], ring[:, 2, k]) for k in range(KT)]
                         ).then_inc(S("q2_ready"), 1)
            slot_done(pe, 2)
            pe.wait_ge(once("k2_normed"), nth("k2_normed", 1))
            pe.wait_ge(S("kv2_taken"), 2)
            for h in range(MH):
                for t in range(2):
                    last = nc.tensor.transpose(pair[0][:, (2 * h + t) * P:(2 * h + t + 1) * P],
                                               kvM[t][:, h * P:(h + 1) * P], ident)
            last.then_inc(once("k2_turned"), 1)
            pe.wait_ge(S("q2_taken"), NT)
            for t in range(NT):
                pe.wait_ge(S("q2_normed"), t + 1)
                if t >= 2:
                    pe.wait_ge(S("q2t_taken"), t - 1)
                for h in range(MH):
                    last = nc.tensor.transpose(pair[2 + t % 2][:, h * P:(h + 1) * P], qM[:, t, h * P:(h + 1) * P], ident)
                last.then_inc(S("q2_turned"), 1)
            pe.wait_ge(once("k2t_taken"), nth("k2t_taken", 1))
            pe.wait_ge(S("q2t_taken"), NT)

            def xb_scores(t):
                if t >= 2:
                    pe.wait_ge(S("mem_exp"), t - 1 + NT)
                for h in range(MH):
                    last = nc.tensor.matmul(pair[t % 2][:, h * MEM:(h + 1) * MEM], qF2[:, h, t * P:(t + 1) * P],
                                            kF2[:, h], start=True, stop=True)
                last.then_inc(S("mem_scores"), 1)

            xb_scores(0)
            for t in range(NT):
                if t + 1 < NT:
                    xb_scores(t + 1)
                pe.wait_ge(S("mem_probs"), t + 1 + NT)
                if t >= 1:
                    pe.wait_ge(S("probs_t_taken"), t + NT)
                for n in range(8):
                    last = nc.tensor.transpose(pair[2][:, n * P:(n + 1) * P], ex2[t % 2][:, n * P:(n + 1) * P], ident)
                last.then_inc(S("mem_turned"), 1)
                if t % 4 == 3:
                    pe.wait_ge(S("probs_t_taken"), t + 1 + NT)
                    for h in range(MH):
                        n = MH * (t // 4) + h
                        if n >= 2:
                            pe.wait_ge(S("co_taken"), n - 1)
                        products(pair[3][:, (h % 2) * HALF:(h % 2 + 1) * HALF],
                                 [(kvM[m][:, HALF + h * P:HALF + (h + 1) * P], pT2[:, 2 * h + m]) for m in range(2)]
                                 ).then_inc(S("co_ready"), 1)
            slot_ready(pe, 3)
            pe.wait_ge(S("co_taken"), 8)
            w_co = ring[:, 3].rearrange("p k n -> p (k n)").rearrange("p (k n) -> p k n", n=D)
            for t in range(NT + 1):
                if t < NT:
                    if t >= 2:
                        pe.wait_ge(S("rows_ready"), t - 1 + 2 * NT)
                    for c in range(2):
                        last = products(pair[t % 2][:, c * HALF:(c + 1) * HALF],
                                        [(oF2[:, k, t * P:(t + 1) * P], w_co[:, k, c * HALF:(c + 1) * HALF])
                                         for k in range(MH)])
                    last.then_inc(S("o_rows_ready"), 1)
                if t >= 1:
                    pe.wait_ge(S("rows_normed"), t + 2 * NT)
                    if t >= 3:
                        pe.wait_ge(S("rows_taken"), t - 2 + 2 * NT)
                    for k in range(KT):
                        last = nc.tensor.transpose(pair[2 + (t - 1) % 2][:, k * P:(k + 1) * P],
                                                   hx3[(t - 1) % 2][:, k * P:(k + 1) * P], ident)
                    last.then_inc(S("rows_turned"), 1)
            slot_done(pe, 3)
            pe.wait_ge(S("rows_taken"), NT + 2 * NT)
            pe.wait_ge(S("rows_ready"), NT + 2 * NT)
            pe.wait_ge(S("vectors_in"), 64 + 224)
            for t in range(NT):
                last = products(pair[0][:, t * 36:(t + 1) * 36],
                                [(regA[:, k, t * P:(t + 1) * P], w_r[:, k]) for k in range(KT)])
            last.then_inc(once("router_done"), 1)
            pe.wait_ge(once("chosen"), nth("chosen", 1))
            pe.wait_ge(once("route_consts"), nth("route_consts", 1))
            for t in range(NT):
                last = products(pair[1][:, t * EXPERTS:(t + 1) * EXPERTS],
                                [(tri, Mb[:, t])] + [(ones, Mb[:, n]) for n in range(t)])
            last = products(pair[1][:, HALF:HALF + EXPERTS], [(ones, Mb[:, n]) for n in range(NT)])
            last.then_inc(once("ranked"), 1)

            def w_of(par, c):
                n = D if c == 2 else HALF
                return slots6[:, par, c].rearrange("p (k n) -> p k n", n=n)

            def up(e, par):
                n16 = (e // 2) * 16 + 16 if isinstance(e, int) else e * 8 + 16 - 8 * par
                pe.wait_ge(S("xgt_ready"), e + 1)
                for c in range(2):
                    pe.wait_ge(S(f"w_full{par}{c}"), n16)
                    products(pair[par][:, c * HALF:(c + 1) * HALF], [(xgT[par][:, k], w_of(par, c)[:, k]) for k in range(KT)]
                             ).then_inc(S(("gate_done", "up_done")[c]), 1)

            def turn_product(e):
                pe.wait_ge(S("a_made"), e + 1)
                pe.wait_ge(S("xgt_ready"), e + 2)
                for k in range(4):
                    last = nc.tensor.transpose(pair[3][:, k * P:(k + 1) * P], aa[:, k * P:(k + 1) * P], ident)
                last.then_inc(S("a_turned"), 1)

            def down(e, par):
                n16 = (e // 2) * 16 + 16 if isinstance(e, int) else e * 8 + 16 - 8 * par
                pe.wait_ge(S(f"w_full{par}2"), n16)
                pe.wait_ge(S("at_ready"), e + 1)
                pe.wait_ge(S("y_taken"), e + 1)
                for c in range(2):
                    last = products(pair[2][:, c * HALF:(c + 1) * HALF],
                                    [(aT[:, k], w_of(par, 2)[:, k, c * HALF:(c + 1) * HALF]) for k in range(4)])
                last.then_inc(S("down_done"), 1)

            pe.wait_ge(once("dest_ready"), nth("dest_ready", 1))
            pe.wait_ge(S("xg_full0"), 16)
            for k in range(KT):
                last = nc.tensor.transpose(pair[3][:, k * P:(k + 1) * P], xg[0][:, k * P:(k + 1) * P], ident)
            last.then_inc(S("xg_turned"), 1)
            up(0, 0)
            pe.wait_ge(S("xg_full1"), 16)
            for k in range(KT):
                last = nc.tensor.transpose(pair[3][:, k * P:(k + 1) * P], xg[1][:, k * P:(k + 1) * P], ident)
            last.then_inc(S("xg_turned"), 1)
            turn_product(0)
            with pe.Fori(0, EXPERTS // 2 - 1) as i:
                for m in range(2):
                    e, par = pe.snap(i * 2 + (1 + m)), 1 - m
                    up(e, par)
                    pe.wait_ge(S("at_ready"), e)
                    pe.wait_ge(S(f"xg_full{1 - par}"), i * 16 + 32)
                    for k in range(KT):
                        last = nc.tensor.transpose(pair[3][:, k * P:(k + 1) * P], xg[1 - par][:, k * P:(k + 1) * P], ident)
                    last.then_inc(S("xg_turned"), 1)
                    down(e - 1, 1 - par)
                    turn_product(e)
            up(EXPERTS - 1, 1)
            down(EXPERTS - 2, 0)
            pe.wait_ge(S("a_made"), EXPERTS)
            for k in range(4):
                last = nc.tensor.transpose(pair[3][:, k * P:(k + 1) * P], aa[:, k * P:(k + 1) * P], ident)
            last.then_inc(S("a_turned"), 1)
            down(EXPERTS - 1, 1)
            pe.wait_ge(once("over_ready"), nth("over_ready", 1))
            n_over = pe.value_load(over_i[0:1, 16:17], min_val=0, max_val=OVER)
            with pe.Fori(0, OVER) as j:
                with pe.If(j < n_over):
                    pe.wait_ge(S("xg_full0"), j * 16 + 16 + 8 * EXPERTS)
                    for k in range(KT):
                        last = nc.tensor.transpose(pair[3][:, k * P:(k + 1) * P], xg[0][:, k * P:(k + 1) * P], ident)
                    last.then_inc(S("xg_turned"), 1)
                    pe.wait_ge(S("o_w_full"), j * 48 + 48)
                    pe.wait_ge(S("xgt_ready"), j + 1 + EXPERTS)
                    for c in range(2):
                        last = products(pair[0][:, c * HALF:(c + 1) * HALF],
                                        [(xgT[0][:, k], w_of(0, c)[:, k]) for k in range(KT)])
                    last.then_inc(S("up_done"), 1)
                    pe.wait_ge(S("a_made"), j + 1 + EXPERTS)
                    for k in range(4):
                        last = nc.tensor.transpose(pair[3][:, k * P:(k + 1) * P], aa[:, k * P:(k + 1) * P], ident)
                    last.then_inc(S("a_turned"), 1)
                    pe.wait_ge(S("at_ready"), j + 1 + EXPERTS)
                    for c in range(2):
                        last = products(pair[2][:, c * HALF:(c + 1) * HALF],
                                        [(aT[:, k], w_of(0, 2)[:, k, c * HALF:(c + 1) * HALF]) for k in range(4)])
                    last.then_inc(S("down_done"), 1)

        @block.scalar
        def _(act):
            for name in ("lin_taken", "gate_taken", "r_taken", "i_taken", "qkv_taken", "exp_done", "wt_taken2", "o_taken", "y_taken"):
                act.sem_inc(S(name), 1)
            for t in range(NT + 2):
                act.wait_ge(S("xin_turned"), t + 1)
                dst = regA[:, 4:8, t * P:(t + 1) * P] if t < NT else memT[:, 4:8, (t - NT) * P:(t - NT + 1) * P]
                nc.scalar.copy(dst, pair[t % 2][:, HALF:].rearrange("p (k n) -> p k n", n=P)
                               ).then_inc(S("xt_copied_a"), 1)
            for f in range(2):
                act.wait_ge(S("xs_ready"), f + 1)
                nc.scalar.copy(xb[:, f], pair[f]).then_inc(S("xs_taken"), 1)
            for f in range(2):
                act.wait_ge(S("xs_ready"), 3 + f)
                nc.scalar.activation(gb[:, f], pair[2 + f], ACT.Tanh, scale=0.5).then_inc(S("gb_tanh"), 1)
            act.wait_ge(once("kv_ready"), nth("kv_ready", 1))
            nc.scalar.copy(kF.rearrange("p f n -> p (f n)"), pair[0][:, 0:HALF])
            nc.scalar.copy(vM.rearrange("p f n -> p (f n)"), pair[0][:, HALF:]).then_inc(once("kv_taken"), 1)
            act.wait_ge(once("wgm_turned"), nth("wgm_turned", 1))
            nc.scalar.copy(wT.rearrange("p h t -> p (h t)"), pair[1][:, 0:HALF]).then_inc(once("wt_taken"), 1)
            act.wait_ge(once("ct_turned"), nth("ct_turned", 1))
            cre = pair[2].rearrange("p (s n) -> p s n", n=P)
            nc.scalar.copy(CT[:, :, 0], cre)
            nc.scalar.mul(CT[:, :, 1], cre, -1.0).then_inc(once("ct_ready"), 1)
            act.wait_ge(once("ct_turned"), nth("ct_turned", 2))
            nc.scalar.mul(CT[:, :, 2], pair[3].rearrange("p (s n) -> p s n", n=P), -1.0).then_inc(once("ct_ready"), 1)
            for m in range(2):
                act.wait_ge(once("bt_turned"), nth("bt_turned", m + 1))
                nc.scalar.copy(BT[:, :, m], pair[m].rearrange("p (s n) -> p s n", n=P)).then_inc(once("bt_ready"), 1)
            for f in range(2):
                act.wait_ge(S("yd_ready"), f + 1)
                nc.scalar.activation(yb[:, f], yb[:, f], ACT.Gelu_apprx_tanh).then_inc(S("yb_ready"), 1)
            for f in range(2):
                act.wait_ge(S("glu_ready"), f + 1)
                act.wait_ge(once("half_glu_b"), nth("half_glu_b", 1))
                nc.scalar.activation(rot[f], pair[f], ACT.Tanh, bias=ssmp["t4"][:, f:f + 1], scale=0.5
                                     ).then_inc(S("glu_tanh"), 1)

            for t in range(NT):
                act.wait_ge(S("v_ready"), t + 1)
                nc.scalar.activation(vg[:, t], pair[t % 2][:, 0:HALF], ACT.Gelu_apprx_tanh).then_inc(S("vg_ready"), 1)
            for h in range(GM_HEADS):
                act.wait_ge(S("branch_b"), 2)
                if h >= 2:
                    act.wait_ge(S("ya_ready"), h - 1)
                act.wait_ge(S("u_ready"), h + 1)
                nc.scalar.activation(gu[h % 2], pair[3 * h % 4], ACT.Gelu_apprx_tanh).then_inc(S("u_taken"), 1)
                act.wait_ge(S("g_ready"), h + 1)
                nc.scalar.activation(th[h % 2], pair[(3 * h + 1) % 4], ACT.Tanh, scale=0.5).then_inc(S("ga_tanh"), 1)
            for f in range(2):
                act.wait_ge(S("qx_ready"), f + 1)
                nc.scalar.copy(qF[:, f], pair[f]).then_inc(S("qx_taken"), 1)
            for f in range(2):
                act.wait_ge(S("qx_ready"), 3 + f)
                nc.scalar.activation(regB[:, 6 + f], pair[2 + f], ACT.Tanh, scale=0.5).then_inc(S("gx_tanh"), 1)
            for t in range(NT):
                act.wait_ge(S("mem_max"), t + 1)
                if t >= 2:
                    act.wait_ge(S("mem_turned"), t - 1)
                    act.wait_ge(S("mem_probs"), t - 1)
                for h in range(XA_HEADS):
                    c = slice(h * MEM, (h + 1) * MEM)
                    last = nc.scalar.activation(ex[t % 2][:, c], pair[t % 2][:, c], ACT.Exp,
                                                bias=xa_nm[t % 2][:, h:h + 1], scale=XA_DIM ** -0.5,
                                                accum_out=xa_sum[t % 2][:, h:h + 1])
                last.then_inc(S("mem_exp"), 1)
                act.wait_ge(S("mem_turned"), t + 1)
                if t == 4:
                    act.wait_ge(S("xa_out"), 2)
                nc.scalar.copy(pT[:, :, (t % 4) * P:(t % 4 + 1) * P], pair[2].rearrange("p (n c) -> p n c", c=P)
                               ).then_inc(S("probs_t_taken"), 1)
            for t in range(NT):
                act.wait_ge(S("rows_ready"), t + 1)
                if t >= 1:
                    act.wait_ge(S("rows_rms"), t)
                nc.scalar.activation(sqj, xr[t % 2], ACT.Square, accum_out=sm["ss"][:, 0:1]).then_inc(S("rows_squared"), 1)
                act.drain()

            with act.Fori(0, KT // 2) as i:
                for par in range(2):
                    b = i * 2 + par
                    act.wait_ge(S("lin_ready"), b + 1)
                    act.wait_ge(S("xc_ready"), b + 1)
                    act.wait_ge(once("xp_zeroed"), nth("xp_zeroed", 1))
                    nc.scalar.copy(xp[par][:, 3:3 + SEQ], pair[0]).then_inc(S("lin_taken"), 1)
                    act.wait_ge(S("gate_ready"), b + 1)
                    act.wait_ge(S("lru_done"), b + 1)
                    nc.scalar.activation(gg, pair[1], ACT.Gelu_apprx_tanh).then_inc(S("gate_taken"), 1)
                    pc = pcol[par]
                    act.wait_ge(S("r_ready"), b + 1)
                    nc.scalar.activation(thr, pair[2], ACT.Tanh, bias=pc[:, 5:6], scale=0.5).then_inc(S("r_taken"), 1)
                    act.wait_ge(S("i_ready"), b + 1)
                    nc.scalar.activation(thi, pair[3], ACT.Tanh, bias=pc[:, 6:7], scale=0.5).then_inc(S("i_taken"), 1)
                    act.drain()
                    nc.scalar.activation(av, thr, ACT.Exp, bias=pc[:, 7:8], scale=pc[:, 7:8])
                    nc.scalar.activation(tl, thr, ACT.Tanh, bias=pc[:, 7:8], scale=pc[:, 7:8])
                    act.drain()
                    nc.scalar.activation(sq, av, ACT.Square).then_inc(S("a_ready"), 1)
                    act.wait_ge(S("one_less"), b + 1)
                    nc.scalar.activation(sq, sq, ACT.Sqrt, scale=-1.0).then_inc(S("root_ready"), 1)

            def merge_gates(count0):
                for m in range(KT):
                    act.wait_ge(S("merge_g"), count0 + m + 1)
                    if m >= 2:
                        act.wait_ge(S("merged"), count0 + m - 1)
                    nc.scalar.activation(mth[m % 2], pair[2 * (m % 2) + 1], ACT.Tanh, scale=0.5
                                         ).then_inc(S("merge_t"), 1)

            act.wait_ge(S("lru_done"), KT + 1)
            merge_gates(0)

            def project(h, t):
                act.wait_ge(S("qkv_ready"), h * 8 + t + 1)
                wait_unless_first(act, S("kt_turned"), h)
                nc.scalar.copy(qkv[:, t], pair[2][:, 0:384]).then_inc(S("qkv_taken"), 1)

            def prepare(h):
                act.drain()
                act.wait_ge(S("w_ready"), h * 8 + 1)
                nc.scalar.activation(sq8, qkv[:, :, 0:256], ACT.Square).then_inc(S("qk_squared"), 1)
                act.wait_ge(S("o_ready"), h * 8 + 1)
                nc.scalar.copy(vv, qkv[:, :, 256:384]).then_inc(S("v_copied"), 1)
                act.wait_ge(S("qt_turned"), h + 1)
                nc.scalar.copy(qT, pair[3]).then_inc(S("qt_ready"), 1)

            def values(h, j):
                n = (j + 1) * P
                act.wait_ge(S("wt_turned"), h * 8 + j + 1)
                act.wait_ge(S("o_ready"), h * 8 + j + 1)
                nc.scalar.copy(wmT[:, 0:n], pair[3][:, 0:n]).then_inc(S("wt_taken2"), 1)
                act.drain()
                act.wait_ge(S("ot_turned"), h + 1)
                act.wait_ge(S("o_ready"), h * 8 + j + 2)
                nc.scalar.copy(obuf[:, j], pair[2][:, HALF:HALF + P])
                nc.scalar.activation(junk, pair[2][:, HALF:HALF + P], ACT.Square, accum_out=ho["ss"][:, j:j + 1]
                                     ).then_inc(S("o_taken"), 1)

            def attend(h, then):
                for j in range(NT):
                    n = (j + 1) * P
                    act.wait_ge(S("nm_ready"), h * 8 + j + 1)
                    act.wait_ge(S("w_ready"), h * 8 + j + 1)
                    for m in range(2):
                        last = nc.scalar.activation(e2[:, m, 0:n], pair[m][:, 0:n], ACT.Exp, bias=ho["nm"][:, m:m + 1],
                                                    scale=0.125, accum_out=ho["sum"][:, m:m + 1])
                    last.then_inc(S("exp_done"), 1)
                    then(j)
                    if j:
                        values(h, j - 1)
                values(h, NT - 1)

            act.wait_ge(once("lam_sums"), nth("lam_sums", 1))
            nc.scalar.activation(ho["rc"][:, 0:2], ho["rl"][:, 0:2], ACT.Exp).then_inc(once("lam_exp"), 1)
            for t in range(NT):
                project(0, t)
            prepare(0)
            with act.Fori(0, HEADS - 1) as h:
                attend(h, lambda j: project(h + 1, j))
                prepare(h + 1)
            attend(HEADS - 1, lambda j: None)
            merge_gates(KT)
            for t in range(NT):
                act.wait_ge(S("rows_ready"), t + 1 + NT)
                if t >= 1:
                    act.wait_ge(S("rows_rms"), t + NT)
                nc.scalar.activation(sqj2, xr2[t % 2], ACT.Square, accum_out=sm["ss"][:, 0:1]).then_inc(S("rows_squared"), 1)
                act.drain()

            for t in range(2):
                act.wait_ge(S("vectors_in"), 32 + 192)
                nc.scalar.activation(ex2[t], mrow[t], ACT.Square, accum_out=cs["ss"][:, t:t + 1])
            last = act.drain()
            act.sem_inc(once("mrow_squared"), 1)
            for t in range(2):
                act.wait_ge(S("kv2_ready"), t + 1)
                nc.scalar.copy(kvM[t], pair[t]).then_inc(S("kv2_taken"), 1)
                act.wait_ge(S("mrow_normed"), 2)
                act.drain()
                for h in range(MH):
                    last = nc.scalar.activation(jk, kvM[t][:, h * P:(h + 1) * P], ACT.Square,
                                                accum_out=cs["ss"][:, 4 * t + h:4 * t + h + 1])
                    act.drain()
                act.sem_inc(once("k2_squared"), 1)
            for t in range(NT):
                act.wait_ge(S("q2_ready"), t + 1)
                if t == 0:
                    act.wait_ge(once("k2_normed"), nth("k2_normed", 1))
                    act.wait_ge(S("rows_taken"), NT + NT)
                for h in range(MH):
                    act.drain()
                    nc.scalar.activation(jk, pair[2 + t % 2][:, h * P:(h + 1) * P], ACT.Square,
                                         accum_out=cs["ss"][:, 4 * t + h:4 * t + h + 1])
                nc.scalar.copy(qM[:, t], pair[2 + t % 2][:, 0:HALF]).then_inc(S("q2_taken"), 1)
            act.wait_ge(once("k2_turned"), nth("k2_turned", 1))
            nc.scalar.activation(kF2.rearrange("p h m -> p (h m)"), pair[0], ACT.Copy, scale=col("ck_norm", 1)
                                 ).then_inc(once("k2t_taken"), 1)
            for t in range(NT):
                act.wait_ge(S("mem_max"), t + 1 + NT)
                if t >= 2:
                    act.wait_ge(S("mem_turned"), t - 1 + NT)
                    act.wait_ge(S("mem_probs"), t - 1 + NT)
                for h in range(MH):
                    c = slice(h * MEM, (h + 1) * MEM)
                    last = nc.scalar.activation(ex2[t % 2][:, c], pair[t % 2][:, c], ACT.Exp,
                                                bias=xa_nm[t % 2][:, h:h + 1], scale=P ** -0.5,
                                                accum_out=xa_sum[t % 2][:, h:h + 1])
                last.then_inc(S("mem_exp"), 1)
                act.wait_ge(S("mem_turned"), t + 1 + NT)
                if t == 4:
                    act.wait_ge(S("co_ready"), 4)
                nc.scalar.copy(pT2[:, :, (t % 4) * P:(t % 4 + 1) * P], pair[2].rearrange("p (n c) -> p n c", c=P)
                               ).then_inc(S("probs_t_taken"), 1)
                if t % 4 == 3:
                    for h in range(MH):
                        act.wait_ge(S("co_ready"), MH * (t // 4) + h + 1)
                        nc.scalar.copy(oF2[:, h, (t // 4) * HALF:(t // 4 + 1) * HALF],
                                       pair[3][:, (h % 2) * HALF:(h % 2 + 1) * HALF]).then_inc(S("co_taken"), 1)
            for t in range(NT):
                act.wait_ge(S("rows_ready"), t + 1 + 2 * NT)
                if t >= 1:
                    act.wait_ge(S("rows_rms"), t + 2 * NT)
                nc.scalar.activation(sqj3, xr3[t % 2], ACT.Square, accum_out=sm["ss"][:, 0:1]).then_inc(S("rows_squared"), 1)
                act.drain()
            act.wait_ge(once("group_less_max"), nth("group_less_max", 1))
            nc.scalar.activation(grp["e"], grp["e"], ACT.Exp).then_inc(once("group_exp"), 1)
            act.wait_ge(once("second_less_first"), nth("second_less_first", 1))
            nc.scalar.activation(r8["e2"], r8["e2"], ACT.Exp).then_inc(once("second_exp"), 1)

            def gate(e, par):
                wait_unless_first(act, S("a_made"), e)
                act.wait_ge(S("gate_done"), e + 1)
                nc.scalar.activation(ga, pair[par][:, 0:HALF], ACT.Tanh, scale=0.5).then_inc(S("ga_ready"), 1)

            def take_y(e, par, n16):
                if not (isinstance(n16, int) and n16 == 0):
                    act.wait_ge(S(f"y_stored{par}"), n16)
                act.wait_ge(S("down_done"), e + 1)
                nc.scalar.copy(ys[par], pair[2]).then_inc(S("y_taken"), 1)
                act.wait_ge(S("y_taken"), e + 2)
                rows0 = e * P
                act.dma_start(y_dram[bass.ds(rows0, P), :], ys[par]).then_inc(S(f"y_stored{par}"), 16)

            act.wait_ge(once("ranked"), nth("ranked", 1))
            act.wait_ge(S("xg_turned"), 1)
            gate(0, 0)
            gate(1, 1)
            take_y(0, 0, 0)
            gate(2, 0)
            take_y(1, 1, 0)
            with act.Fori(1, EXPERTS // 2 - 1) as i:
                for m in range(2):
                    e = act.snap(i * 2 + m)
                    gate(e + 1, 1 - m)
                    take_y(e, m, i * 16)
            gate(EXPERTS - 1, 1)
            take_y(EXPERTS - 2, 0, (EXPERTS // 2 - 1) * 16)
            take_y(EXPERTS - 1, 1, (EXPERTS // 2 - 1) * 16)
            act.wait_ge(once("over_ready"), nth("over_ready", 1))
            act.wait_ge(S("y_stored0"), 16 * EXPERTS // 2)
            n_over = act.value_load(over_i[0:1, 16:17], min_val=0, max_val=OVER)
            with act.Fori(0, OVER) as j:
                with act.If(j < n_over):
                    act.wait_ge(S("up_done"), j + 1 + EXPERTS)
                    nc.scalar.activation(ga, pair[0][:, 0:HALF], ACT.Tanh, scale=0.5).then_inc(S("ga_ready"), 1)
                    act.wait_ge(S("y_stored0"), j * 16 + 8 * EXPERTS)
                    act.wait_ge(S("down_done"), j + 1 + EXPERTS)
                    nc.scalar.copy(ys[0], pair[2]).then_inc(S("y_taken"), 1)

        @block.vector
        def _(v):
            for name in ("xc_ready", "lru_done", "ot_taken", "w_ready"):
                v.sem_inc(S(name), 1)
            def after(op, *a, **k):
                v.drain()
                return op(*a, **k)

            tt, ts, stt = nc.vector.tensor_tensor, nc.vector.tensor_scalar, nc.vector.scalar_tensor_tensor

            def sincos(x, c, s, tmp):
                k, y, y2, m, pc_, ps_ = tmp
                after(ts, k, x, 4.0 / TWO_PI, ROUND, ALU.mult, ALU.add)
                after(ts, k, k, ROUND, None, ALU.subtract)
                after(stt, y, k, -PI_A / 4, x, ALU.mult, ALU.add)
                after(stt, y, k, -PI_B / 4, y, ALU.mult, ALU.add)
                after(stt, y, k, -PI_C / 4, y, ALU.mult, ALU.add)
                after(tt, y2, y, y, ALU.mult)
                after(ts, pc_, y2, -1.0 / 3628800, None, ALU.mult)
                ts(ps_, y2, 1.0 / 362880, None, ALU.mult)
                for a, b in ((1.0 / 40320, -1.0 / 5040), (-1.0 / 720, 1.0 / 120), (1.0 / 24, -1.0 / 6)):
                    after(stt, pc_, pc_, a, y2, ALU.add, ALU.mult)
                    stt(ps_, ps_, b, y2, ALU.add, ALU.mult)
                after(stt, pc_, pc_, -0.5, y2, ALU.add, ALU.mult)
                stt(ps_, ps_, 1.0, y, ALU.add, ALU.mult)
                after(ts, pc_, pc_, 1.0, None, ALU.add)
                after(ts, m, k, 0.25, ROUND, ALU.mult, ALU.add)
                after(ts, m, m, ROUND, None, ALU.subtract)
                after(stt, m, m, -4.0, k, ALU.mult, ALU.add)
                after(stt, k, m, -1.0, m, ALU.mult, ALU.max)
                after(ts, y, k, -1.0, 2.0, ALU.mult, ALU.add)
                after(tt, y, y, m, ALU.mult)
                ts(k, k, -1.0, 1.0, ALU.mult, ALU.add)
                after(tt, c, pc_, k, ALU.mult)
                tt(s, ps_, k, ALU.mult)
                tt(y2, ps_, y, ALU.mult)
                tt(m, pc_, y, ALU.mult)
                after(tt, c, c, y2, ALU.subtract)
                tt(s, s, m, ALU.add)

            def exponential(dst, x, tmp, itmp):
                k, y, p = tmp
                after(ts, y, x, 88.0, -87.0, ALU.min, ALU.max)
                after(ts, k, y, float(np.log2(np.e)), ROUND, ALU.mult, ALU.add)
                after(ts, k, k, ROUND, None, ALU.subtract)
                after(stt, y, k, -LN2_A, y, ALU.mult, ALU.add)
                after(stt, y, k, -LN2_B, y, ALU.mult, ALU.add)
                after(ts, p, y, 1.0 / 5040, None, ALU.mult)
                for c in (1.0 / 720, 1.0 / 120, 1.0 / 24, 1.0 / 6, 0.5, 1.0):
                    after(stt, p, p, c, y, ALU.add, ALU.mult)
                ts(itmp, k, 127.0, float(2 ** 23), ALU.add, ALU.mult)
                after(ts, p, p, 1.0, None, ALU.add)
                after(tt, dst, p, itmp.bitcast(F32), ALU.mult)

            def rsqrt(dst, x, n):
                r, h, i = rs[0][:, 0:n], rs[1][:, 0:n], rs[2][:, 0:n]
                after(ts, i, x.bitcast(I32), 1, None, ALU.logical_shift_right)
                after(ts, i, i, -1.0, float(0x5f3759df), ALU.mult, ALU.add)
                v.drain()
                y = i.bitcast(F32)
                for step in range(3):
                    o = dst if step == 2 else r
                    tt(h, y, y, ALU.mult)
                    after(tt, h, h, x, ALU.mult)
                    after(ts, h, h, -0.5, 1.5, ALU.mult, ALU.add)
                    after(tt, o, y, h, ALU.mult)
                    v.drain()
                    y = o
            def turned_with_gain(t, count0, gain, dst):
                v.wait_ge(S("rows_turned"), count0 + t + 1)
                tt(dst[:, :, t * P:(t + 1) * P], pair[2 + t % 2].rearrange("p (k n) -> p k n", n=P),
                   col(gain).unsqueeze(2).broadcast_to([P, KT, P]), ALU.mult).then_inc(S("rows_taken"), 1)

            v.wait_ge(once("zeroed"), nth("zeroed", 1))
            v.wait_ge(S("params_in"), PARAMS)
            nc.vector.tensor_copy(rows[96:104, :], irows[96:104, :]).then_inc(once("rows_filled"), 1)
            v.wait_ge(once("cols_turned"), nth("cols_turned", 1))
            nc.vector.tensor_copy(cols, pair[3][:, 0:P]).then_inc(once("cols_ready"), 1)
            v.drain()
            c8 = cols[:, 8:64].rearrange("p (m b) -> p m b", b=8)
            nc.vector.tensor_copy(tab8[:, 0:5], c8[:, 0:5])
            ts(tab8[:, 5:7], c8[:, 5:7], 0.5, None, ALU.mult)
            lam = col("lru_lambda")
            x, e, z, z2, pz, mx_ = (tiny[n][:, 0:KT] for n in "abcdef")
            ts(mx_, lam, -1.0, 0.0, ALU.mult, ALU.max)
            after(stt, x, lam, -1.0, lam, ALU.mult, ALU.min)
            exponential(e, x, (z, z2, pz), rs[2][:, 0:KT])
            after(ts, z, e, 2.0, None, ALU.add)
            after(nc.vector.reciprocal, z, z)
            after(tt, z, z, e, ALU.mult)
            after(tt, z2, z, z, ALU.mult)
            after(ts, pz, z2, 1.0 / 17, None, ALU.mult)
            for n in (15, 13, 11, 9, 7, 5, 3):
                after(stt, pz, pz, 1.0 / n, z2, ALU.add, ALU.mult)
            after(stt, pz, pz, 1.0, z, ALU.add, ALU.mult)
            after(stt, pz, pz, 2.0, mx_, ALU.mult, ALU.add)
            after(ts, tab8[:, 7], pz, -4.0, None, ALU.mult)
            ts(subln, col("subln", 1), 0.8, None, ALU.mult)
            for n, f in enumerate(INV_FREQ):
                ts(tiny["g"].rearrange("p (t d) -> p t d", d=8)[:, :, n], col("positions"), f, None, ALU.mult)
            v.drain()
            sincos(tiny["g"], rope_c.rearrange("p t d -> p (t d)"), rope_s.rearrange("p t d -> p (t d)"),
                   [tiny[n] for n in "abcdef"])
            for t in range(NT + 2):
                v.wait_ge(S("xin_turned"), t + 1)
                dst = regA[:, 0:4, t * P:(t + 1) * P] if t < NT else memT[:, 0:4, (t - NT) * P:(t - NT + 1) * P]
                nc.vector.tensor_copy(dst, pair[t % 2][:, 0:HALF].rearrange("p (k n) -> p k n", n=P)
                                      ).then_inc(S("xt_copied_v"), 1)
            for f in range(2):
                v.wait_ge(S("gb_tanh"), f + 1)
                stt(gb[:, f], gb[:, f], 1.0, pair[2 + f], ALU.add, ALU.mult).then_inc(S("xs_taken"), 1)
            q = ssmp
            v.wait_ge(S("ssm_in"), 64)
            three = [tiny[n][:, 0:ST] for n in "abc"]
            exponential(q["step"], lstep, three, rs[2][:, 0:ST])
            after(tt, q["t1"], col("lam_re"), q["step"], ALU.mult)
            exponential(q["r"], q["t1"], three, rs[2][:, 0:ST])
            after(tt, q["ang"], col("lam_im"), q["step"], ALU.mult)
            sincos(q["ang"], q["c"], q["s"], [tiny[n][:, 0:ST] for n in "abcdef"])
            after(tt, q["lr"], q["r"], q["c"], ALU.mult)
            tt(q["li"], q["r"], q["s"], ALU.mult)
            after(ts, q["lr"], q["lr"], -1.0, None, ALU.add)
            lre, lim = col("lam_re"), col("lam_im")
            after(tt, q["t1"], lre, lre, ALU.mult)
            tt(q["t2"], lim, lim, ALU.mult)
            after(tt, q["den"], q["t1"], q["t2"], ALU.add)
            after(nc.vector.reciprocal, q["den"], q["den"])
            tt(q["t1"], q["lr"], lre, ALU.mult)
            tt(q["t2"], q["li"], lim, ALU.mult)
            tt(q["t3"], q["li"], lre, ALU.mult)
            tt(q["t4"], q["lr"], lim, ALU.mult)
            after(tt, q["t1"], q["t1"], q["t2"], ALU.add)
            tt(q["t3"], q["t3"], q["t4"], ALU.subtract)
            after(tt, q["br"], q["t1"], q["den"], ALU.mult)
            tt(q["bi"], q["t3"], q["den"], ALU.mult)
            wide16 = lambda a: a.unsqueeze(2).broadcast_to([P, ST, 16])
            after(tt, b_bar[:, 0], b_raw[:, 0], wide16(q["br"]), ALU.mult)
            tt(b_bar[:, 1], b_raw[:, 1], wide16(q["br"]), ALU.mult)
            tt(b_tmp, b_raw[:, 1], wide16(q["bi"]), ALU.mult)
            after(tt, b_bar[:, 0], b_bar[:, 0], b_tmp, ALU.subtract)
            after(tt, b_tmp, b_raw[:, 0], wide16(q["bi"]), ALU.mult)
            after(tt, b_bar[:, 1], b_bar[:, 1], b_tmp, ALU.add)
            v.drain()
            for m in range(2):
                for a in range(2):
                    for j in range(4):
                        last = nc.vector.tensor_copy(
                            blockB[64 * a:64 * a + 64, j:ST:4, m, 32 * j + 16 * a:32 * j + 16 * a + 16],
                            b_bar[64 * a:64 * a + 64, m, j:ST:4])
            last.then_inc(once("bbar_placed"), 1)
            nc.vector.tensor_copy(phase[1][0], q["c"])
            nc.vector.tensor_copy(phase[1][1], q["s"])
            n = 1
            while n < 512:
                c, s = phase[n]
                after(tt, q["t1"], c, c, ALU.mult)
                tt(q["t2"], s, s, ALU.mult)
                tt(q["t3"], c, s, ALU.mult)
                after(tt, phase[2 * n][0], q["t1"], q["t2"], ALU.subtract)
                ts(phase[2 * n][1], q["t3"], 2.0, None, ALU.mult)
                n *= 2
            after(nc.vector.memset, tabc[:, :, 0:1], 1.0)
            nc.vector.memset(tabs[:, :, 0:1], 0.0)
            n = 1
            t0, t1 = rot[0].rearrange("p (s n) -> p s n", n=P), rot[1].rearrange("p (s n) -> p s n", n=P)
            while n < P:
                c, s = (x.unsqueeze(2).broadcast_to([P, ST, n]) for x in phase[n])
                tc, tsn = tabc[:, :, 0:n], tabs[:, :, 0:n]
                after(tt, t0[:, :, 0:n], tsn, s, ALU.mult)
                tt(t1[:, :, 0:n], tc, s, ALU.mult)
                tt(tabc[:, :, n:2 * n], tc, c, ALU.mult)
                tt(tabs[:, :, n:2 * n], tsn, c, ALU.mult)
                after(tt, tabc[:, :, n:2 * n], tabc[:, :, n:2 * n], t0[:, :, 0:n], ALU.subtract)
                tt(tabs[:, :, n:2 * n], tabs[:, :, n:2 * n], t1[:, :, 0:n], ALU.add)
                n *= 2
            for s in range(ST):
                if s:
                    v.wait_ge(S("h_ready"), s)
                after(nc.vector.tensor_copy, wcos[:, 0:P], tabc[:, s])
                nc.vector.tensor_copy(wsin[:, 0:P], tabs[:, s])
                for n in (128, 256, 512):
                    pc_, ps_ = phase[n][0][:, s:s + 1], phase[n][1][:, s:s + 1]
                    after(ts, rot[0][:, 0:n], wsin[:, 0:n], ps_, None, ALU.mult)
                    ts(rot[1][:, 0:n], wcos[:, 0:n], ps_, None, ALU.mult)
                    after(stt, wcos[:, n:2 * n], wcos[:, 0:n], pc_, rot[0][:, 0:n], ALU.mult, ALU.subtract)
                    stt(wsin[:, n:2 * n], wsin[:, 0:n], pc_, rot[1][:, 0:n], ALU.mult, ALU.add)
                v.wait_ge(S("bx_ready"), s + 1)
                after(tt, rot[0], pair[0], wcos, ALU.mult)
                tt(rot[1], pair[1], wsin, ALU.mult)
                tt(rot[2], pair[1], wcos, ALU.mult)
                tt(rot[3], pair[0], wsin, ALU.mult).then_inc(S("bx_taken"), 1)
                after(tt, rot[0], rot[0], rot[1], ALU.add)
                tt(rot[2], rot[2], rot[3], ALU.subtract)
                r = q["r"][:, s:s + 1].broadcast_to([P, SEQ])
                after(nc.vector.tensor_tensor_scan, gr, r, rot[0], 0.0, ALU.mult, ALU.add)
                nc.vector.tensor_tensor_scan(gi, r, rot[2], 0.0, ALU.mult, ALU.add).then_inc(S("scanned"), 1)
                if s % 4 == 3:
                    f = s // 4
                    v.wait_ge(S("h_used"), s + 1)
                    stt(yb[:, f], xb[:, f], cols[:, ROW["ssm_d"] + f:ROW["ssm_d"] + f + 1], pair[2 + f],
                        ALU.mult, ALU.add).then_inc(S("yd_ready"), 1)
            ts(q["t4"][:, 0:2], col("glu_b", 2), 0.5, None, ALU.mult).then_inc(once("half_glu_b"), 1)
            for f in range(2):
                v.wait_ge(S("glu_tanh"), f + 1)
                after(stt, rot[2 + f], rot[f], 1.0, yb[:, f], ALU.add, ALU.mult)
                after(stt, regB[:, 4 + f], rot[2 + f], 0.25, gb[:, f], ALU.mult, ALU.mult).then_inc(S("branch_b"), 1)
            for t in range(NT):
                v.wait_ge(S("vg_ready"), t + 1)
                for h in range(GM_HEADS):
                    nc.vector.bn_stats(gm_st[:, 4 * t + h], vg[:, t, h * P:(h + 1) * P])
            v.drain()
            for n in range(32):
                nc.vector.bn_aggr(gm_mv[:, n], gm_st[:, n])
            after(ts, tiny["a"][:, 0:32], gm_mv[:, :, 1], LN_EPS, None, ALU.add)
            rsqrt(gm_r, tiny["a"][:, 0:32], 32)
            v.wait_ge(S("vectors_in"), 32)
            for t in range(NT):
                for h in range(GM_HEADS):
                    n = 4 * t + h
                    ts(vh[:, t, h * P:(h + 1) * P], vg[:, t, h * P:(h + 1) * P], gm_mv[:, n, 0:1], gm_r[:, n:n + 1],
                       ALU.subtract, ALU.mult)
                after(tt, vh[:, t], vh[:, t], gm_g, ALU.mult)
                after(tt, vh[:, t], vh[:, t], gm_b, ALU.add).then_inc(S("vh_ready"), 1)
            for h in range(GM_HEADS):
                v.wait_ge(S("ga_tanh"), h + 1)
                after(stt, th[h % 2], th[h % 2], 1.0, pair[(3 * h + 1) % 4], ALU.add, ALU.mult).then_inc(S("g_taken"), 1)
                v.wait_ge(S("mix_ready"), h + 1)
                after(tt, mb.rearrange("p (c t) -> p c t", t=P), pair[(3 * h + 2) % 4].rearrange("p (c t) -> p c t", t=P),
                      gm_bs[:, h].unsqueeze(1).broadcast_to([P, NT, P]), ALU.add).then_inc(S("mix_taken"), 1)
                v.wait_ge(S("u_taken"), h + 1)
                tt(gu[h % 2], gu[h % 2], th[h % 2], ALU.mult)
                after(stt, regB[:, h], mb, 0.5, gu[h % 2], ALU.mult, ALU.mult).then_inc(S("ya_ready"), 1)
            for f in range(2):
                v.wait_ge(S("gx_tanh"), f + 1)
                stt(regB[:, 6 + f], regB[:, 6 + f], 1.0, pair[2 + f], ALU.add, ALU.mult).then_inc(S("qx_taken"), 1)
            for t in range(NT + 1):
                if t < NT:
                    v.wait_ge(S("mem_scores"), t + 1)
                    nc.vector.tensor_reduce(sm["mx"][:, 0:4], pair[t % 2].rearrange("p (h m) -> p h m", m=MEM), AX.X, ALU.max)
                    after(ts, xa_nm[t % 2], sm["mx"][:, 0:4], -(XA_DIM ** -0.5), None, ALU.mult).then_inc(S("mem_max"), 1)
                if t in (4, 8):
                    for f in range(2):
                        o = regB[:, 6 + f, (t // 4 - 1) * HALF:(t // 4) * HALF]
                        v.wait_ge(S("xa_out"), 2 * (t // 4 - 1) + f + 1)
                        stt(o, pair[3][:, f * HALF:(f + 1) * HALF], 0.5, o, ALU.mult, ALU.mult).then_inc(S("yx_ready"), 1)
                if t < NT:
                    v.wait_ge(S("mem_exp"), t + 1)
                    after(nc.vector.reciprocal, sm["rc"][:, 0:4], xa_sum[t % 2])
                    p3 = ex[t % 2].rearrange("p (h m) -> p h m", m=MEM)
                    after(tt, p3, p3, sm["rc"][:, 0:4].unsqueeze(2).broadcast_to([P, XA_HEADS, MEM]), ALU.mult
                          ).then_inc(S("mem_probs"), 1)
            for t in range(NT + 1):
                if t < NT:
                    x = xr[t % 2]
                    v.wait_ge(S("o_rows_ready"), t + 1)
                    v.wait_ge(S(f"rows_full{t % 2}"), 16 * (t // 2 + 1))
                    stt(x, x, DN_ALPHA, pair[t % 2], ALU.mult, ALU.add).then_inc(S("xr_added"), 1)
                    v.drain()
                    for c in range(2):
                        nc.vector.bn_stats(gm_st[:, c], x[:, c * HALF:(c + 1) * HALF])
                    after(nc.vector.bn_aggr, gm_mv[:, 0], gm_st[:, 0:2])
                    after(ts, sm["v1"][:, 0:1], gm_mv[:, 0, 1:2], LN_EPS, None, ALU.add)
                    rsqrt(sm["r1"][:, 0:1], sm["v1"][:, 0:1], 1)
                    after(ts, x, x, gm_mv[:, 0, 0:1], sm["r1"][:, 0:1], ALU.subtract, ALU.mult).then_inc(S("xr_normed"), 1)
                if t >= 1:
                    turned_with_gain(t - 1, 0, "norm_mix", regA)
                if t < NT:
                    v.wait_ge(S("rows_squared"), t + 1)
                    after(ts, sm["v1"][:, 0:1], sm["ss"][:, 0:1], 1.0 / D, EPS, ALU.mult, ALU.add).then_inc(S("rows_rms"), 1)
                    rsqrt(sm["r2"][:, 0:1], sm["v1"][:, 0:1], 1)
                    if t >= 2:
                        v.wait_ge(S("rows_turned"), t - 1)
                    after(ts, hx[t % 2], xr[t % 2], sm["r2"][:, 0:1], None, ALU.mult).then_inc(S("rows_normed"), 1)
            v.wait_ge(S("rows_turned"), NT)
            for par in range(2):
                v.wait_ge(S(f"rows_stored{par}"), 16 * NT // 2)
            for n in range(2):
                last = nc.vector.memset(xp[n][:, 0:3], 0.0)
            last.then_inc(once("xp_zeroed"), 1)
            with v.Fori(0, KT // 2) as i:
                for par in range(2):
                    b = i * 2 + par
                    pc = pcol[par]
                    x, o = xp[par], xc[par]
                    v.drain()
                    nc.vector.tensor_copy(pc, tab8[:, :, bass.ds(b, 1)].rearrange("p m o -> p (m o)"))
                    v.drain()
                    v.wait_ge(S("lin_taken"), b + 2)
                    ts(o, x[:, 0:SEQ], pc[:, 1:2], pc[:, 0:1], ALU.mult, ALU.add)
                    for j in range(1, 4):
                        last = after(stt, o, x[:, j:j + SEQ], pc[:, 1 + j:2 + j], o, ALU.mult, ALU.add)
                    last.then_inc(S("xc_ready"), 1)
                    v.drain()
                    v.wait_ge(S("a_ready"), b + 1)
                    stt(sq, sq, 1.0, tl, ALU.add, ALU.mult).then_inc(S("one_less"), 1)
                    stt(thi, thi, 1.0, o, ALU.add, ALU.mult)
                    v.drain()
                    v.wait_ge(S("root_ready"), b + 1)
                    stt(thi, thi, 0.5, sq, ALU.mult, ALU.mult)
                    after(nc.vector.tensor_tensor_scan, thr, av, thi, 0.0, ALU.mult, ALU.add)
                    after(tt, regB[:, bass.ds(b, 1)].rearrange("p o n -> p (o n)"), thr, gg, ALU.mult
                          ).then_inc(S("lru_done"), 1)
            for m in range(KT):
                v.wait_ge(S("merge_y"), m + 1)
                v.wait_ge(S("merge_t"), m + 1)
                after(stt, regC[:, m], mth[m % 2], 1.0, pair[2 * (m % 2)], ALU.add, ALU.mult).then_inc(S("merged"), 1)
            v.wait_ge(S("vectors_in"), 128 + 64)
            for n in range(2):
                tt(junk[:, 64 * n:64 * n + 64], lam4[:, 2 * n], lam4[:, 2 * n + 1], ALU.mult)
            after(nc.vector.tensor_reduce, ho["rl"][:, 0:2], junk.rearrange("p (n d) -> p n d", n=2), AX.X, ALU.add
                  ).then_inc(once("lam_sums"), 1)
            v.wait_ge(once("lam_exp"), nth("lam_exp", 1))
            after(tt, neg_lam, ho["rc"][:, 1:2], ho["rc"][:, 0:1], ALU.subtract)
            after(ts, neg_lam, neg_lam, -0.2, None, ALU.add)

            def norm_qk(h):
                v.drain()
                wait_unless_first(v, S("wt_turned"), h * 8)
                v.wait_ge(S("qk_squared"), h + 1)
                qk = qkv[:, :, 0:256].rearrange("p t (m d) -> p t m d", d=64)
                nc.vector.tensor_reduce(hs["ss"], sq8.rearrange("p t (m d) -> p (t m) d", d=64), AX.X, ALU.add)
                after(ts, hs["v1"], hs["ss"], 1.0 / 64, EPS, ALU.mult, ALU.add)
                rsqrt(hs["r"], hs["v1"], 32)
                after(tt, qk, qk, hs["r"].rearrange("p (t m) -> p t m", m=4).unsqueeze(3).broadcast_to([P, NT, 4, 64]),
                      ALU.mult)
                after(tt, qkv[:, :, 0:256], qkv[:, :, 0:256],
                      qk_gain.rearrange("p m d -> p (m d)").unsqueeze(1).broadcast_to([P, NT, 256]), ALU.mult)
                x1, x2 = qk[:, :, :, 0:8], qk[:, :, :, 8:16]
                c, s = (x.unsqueeze(2).broadcast_to([P, NT, 4, 8]) for x in (rope_c, rope_s))
                after(tt, rope_t[0], x1, c, ALU.mult)
                tt(rope_t[1], x2, s, ALU.mult)
                tt(rope_t[2], x2, c, ALU.mult)
                tt(rope_t[3], x1, s, ALU.mult)
                after(tt, x1, rope_t[0], rope_t[1], ALU.subtract)
                tt(x2, rope_t[2], rope_t[3], ALU.add).then_inc(S("qk_normed"), 1)
                v.wait_ge(S("kt_turned"), h + 1)
                nc.vector.tensor_copy(kT, pair[0]).then_inc(S("kt_ready"), 1)

            def attend(h):
                for j in range(NT):
                    n = (j + 1) * P
                    v.wait_ge(S("s_ready"), h * 8 + j + 1)
                    nc.vector.memset(psum[0:64, 0:2, j * P + 64:(j + 1) * P], -1e30)
                    after(nc.vector.tensor_reduce, ho["mx"][:, 0:2], psum[:, 0:2, 0:n], AX.X, ALU.max)
                    after(ts, ho["nm"][:, 0:2], ho["mx"][:, 0:2], -0.125, None, ALU.mult).then_inc(S("nm_ready"), 1)
                    v.drain()
                    v.wait_ge(S("exp_done"), h * 8 + j + 2)
                    nc.vector.reciprocal(ho["rc"][:, 0:2], ho["sum"][:, 0:2])
                    after(tt, ho["rl"][:, 0:1], ho["rc"][:, 1:2], neg_lam, ALU.mult)
                    v.drain()
                    if j >= 2:
                        v.wait_ge(S("wt_turned"), h * 8 + j - 1)
                    ts(wmix[j % 2][:, 0:n], e2[:, 0, 0:n], ho["rc"][:, 0:1], None, ALU.mult)
                    after(stt, wmix[j % 2][:, 0:n], e2[:, 1, 0:n], ho["rl"][:, 0:1], wmix[j % 2][:, 0:n],
                          ALU.mult, ALU.add).then_inc(S("w_ready"), 1)

            def norm_o(h, dst):
                v.drain()
                v.wait_ge(S("o_taken"), h * 8 + 8 + 1)
                ts(ho["v1"], ho["ss"], 1.0 / P, EPS, ALU.mult, ALU.add)
                rsqrt(ho["r"], ho["v1"], 8)
                after(tt, obuf, obuf, ho["r"].unsqueeze(2).broadcast_to([P, NT, P]), ALU.mult).then_inc(S("o_normed"), 1)
                v.wait_ge(S("ot_turned"), h + 2)
                ts(dst, pair[1], subln[:, 0:1], None, ALU.mult).then_inc(S("ot_taken"), 1)

            norm_qk(0)
            with v.Fori(0, HEADS - 1) as h:
                attend(h)
                norm_qk(h + 1)
                norm_o(h, regB[:, bass.ds(h, 1)].rearrange("p o n -> p (o n)"))
            attend(HEADS - 1)
            norm_o(HEADS - 1, regB[:, HEADS - 1])
            v.wait_ge(S("ot_turned"), HEADS + 1)
            v.drain()
            v.sem_inc(once("heads_done"), 1)
            for m in range(KT):
                v.wait_ge(S("merge_y"), m + 1 + KT)
                v.wait_ge(S("merge_t"), m + 1 + KT)
                after(stt, mtmp, mth[m % 2], 1.0, pair[2 * (m % 2)], ALU.add, ALU.mult)
                after(tt, regC[:, m], regC[:, m], mtmp, ALU.add).then_inc(S("merged"), 1)
            for t in range(NT + 1):
                if t < NT:
                    x = xr2[t % 2]
                    v.wait_ge(S("o_rows_ready"), t + 1 + NT)
                    v.wait_ge(S(f"rows_full{t % 2}"), 16 * (t // 2 + 1) + 8 * NT)
                    stt(x, pair[t % 2], 0.5, x, ALU.mult, ALU.add).then_inc(S("rows_ready"), 1)
                if t >= 1:
                    turned_with_gain(t - 1, 1 * NT, "norm_cx", regA)
                if t < NT:
                    v.wait_ge(S("rows_squared"), t + 1 + NT)
                    after(ts, sm["v1"][:, 0:1], sm["ss"][:, 0:1], 1.0 / D, EPS, ALU.mult, ALU.add).then_inc(S("rows_rms"), 1)
                    rsqrt(sm["r2"][:, 0:1], sm["v1"][:, 0:1], 1)
                    if t >= 2:
                        v.wait_ge(S("rows_turned"), t - 1 + NT)
                    after(ts, hx2[t % 2], xr2[t % 2], sm["r2"][:, 0:1], None, ALU.mult).then_inc(S("rows_normed"), 1)
            v.wait_ge(once("mrow_squared"), nth("mrow_squared", 1))
            ts(cs["v1"][:, 0:2], cs["ss"][:, 0:2], 1.0 / D, EPS, ALU.mult, ALU.add)
            rsqrt(cs["r"][:, 0:2], cs["v1"][:, 0:2], 2)
            for t in range(2):
                after(ts, mrow[t], mrow[t], cs["r"][:, t:t + 1], None, ALU.mult).then_inc(S("mrow_normed"), 1)
            for t in range(2):
                v.wait_ge(S("m2_turned"), t + 1)
                tt(mT2[:, :, t * P:(t + 1) * P], pair[2 + t].rearrange("p (k n) -> p k n", n=P),
                   col("norm_mem").unsqueeze(2).broadcast_to([P, KT, P]), ALU.mult).then_inc(S("m2_taken"), 1)
            v.wait_ge(once("k2_squared"), nth("k2_squared", 2))
            after(ts, cs["v1"][:, 0:8], cs["ss"][:, 0:8], 1.0 / P, EPS, ALU.mult, ALU.add)
            rsqrt(cs["r"][:, 0:8], cs["v1"][:, 0:8], 8)
            for t in range(2):
                k3 = kvM[t][:, 0:HALF].rearrange("p (h d) -> p h d", d=P)
                last = after(tt, k3, k3, cs["r"][:, 4 * t:4 * t + 4].unsqueeze(2).broadcast_to([P, MH, P]), ALU.mult)
            last.then_inc(once("k2_normed"), 1)
            v.wait_ge(S("q2_taken"), NT)
            after(ts, cs["v1"], cs["ss"], 1.0 / P, EPS, ALU.mult, ALU.add)
            rsqrt(cs["r"], cs["v1"], 32)
            for t in range(NT + 1):
                if t < NT:
                    q3 = qM[:, t].rearrange("p (h d) -> p h d", d=P)
                    after(tt, q3, q3, cs["r"][:, 4 * t:4 * t + 4].unsqueeze(2).broadcast_to([P, MH, P]), ALU.mult
                          ).then_inc(S("q2_normed"), 1)
                if t >= 1:
                    v.wait_ge(S("q2_turned"), t)
                    ts(qF2[:, :, (t - 1) * P:t * P], pair[2 + (t - 1) % 2][:, 0:HALF].rearrange("p (h n) -> p h n", n=P),
                       col("cq_norm", 1), None, ALU.mult).then_inc(S("q2t_taken"), 1)
            for t in range(NT):
                v.wait_ge(S("mem_scores"), t + 1 + NT)
                nc.vector.tensor_reduce(sm["mx"][:, 0:4], pair[t % 2].rearrange("p (h m) -> p h m", m=MEM), AX.X, ALU.max)
                after(ts, xa_nm[t % 2], sm["mx"][:, 0:4], -(P ** -0.5), None, ALU.mult).then_inc(S("mem_max"), 1)
                v.wait_ge(S("mem_exp"), t + 1 + NT)
                after(nc.vector.reciprocal, sm["rc"][:, 0:4], xa_sum[t % 2])
                p3 = ex2[t % 2].rearrange("p (h m) -> p h m", m=MEM)
                after(tt, p3, p3, sm["rc"][:, 0:4].unsqueeze(2).broadcast_to([P, MH, MEM]), ALU.mult
                      ).then_inc(S("mem_probs"), 1)
            for t in range(NT + 1):
                if t < NT:
                    x = xr3[t % 2]
                    v.wait_ge(S("o_rows_ready"), t + 1 + 2 * NT)
                    v.wait_ge(S(f"rows_full{t % 2}"), 16 * (t // 2 + 1) + 16 * NT)
                    tt(x, pair[t % 2], x, ALU.add).then_inc(S("rows_ready"), 1)
                if t >= 1:
                    turned_with_gain(t - 1, 2 * NT, "norm_ffn", regA)
                if t < NT:
                    v.wait_ge(S("rows_squared"), t + 1 + 2 * NT)
                    after(ts, sm["v1"][:, 0:1], sm["ss"][:, 0:1], 1.0 / D, EPS, ALU.mult, ALU.add).then_inc(S("rows_rms"), 1)
                    rsqrt(sm["r2"][:, 0:1], sm["v1"][:, 0:1], 1)
                    if t >= 2:
                        v.wait_ge(S("rows_turned"), t - 1 + 2 * NT)
                        v.wait_ge(S(f"h3_stored{t % 2}"), 16 * (t // 2))
                    after(ts, hx3[t % 2], xr3[t % 2], sm["r2"][:, 0:1], None, ALU.mult).then_inc(S("rows_normed"), 1)
            v.wait_ge(once("router_done"), nth("router_done", 1))
            v.wait_ge(once("route_consts"), nth("route_consts", 1))
            b3 = lambda a, n: a.unsqueeze(2).broadcast_to([P, NT, n])
            after(tt, logit, pair[0][:, 0:NT * 36].rearrange("p (t n) -> p t n", n=36),
                  b_r.unsqueeze(1).broadcast_to([P, NT, 36]), ALU.add)
            gl = logit[:, :, 0:4]
            iota4 = iota_f[:, 0:4].unsqueeze(1).broadcast_to([P, NT, 4])
            iota8 = iota_f[:, 0:8].unsqueeze(1).broadcast_to([P, NT, 8])

            def first_of_max(x, mx_, eq, idx, one, iota, n):
                after(nc.vector.tensor_reduce, mx_, x, AX.X, ALU.max)
                after(tt, eq, x, b3(mx_, n), ALU.is_equal)
                after(stt, eq, eq, -100.0, iota, ALU.mult, ALU.add)
                after(nc.vector.tensor_reduce, idx, eq, AX.X, ALU.min)
                after(ts, idx, idx, 100.0, None, ALU.add)
                after(tt, one, iota, b3(idx, n), ALU.is_equal)

            first_of_max(gl, r8["gm"], grp["eq"], r8["gi"], grp["sel"], iota4, 4)
            after(tt, grp["e"], gl, b3(r8["gm"], 4), ALU.subtract).then_inc(once("group_less_max"), 1)
            v.wait_ge(once("group_exp"), nth("group_exp", 1))
            after(nc.vector.tensor_reduce, r8["gv"], grp["e"], AX.X, ALU.add)
            after(nc.vector.reciprocal, r8["gv"], r8["gv"])
            sel4 = grp["sel"].unsqueeze(3).broadcast_to([P, NT, 4, 8])
            after(tt, big, logit[:, :, 4:36].rearrange("p t (g e) -> p t g e", e=8), sel4, ALU.mult)
            after(nc.vector.tensor_reduce, el["v"], big.rearrange("p t g e -> p t e g"), AX.X, ALU.add)
            first_of_max(el["v"], r8["m1"], el["eq"], r8["i1"], el["one"], iota8, 8)
            after(stt, el["v2"], el["one"], -1e38, el["v"], ALU.mult, ALU.add)
            first_of_max(el["v2"], r8["m2"], el["eq"], r8["i1"], el["two"], iota8, 8)
            after(tt, r8["e2"], r8["m2"], r8["m1"], ALU.subtract).then_inc(once("second_less_first"), 1)
            for n, one in enumerate((el["one"], el["two"])):
                tt(M[n].rearrange("p t (g e) -> p t g e", e=8), sel4,
                   one.unsqueeze(2).broadcast_to([P, NT, 4, 8]), ALU.mult)
            after(tt, Mb, M[0], M[1], ALU.add).then_inc(once("chosen"), 1)
            v.wait_ge(once("second_exp"), nth("second_exp", 1))
            after(ts, r8["w1"], r8["e2"], 1.0, None, ALU.add)
            after(nc.vector.reciprocal, r8["w1"], r8["w1"])
            after(tt, r8["t"], r8["w1"], r8["e2"], ALU.mult)
            after(tt, gate_w[:, :, 0], r8["w1"], r8["gv"], ALU.mult)
            tt(gate_w[:, :, 1], r8["t"], r8["gv"], ALU.mult)
            v.wait_ge(once("ranked"), nth("ranked", 1))
            after(nc.vector.tensor_copy, ce["n"], pair[1][:, HALF:HALF + EXPERTS])
            nc.vector.tensor_copy(rank.rearrange("p t e -> p (t e)"), pair[1][:, 0:NT * EXPERTS])
            after(ts, ce["ov"], ce["n"], float(P), None, ALU.is_gt)
            for n in range(2, SEQ // P):
                after(stt, ce["ov"], ce["n"], float(n * P), ce["ov"], ALU.is_gt, ALU.add)
            after(nc.vector.tensor_tensor_scan, ce["end"], ones[:, 0:EXPERTS], ce["ov"], 0.0, ALU.mult, ALU.add)
            after(tt, ce["off"], ce["end"], ce["ov"], ALU.subtract)
            after(ts, ce["off"], ce["off"], float(P), float(P * (EXPERTS - 1)), ALU.mult, ALU.add)
            after(stt, ce["off"], iota_f, -float(P), ce["off"], ALU.mult, ALU.add)
            after(ts, rt, rank, float(P), None, ALU.is_ge)
            after(tt, rt, rt, ce["off"].unsqueeze(1).broadcast_to([P, NT, EXPERTS]), ALU.mult)
            after(tt, rt, rt, rank, ALU.add)
            after(stt, ce["t"], iota_f, float(P), ones[:, 0:EXPERTS], ALU.mult, ALU.mult)
            after(tt, rt, rt, ce["t"].unsqueeze(1).broadcast_to([P, NT, EXPERTS]), ALU.add)
            for n in range(2):
                after(tt, M[n], M[n], rt, ALU.mult)
                after(nc.vector.tensor_reduce, r8["t"], M[n], AX.X, ALU.add)
                after(nc.vector.tensor_copy, dest_i[n], r8["t"])
            v.drain()
            v.sem_inc(once("dest_ready"), 1)
            tt(oj, ce["end"].unsqueeze(1).broadcast_to([P, OVER + 1, EXPERTS]),
               iota_f[:, 0:OVER + 1].unsqueeze(2).broadcast_to([P, OVER + 1, EXPERTS]), ALU.is_le)
            after(nc.vector.tensor_reduce, of[:, 0:16], oj, AX.X, ALU.add)
            nc.vector.tensor_copy(of[:, 16:17], ce["end"][:, EXPERTS - 1:EXPERTS])
            nc.vector.memset(of[:, 17:32], 0.0)
            after(ts, of[:, 0:16], of[:, 0:16], float(EXPERTS - 1), None, ALU.min)
            after(nc.vector.tensor_copy, over_i, of).then_inc(once("over_ready"), 1)

            gain = col("norm_ffn").unsqueeze(2).broadcast_to([P, KT, P])

            def take_rows(e, par):
                v.wait_ge(S("xg_turned"), e + 1)
                tt(xgT[par], pair[3].rearrange("p (k n) -> p k n", n=P), gain, ALU.mult).then_inc(S("xgt_ready"), 1)

            def make_product(e, par):
                v.drain()
                v.wait_ge(S("ga_ready"), e + 1)
                stt(ga, ga, 1.0, pair[par][:, 0:HALF], ALU.add, ALU.mult)
                v.drain()
                wait_unless_first(v, S("a_turned"), e)
                v.wait_ge(S("up_done"), e + 1)
                stt(aa, ga, 0.5, pair[par][:, HALF:], ALU.mult, ALU.mult).then_inc(S("a_made"), 1)

            def take_product(e):
                wait_unless_first(v, S("down_done"), e)
                v.wait_ge(S("a_turned"), e + 1)
                nc.vector.tensor_copy(aT.rearrange("p k n -> p (k n)"), pair[3][:, 0:HALF]).then_inc(S("at_ready"), 1)

            for par in range(2):
                v.wait_ge(S(f"h3_stored{par}"), 16 * NT // 2)
                v.wait_ge(S(f"rows_stored{par}"), 16 * NT // 2 + 16 * NT)
            take_rows(0, 0)
            take_rows(1, 1)
            make_product(0, 0)
            take_product(0)
            with v.Fori(0, EXPERTS // 2 - 1) as i:
                for m in range(2):
                    e, par = v.snap(i * 2 + (1 + m)), 1 - m
                    take_rows(e + 1, 1 - par)
                    make_product(e, par)
                    take_product(e)
            make_product(EXPERTS - 1, 1)
            take_product(EXPERTS - 1)
            n_over = v.value_load(over_i[0:1, 16:17], min_val=0, max_val=OVER)
            with v.Fori(0, OVER) as j:
                with v.If(j < n_over):
                    v.wait_ge(S("xg_turned"), j + 1 + EXPERTS)
                    tt(xgT[0], pair[3].rearrange("p (k n) -> p k n", n=P), gain, ALU.mult).then_inc(S("xgt_ready"), 1)
                    v.wait_ge(S("ga_ready"), j + 1 + EXPERTS)
                    stt(ga, ga, 1.0, pair[0][:, 0:HALF], ALU.add, ALU.mult)
                    after(stt, aa, ga, 0.5, pair[0][:, HALF:], ALU.mult, ALU.mult).then_inc(S("a_made"), 1)
                    v.wait_ge(S("a_turned"), j + 1 + EXPERTS)
                    nc.vector.tensor_copy(aT.rearrange("p k n -> p (k n)"), pair[3][:, 0:HALF]).then_inc(S("at_ready"), 1)
            for t in range(NT):
                v.wait_ge(S(f"rows_full{t % 2}"), 16 * (t // 2 + 1) + 24 * NT)
                v.wait_ge(S(f"yg_full{t % 2}"), 32 * (t // 2 + 1))
                after(stt, xf[t % 2], yg[0][t % 2], gate_w[:, t, 0:1], xf[t % 2], ALU.mult, ALU.add)
                after(stt, xf[t % 2], yg[1][t % 2], gate_w[:, t, 1:2], xf[t % 2], ALU.mult, ALU.add
                      ).then_inc(S("out_ready"), 1)


def kernel(**inputs):
    import concourse.bacc as bacc
    from concourse.bass_utils import run_bass_kernel_spmd

    nc = bacc.Bacc("TRN2", target_bir_lowering=False, num_devices=1)
    arrays, tensors = {}, {}
    for name, a in inputs.items():
        a = np.ascontiguousarray(a)
        arrays[f"in_{name}_dram"] = a
        tensors[name] = nc.dram_tensor(f"in_{name}_dram", a.shape, mybir.dt.from_np(a.dtype), kind="ExternalInput").ap()
    out = nc.dram_tensor("out_0_dram", [1, SEQ, D], F32, kind="ExternalOutput").ap()
    program(nc, tensors, out)
    result = run_bass_kernel_spmd(nc, [arrays], core_ids=[0])
    return result.results[0]["out_0_dram"]
```

```python
from contextlib import ExitStack

import numpy as np
import concourse.bass as bass
from concourse import mybir

F32 = mybir.dt.float32
I32 = mybir.dt.int32
ALU = mybir.AluOpType
ACT = mybir.ActivationFunctionType
AX = mybir.AxisListType

P = 128
SEQ = 1024
D = 1024
NT = SEQ // P
KT = D // P
HALF = 512
SLOT = KT * HALF
SLOTS = 4
LOADED = 48
LN_EPS = 1e-5
EPS = 1e-6
MEM = 256
GM = 512
GM_HEADS = 4
SSM = 256
ST = 8
XA = 256
XA_HEADS = 4
XA_DIM = 64
DN_ALPHA = 2.0 ** 0.25

ROW = {"norm_mix": 0, "conv_b": 8, "conv_w": 16, "lru_ba": 48, "lru_bx": 56, "lru_lambda": 64, "norm_cx": 72,
       "norm_mem": 80, "norm_ffn": 88, "positions": 96, "lam_re": 104, "lam_im": 112, "glu_b": 120, "ssm_d": 122,
       "cq_norm": 124, "ck_norm": 125, "subln": 126, "zero": 127}
MH = 4
EXPERTS = 32
GROUPS = 4
FF = 512
OVER = 2 * SEQ // P - 1
BLOCKS = EXPERTS + OVER
TWO_PI = 2.0 * np.pi
PI_A = 6.28125
PI_B = float(np.float32(np.round((TWO_PI - PI_A) * 2 ** 19) / 2 ** 19))
PI_C = float(TWO_PI - PI_A - PI_B)
LN2_A = 0.693359375
LN2_B = float(np.log(2.0) - 0.693359375)
INV_FREQ = [float(np.exp(np.float32(-np.log(500000.0)) * np.float32(n) / np.float32(8), dtype=np.float32)) for n in range(8)]
ROUND = 1.5 * 2 ** 23


def program(nc, I, out):
    ctx = ExitStack()
    base = 16512
    TOP = 229344
    RING = base
    A0 = RING + SLOTS * SLOT * 4
    B0 = A0 + KT * SEQ * 4
    C0 = B0 + KT * SEQ * 4
    K0 = C0 + KT * SEQ * 4
    top = {"K": K0}

    def at(name, shape, offset, dt=F32):
        size = int(np.prod(shape[1:])) * 4
        assert offset + size <= TOP, name
        return nc.alloc_sbuf_tensor_at(name, shape, dt, offset=offset)[:]

    def keep(name, shape, dt=F32):
        o = top["K"]
        top["K"] = o + (int(np.prod(shape[1:])) * 4 + 31) // 32 * 32
        return at(name, shape, o, dt)

    def sem(name):
        return ctx.enter_context(nc.semaphore(name))

    def area(start):
        pos = [start]

        def put(name, shape, dt=F32):
            o = pos[0]
            pos[0] = o + (int(np.prod(shape[1:])) * 4 + 31) // 32 * 32
            return at(name, shape, o, dt)
        put.pos = pos
        return put

    with ctx:
        ring = at("ring", [P, SLOTS, KT, HALF], RING)
        ring_flat = ring.rearrange("p s k n -> p (s k n)")
        regA = at("regA", [P, KT, SEQ], A0)
        regB = at("regB", [P, KT, SEQ], B0)
        regC = at("regC", [P, KT, SEQ], C0)
        ident = keep("ident", [P, P])
        ones = keep("ones", [P, P])
        cols = keep("cols", [P, P])
        psum = ctx.enter_context(nc.psum_tensor("psum", [P, 4, 2 * HALF], F32))[:]
        pair = [psum[:, n] for n in range(4)]

        def col(name, n=8):
            return cols[:, ROW[name]:ROW[name] + n]

        rope_c = keep("rope_c", [P, NT, 8])
        rope_s = keep("rope_s", [P, NT, 8])
        tiny = {n: keep("tiny_" + n, [P, NT * 8]) for n in ("a", "b", "c", "d", "e", "f", "g")}
        gm_st = keep("gm_st", [P, 32, 6])
        gm_mv = keep("gm_mv", [P, 32, 2])
        gm_r = keep("gm_r", [P, 32])
        sm = {n: keep("sm_" + n, [P, 8]) for n in ("mx", "sum", "rc", "mean", "r1", "r2", "ss", "v1")}
        xa_nm = [keep(f"xa_nm{n}", [P, 4]) for n in range(2)]
        xa_sum = [keep(f"xa_sum{n}", [P, 4]) for n in range(2)]
        tab8 = keep("tab8", [P, 8, KT])
        pcol = [keep(f"pcol{n}", [P, 8]) for n in range(2)]
        neg_lam = keep("neg_lam", [P, 1])
        subln = keep("subln", [P, 1])
        rs = (keep("rs_a", [P, 32]), keep("rs_b", [P, 32]), keep("rs_i", [P, 32], I32), keep("rs_h", [P, 32]))

        gate_w = keep("gate_w", [P, NT, 2])
        dest_i = [keep(f"dest_i{n}", [P, NT], I32) for n in range(2)]
        slot_tok = keep("slot_tok", [P, BLOCKS], I32)
        over_i = keep("over_i", [P, 32], I32)
        S0 = top["K"]
        x3_dram = nc.dram_tensor("x3_scratch", [SEQ, D], F32).ap()
        h3_dram = nc.dram_tensor("h3_scratch", [SEQ, D], F32).ap()
        tok_dram = nc.dram_tensor("tok_scratch", [BLOCKS * P, 1], I32).ap()
        y_dram = nc.dram_tensor("y_scratch", [BLOCKS * P, D], F32).ap()
        x1_dram = nc.dram_tensor("x1_scratch", [SEQ, D], F32).ap()
        x2_dram = nc.dram_tensor("x2_scratch", [SEQ, D], F32).ap()

        slot_full = [sem(f"slot_full{n}") for n in range(SLOTS)]
        slot_free = [sem(f"slot_free{n}") for n in range(SLOTS)]
        loads = [0] * SLOTS
        used = [0] * SLOTS

        def slot_wait(sp, s, more=0):
            n = loads[s] + more
            if not isinstance(n, int) or n > 0:
                sp.wait_ge(slot_free[s], n)

        def slot_load(sp, s, w_rows, c0, width=HALF):
            slot_wait(sp, s)
            k = w_rows.shape[0] // P
            dst = ring[:, s].rearrange("p k n -> p (k n)")[:, 0:k * width].rearrange("p (k n) -> p k n", n=width)
            sp.dma_start(dst, w_rows[:, c0:c0 + width].rearrange("(k p) n -> p k n", p=P)).then_inc(slot_full[s], LOADED)
            loads[s] += 1

        def slot_ready(pe, s):
            pe.wait_ge(slot_full[s], LOADED * (used[s] + 1))

        def slot_done(pe, s):
            used[s] += 1
            pe.drain()
            pe.sem_inc(slot_free[s], 1)

        def products(o, terms):
            last = None
            for n, (l, r) in enumerate(terms):
                last = nc.tensor.matmul(o, l, r, start=(n == 0), stop=(n == len(terms) - 1))
            return last


        sems = {}

        def S(name):
            if name not in sems:
                sems[name] = sem(name)
            return sems[name]

        def wait_unless_first(engine, semaphore, count):
            if not isinstance(count, int) or count > 0:
                engine.wait_ge(semaphore, count)

        ONCE = {
            "pe": ("cols_turned", "kv_ready", "wgm_turned", "ct_turned", "ct_turned", "bt_turned", "bt_turned",
                   "k2_turned", "router_done", "ranked"),
            "dve": ("rows_filled", "cols_ready", "bbar_placed", "half_glu_b", "xp_zeroed", "lam_sums", "heads_done",
                    "k2_normed", "group_less_max", "second_less_first", "chosen", "dest_ready", "over_ready"),
            "act": ("kv_taken", "wt_taken", "ct_ready", "ct_ready", "bt_ready", "bt_ready", "lam_exp", "mrow_squared",
                    "k2_squared", "k2_squared", "k2t_taken", "group_exp", "second_exp"),
            "pool": ("zeroed", "ident_ready", "wgm_masked", "route_consts"),
        }

        def once(name):
            return S([e + "_steps" for e in ONCE if name in ONCE[e]][0])

        def nth(name, n):
            steps = [names for names in ONCE.values() if name in names][0]
            return [i + 1 for i, s in enumerate(steps) if s == name][n - 1]

        p0 = area(S0)
        rows = p0("rows", [P, P])
        irows = p0("irows", [P, P], I32)
        wgm = p0("wgm", [P, GM_HEADS, P])
        lstep = p0("lstep", [P, ST])
        ssmp = {n: p0("ssmp_" + n, [P, ST]) for n in
                ("step", "ang", "k", "r", "c", "s", "h", "lr", "li", "br", "bi", "den", "t1", "t2", "t3", "t4")}
        phase = {n: (p0(f"phase_c{n}", [P, ST]), p0(f"phase_s{n}", [P, ST]))
                 for n in (1, 2, 4, 8, 16, 32, 64, 128, 256, 512)}
        b_raw = p0("b_raw", [P, 2, ST, 16])
        b_bar = p0("b_bar", [P, 2, ST, 16])
        b_tmp = p0("b_tmp", [P, ST, 16])
        wT = p0("wT", [P, GM_HEADS, P])
        gm_bs = p0("gm_bs", [P, GM_HEADS, P])
        glu_w = p0("glu_w", [P, 2, SSM])
        MT0 = p0.pos[0]
        memT = p0("memT", [P, KT, MEM])
        kF = p0("kF", [P, 2, MEM])
        vM = p0("vM", [P, 2, XA])
        W0 = p0.pos[0]
        xin = [at(f"xin{n}", [P, D], W0 + n * 4096) for n in range(4)]
        pc = area(C0)
        xb = pc("xb", [P, 2, SEQ])
        gb = pc("gb", [P, 2, SEQ])
        tabc = pc("tabc", [P, ST, P])
        tabs = pc("tabs", [P, ST, P])
        wcos = [pc("wcos0", [P, SEQ]), at("wcos1", [P, SEQ], B0)]
        wsin = [pc("wsin0", [P, SEQ]), at("wsin1", [P, SEQ], B0 + 4096)]
        pb = area(B0)
        blockB = pb("blockB", [P, ST, 2, P])
        blockC = pb("blockC", [P, ST, 2, P])
        CT = pb("CT", [P, ST, 3, P])
        pw = area(RING + 2 * SLOT * 4)
        rot = [pw(f"rot{n}", [P, SEQ]) for n in range(4)]
        gr = [pw("gr0", [P, SEQ]), at("gr1", [P, SEQ], B0 + 8192)]
        gi = [pw("gi0", [P, SEQ]), at("gi1", [P, SEQ], B0 + 12288)]
        BT = pw("BT", [P, ST, 2, P])
        yb = at("yb", [P, 2, SEQ], W0)
        hbuf = [at(f"hbuf{n}", [P, SEQ], RING + SLOT * 4 + n * 4096) for n in range(4)]
        vh = at("vh", [P, NT, GM], C0)
        vg = at("vg", [P, NT, GM], C0 + 16384)
        pg = area(W0)
        gu = [at(f"gu{n}", [P, SEQ], MT0 + 4096 * n) for n in range(2)]
        th = [pg(f"th{n}", [P, SEQ]) for n in range(2)]
        mb = pg("mb", [P, SEQ])
        gm_g, gm_b = pg("gm_g", [P, GM]), pg("gm_b", [P, GM])
        qF = at("qF", [P, 2, SEQ], C0)
        pT = at("pT", [P, 8, HALF], C0 + 8192)
        ex = [at(f"ex{n}", [P, SEQ], C0 + 24576 + 4096 * n) for n in range(2)]
        xr = [at(f"xr{n}", [P, D], C0 + 4096 * n) for n in range(2)]
        hx = [at(f"hx{n}", [P, D], C0 + 8192 + 4096 * n) for n in range(2)]
        ln_g = at("ln_g", [P, D], C0 + 16384)
        ln_b = at("ln_b", [P, D], C0 + 20480)
        sqj = at("sqj", [P, D], C0 + 24576)
        pl = area(C0)
        xp = [pl(f"xp{n}", [P, SEQ + 4]) for n in range(2)]
        xc = [pl(f"xc{n}", [P, SEQ]) for n in range(2)]
        gg = at("gg", [P, SEQ], pl.pos[0])
        pl = area(S0)
        thr, thi, av, tl, sq = (pl(n, [P, SEQ]) for n in ("thr", "thi", "av", "tl", "sq"))
        mth = [at(f"mth{n}", [P, SEQ], S0 + 4096 * n) for n in range(2)]
        mtmp = at("mtmp", [P, SEQ], S0 + 8192)
        ph = area(RING + 2 * SLOT * 4)
        e2 = ph("e2", [P, 2, SEQ])
        wmix = [ph(f"wmix{n}", [P, SEQ]) for n in range(2)]
        wmT = ph("wmT", [P, SEQ])
        obuf = ph("obuf", [P, NT, P])
        qT = [ph("qT0", [P, SEQ])]
        kT = [ph("kT0", [P, SEQ])]
        ph = area(S0)
        qkv = [ph(f"qkv{n}", [P, NT, 384]) for n in range(2)]
        qT.append(ph("qT1", [P, SEQ]))
        kT.append(ph("kT1", [P, SEQ]))
        vv = ph("vv", [P, NT, P])
        qk_gain = ph("qk_gain", [P, 4, 64])
        lam4 = ph("lam4", [P, 4, 64])
        junk = ph("junk", [P, P])
        hs = {n: ph("hs_" + n, [P, 32]) for n in ("ss", "r", "v1")}
        ho = {n: ph("ho_" + n, [P, 8]) for n in ("ss", "r", "v1", "mx", "nm", "sum", "rc", "rl")}
        sq8 = regB[:, 6:8].rearrange("p m n -> p (m n)").rearrange("p (t n) -> p t n", n=256)
        rope_t = [sq8[:, n].rearrange("p (t m d) -> p t m d", m=4, d=8) for n in range(4)]
        xr2 = [at(f"xr2{n}", [P, D], B0 + 4096 * n) for n in range(2)]
        hx2 = [at(f"hx2{n}", [P, D], B0 + 8192 + 4096 * n) for n in range(2)]
        sqj2 = at("sqj2", [P, D], B0 + 16384)
        GATE_L, GATE_A = 5 * D, 6 * D
        HEADS = 8
        px = area(S0)
        ex2 = [px(f"ex2{n}", [P, SEQ]) for n in range(2)]
        px("merge_tmp", [P, SEQ])
        mrow = [px(f"mrow{n}", [P, D]) for n in range(2)]
        mT2 = at("mT2", [P, KT, MEM], S0)
        kvM = [px(f"kvM{n}", [P, D]) for n in range(2)]
        kF2 = px("kF2", [P, MH, MEM])
        jk = px("jk", [P, P])
        cs = {n: px("cs_" + n, [P, 32]) for n in ("ss", "v1", "r")}
        zeros = at("zeros", [P, 256], TOP - 1024)
        assert px.pos[0] <= TOP - 1024
        qM = at("qM", [P, NT, HALF], B0)
        oF2 = at("oF2", [P, MH, SEQ], B0 + 16384)
        qF2 = at("qF2", [P, MH, SEQ], C0)
        pT2 = at("pT2", [P, 8, HALF], C0 + 16384)
        xr3 = [at(f"xr3{n}", [P, D], C0 + 4096 * n) for n in range(2)]
        hx3 = [at(f"hx3{n}", [P, D], C0 + 8192 + 4096 * n) for n in range(2)]
        sqj3 = at("sqj3", [P, D], C0 + 16384)
        pr = area(C0 + 20480)
        w_r = pr("w_r", [P, KT, 36])
        b_r = pr("b_r", [P, 36])
        logit = pr("logit", [P, NT, 36])
        iota_i = pr("iota_i", [P, EXPERTS], I32)
        iota_f = pr("iota_f", [P, EXPERTS])
        tok_i = pr("tok_i", [P, NT], I32)
        tri = pr("tri", [P, P])
        zero_i = pr("zero_i", [P, BLOCKS], I32)
        pr = area(S0)
        grp = {n: pr("grp_" + n, [P, NT, 4]) for n in ("eq", "sel", "e")}
        el = {n: pr("el_" + n, [P, NT, 8]) for n in ("v", "v2", "eq", "one", "two")}
        r8 = {n: pr("r8_" + n, [P, NT]) for n in ("gm", "gi", "gv", "m1", "m2", "i1", "e2", "w1", "t")}
        big = pr("big", [P, NT, GROUPS, 8])
        M = [pr(f"M{n}", [P, NT, EXPERTS]) for n in range(2)]
        Mb = pr("Mb", [P, NT, EXPERTS])
        before = pr("before", [P, NT + 1, EXPERTS])
        rank = pr("rank", [P, NT, EXPERTS])
        rt = pr("rt", [P, NT, EXPERTS])
        ce = {n: pr("ce_" + n, [P, EXPERTS]) for n in ("n", "ov", "end", "off", "t")}
        oj = pr("oj", [P, OVER + 1, EXPERTS])
        of = pr("of", [P, 32])
        assert pr.pos[0] <= TOP - 1024
        slots6 = at("slots6", [P, 2, 3, SLOT], RING)
        pe_ = area(C0)
        xg = [pe_(f"xg{n}", [P, D]) for n in range(2)]
        xgT = [pe_(f"xgT{n}", [P, KT, P]) for n in range(2)]
        ga = pe_("ga", [P, FF])
        aa = pe_("aa", [P, FF])
        aT = pe_("aT", [P, 4, P])
        pe_ = area(B0)
        ys = [pe_(f"ys{n}", [P, D]) for n in range(2)]
        gidx = [pe_(f"gidx{n}", [P, 8], I32) for n in range(2)]
        xf = [at(f"xf{n}", [P, D], S0 + 4096 * n) for n in range(NT)]
        yg = [[at(f"yg{m}{n}", [P, D], RING + 4096 * (4 * m + n)) for n in range(4)] for m in range(2)]

        PARAMS = 16 * 17

        def flat(a):
            return a.rearrange("(r c) -> r c", c=P)

        block = ctx.enter_context(nc.Block())

        @block.sync
        def _(sp):
            for t in range(NT + 2):
                if t >= 4:
                    sp.wait_ge(S("xin_turned"), t - 3)
                src = I["x"][0, t * P:(t + 1) * P, :] if t < NT else I["mem"][0, (t - NT) * P:(t - NT + 1) * P, :]
                sp.dma_start(xin[t % 4], src).then_inc(S(f"xin_full{t % 4}"), 16)
                if t == 3:
                    slot_load(sp, 0, I["w_in"][0], 3 * GM)
            slot_wait(sp, 1)
            for m, key in enumerate(("xa_w_k", "xa_w_v")):
                sp.dma_start(ring[:, 1, :, XA * m:XA * (m + 1)], I[key][0].rearrange("(k p) n -> p k n", p=P)
                             ).then_inc(slot_full[1], 16 + 16 * m)
            loads[1] += 1
            slot_load(sp, 0, I["w_in"][0], GM)
            sp.wait_ge(S("branch_b"), 2)
            slot_load(sp, 1, I["w_in"][0], 0)
            slot_load(sp, 2, I["w_in"][0], 2 * GM)
            slot_load(sp, 3, I["w_in"][0], 3 * GM + 2 * SSM)
            for m, key in enumerate(("gm_ln_g", "gm_ln_b")):
                sp.dma_start((gm_g, gm_b)[m], I[key][0].rearrange("h d -> (h d)").partition_broadcast(P)
                             ).then_inc(S("vectors_in"), 16)
            slot_load(sp, 0, I["w_out"][0], 0)
            slot_load(sp, 1, I["w_out"][0], HALF)
            sp.wait_ge(S("yx_ready"), 4)
            for m, key in enumerate(("ln_g", "ln_b")):
                sp.dma_start((ln_g, ln_b)[m], I[key][0].partition_broadcast(P)).then_inc(S("vectors_in"), 16)
            for t in range(NT + 1):
                if t < NT:
                    if t >= 2:
                        sp.wait_ge(S(f"rows_stored{t % 2}"), 16 * (t // 2))
                        sp.wait_ge(S("rows_normed"), t - 1)
                    sp.dma_start(xr[t % 2], I["x"][0, t * P:(t + 1) * P, :]).then_inc(S(f"rows_full{t % 2}"), 16)
                if t >= 1:
                    sp.wait_ge(S("rows_ready"), t)
                    sp.dma_start(x1_dram[(t - 1) * P:t * P, :], xr[(t - 1) % 2]).then_inc(S(f"rows_stored{(t - 1) % 2}"), 16)
            w2 = I["w_in_2"][0]
            with sp.Fori(0, KT // 2) as i:
                for par in range(2):
                    c0 = sp.snap((i * 2 + par) * P)
                    c1 = sp.snap(c0 + D)
                    uses = sp.snap(i + loads[2 + par])
                    sp.wait_ge(slot_free[2 + par], uses)
                    flat_slot = ring[:, 2 + par].rearrange("p k n -> p (k n)")
                    for m in range(2):
                        sp.dma_start(flat_slot[:, m * 1024:(m + 1) * 1024].rearrange("p (k n) -> p k n", n=P),
                                     w2[:, bass.ds((c0, c1)[m], P)].rearrange("(k p) n -> p k n", p=P)
                                     ).then_inc(slot_full[2 + par], 16 + 16 * m)
                    for m, key in enumerate(("lru_wa_2", "lru_wx_2")):
                        sp.dma_start(flat_slot[:, 2048 + m * P:2048 + (m + 1) * P],
                                     I[key][0].rearrange("b i o -> (b i) o")[bass.ds(c0, P), :]
                                     ).then_inc(S("lru_w_full%d" % par), 16)
            for par in range(2):
                loads[2 + par] += KT // 2
            for c in range(2):
                slot_load(sp, 2 * c, I["w_lru_o_2"][0], c * HALF)
                slot_load(sp, 2 * c + 1, w2, GATE_L + c * HALF)
            def head_load(cols0, at0):
                dst = ring_flat[:, bass.ds(at0, KT * 384)].rearrange("p (k n) -> p k n", n=384)
                for m in range(3):
                    sp.dma_start(dst[:, :, m * P:(m + 1) * P],
                                 w2[:, bass.ds(cols0[m], P)].rearrange("(k p) n -> p k n", p=P)
                                 ).then_inc(S("head_full"), 16)

            slot_wait(sp, 0)
            slot_wait(sp, 1)
            head_load([2 * D, 3 * D, 4 * D], 0)
            sp.wait_ge(S("merged"), KT)
            for n, key in enumerate(("q_norm_2", "q_norm_2", "k_norm_2", "k_norm_2")):
                sp.dma_start(qk_gain[:, n], I[key][0].partition_broadcast(P)).then_inc(S("vectors_in"), 16)
            for n, key in enumerate(("lambda_q1_2", "lambda_k1_2", "lambda_q2_2", "lambda_k2_2")):
                sp.dma_start(lam4[:, n], I[key][0].partition_broadcast(P)).then_inc(S("vectors_in"), 16)

            sp.sem_inc(S("head_free"), 48)
            with sp.Fori(1, HEADS) as h:
                cols0, at0 = [sp.snap(h * P + (2 + m) * D) for m in range(3)], sp.snap((h % 2) * SLOT)
                before = sp.snap(h * 48)
                sp.wait_ge(S("head_free"), before)
                sp.wait_ge(S("head_full"), before)
                head_load(cols0, at0)
            sp.wait_ge(S("head_free"), 48 * HEADS + 48)
            slot_load(sp, 0, I["w_attn_o_2"][0], 0)
            slot_load(sp, 1, w2, GATE_A)
            sp.wait_ge(once("heads_done"), nth("heads_done", 1))
            slot_load(sp, 2, I["w_attn_o_2"][0], HALF)
            slot_load(sp, 3, w2, GATE_A + HALF)
            for t in range(2):
                sp.dma_start(mrow[t], I["mem_2"][0, t * P:(t + 1) * P, :]).then_inc(S("vectors_in"), 16)
            slot_load(sp, 0, I["w_out_2"][0], 0)
            slot_load(sp, 1, I["w_out_2"][0], HALF)
            slot_load(sp, 2, I["w_ckv_2"][0], 0)
            slot_load(sp, 3, I["w_ckv_2"][0], HALF)
            sp.wait_ge(S("merged"), 2 * KT)
            for t in range(NT + 1):
                if t < NT:
                    if t >= 2:
                        sp.wait_ge(S(f"rows_stored{t % 2}"), 16 * (t // 2) + 8 * NT)
                        sp.wait_ge(S("rows_normed"), t - 1 + NT)
                    else:
                        for par in range(2):
                            sp.wait_ge(S(f"rows_stored{par}"), 16 * NT // 2)
                    sp.dma_start(xr2[t % 2], x1_dram[t * P:(t + 1) * P, :]).then_inc(S(f"rows_full{t % 2}"), 16)
                if t >= 1:
                    sp.wait_ge(S("rows_ready"), NT + t)
                    sp.dma_start(x2_dram[(t - 1) * P:t * P, :], xr2[(t - 1) % 2]
                                 ).then_inc(S(f"rows_stored{(t - 1) % 2}"), 16)
            slot_load(sp, 0, I["w_cq_2"][0], 0)
            slot_wait(sp, 3)
            sp.dma_start(ring[:, 3].rearrange("p k n -> p (k n)").rearrange("p (k n) -> p k n", n=D),
                         I["w_co_2"][0].rearrange("(k p) n -> p k n", p=P)).then_inc(slot_full[3], LOADED)
            loads[3] += 1
            sp.wait_ge(S("co_taken"), 8)
            sp.dma_start(w_r[:, :, 0:4], I["w_group_2"][0].rearrange("(k p) n -> p k n", p=P)).then_inc(S("vectors_in"), 16)
            sp.dma_start(w_r[:, :, 4:36], I["w_router_2"][0].rearrange("(k p) n -> p k n", p=P)).then_inc(S("vectors_in"), 16)
            sp.dma_start(b_r[:, 0:4], I["b_group_2"][0].partition_broadcast(P)).then_inc(S("vectors_in"), 16)
            sp.dma_start(b_r[:, 4:36], I["b_router_2"][0].partition_broadcast(P)).then_inc(S("vectors_in"), 16)
            for t in range(NT + 1):
                if t < NT:
                    if t >= 2:
                        sp.wait_ge(S(f"rows_stored{t % 2}"), 16 * (t // 2) + 16 * NT)
                        sp.wait_ge(S("rows_normed"), t - 1 + 2 * NT)
                    else:
                        for par in range(2):
                            sp.wait_ge(S(f"rows_stored{par}"), 16 * NT // 2 + 8 * NT)
                    sp.dma_start(xr3[t % 2], x2_dram[t * P:(t + 1) * P, :]).then_inc(S(f"rows_full{t % 2}"), 16)
                if t >= 1:
                    sp.wait_ge(S("rows_ready"), t + 2 * NT)
                    sp.dma_start(x3_dram[(t - 1) * P:t * P, :], xr3[(t - 1) % 2]
                                 ).then_inc(S(f"rows_stored{(t - 1) % 2}"), 16)
                    sp.wait_ge(S("rows_normed"), t + 2 * NT)
                    sp.dma_start(h3_dram[(t - 1) * P:t * P, :], hx3[(t - 1) % 2]
                                 ).then_inc(S(f"h3_stored{(t - 1) % 2}"), 16)
            def expert_load(e, par, waits):
                gu_, dn = I["w_gate_up_2"][0], I["w_down_2"][0]
                rows_gu = gu_.rearrange("e k n -> (e k) n")
                rows_dn = dn.rearrange("e k n -> (e k) n")
                r_gu, r_dn = (e * D, e * FF) if isinstance(e, int) else (sp.snap(e * D), sp.snap(e * FF))
                freed = sp.snap(e - 1) if waits else None
                for c in range(2):
                    if waits:
                        sp.wait_ge(S(("gate_done", "up_done")[c]), freed)
                    sp.dma_start(slots6[:, par, c].rearrange("p (k n) -> p k n", n=HALF),
                                 rows_gu[bass.ds(r_gu, D), c * FF:(c + 1) * FF].rearrange("(k p) n -> p k n", p=P)
                                 ).then_inc(S(f"w_full{par}{c}"), 16)
                if waits:
                    sp.wait_ge(S("down_done"), freed)
                sp.dma_start(slots6[:, par, 2].rearrange("p (k n) -> p k n", n=D),
                             rows_dn[bass.ds(r_dn, FF), :].rearrange("(k p) n -> p k n", p=P)
                             ).then_inc(S(f"w_full{par}2"), 16)

            slot_wait(sp, 0)
            slot_wait(sp, 1)
            slot_wait(sp, 2)
            expert_load(0, 0, False)
            slot_wait(sp, 3)
            sp.wait_ge(once("router_done"), nth("router_done", 1))
            expert_load(1, 1, False)
            with sp.Fori(1, EXPERTS // 2) as i:
                for par in range(2):
                    expert_load(sp.snap(i * 2 + par), par, True)
            sp.wait_ge(once("over_ready"), nth("over_ready", 1))
            for t in range(NT):
                sp.dma_start(xf[t], x3_dram[t * P:(t + 1) * P, :]).then_inc(S(f"rows_full{t % 2}"), 16)
            sp.wait_ge(once("over_ready"), nth("over_ready", 1))
            n_over = sp.value_load(over_i[0:1, 16:17], min_val=0, max_val=OVER)
            with sp.Fori(0, OVER) as j:
                with sp.If(j < n_over):
                    e = sp.value_load(over_i[0:1, bass.ds(j, 1)], min_val=0, max_val=EXPERTS - 1)
                    r_gu, r_dn, row0 = sp.snap(e * D), sp.snap(e * FF), sp.snap(j * P + EXPERTS * P)
                    before, made = sp.snap(j + EXPERTS), sp.snap(j + 1 + EXPERTS)
                    sp.wait_ge(S("down_done"), before)
                    for c in range(2):
                        sp.dma_start(slots6[:, 0, c].rearrange("p (k n) -> p k n", n=HALF),
                                     I["w_gate_up_2"][0].rearrange("e k n -> (e k) n")[bass.ds(r_gu, D), c * FF:(c + 1) * FF]
                                     .rearrange("(k p) n -> p k n", p=P)).then_inc(S("o_w_full"), 16)
                    sp.dma_start(slots6[:, 0, 2].rearrange("p (k n) -> p k n", n=D),
                                 I["w_down_2"][0].rearrange("e k n -> (e k) n")[bass.ds(r_dn, FF), :]
                                 .rearrange("(k p) n -> p k n", p=P)).then_inc(S("o_w_full"), 16)
                    sp.wait_ge(S("y_taken"), made + 1)
                    sp.dma_start(y_dram[bass.ds(row0, P), :], ys[0]).then_inc(S("y_stored0"), 16)
            sp.wait_ge(S("y_stored0"), n_over * 16 + 8 * EXPERTS)
            sp.sem_inc(S("over_stored"), 1)
            for t in range(NT):
                sp.wait_ge(S("out_ready"), t + 1)
                sp.dma_start(out[0, t * P:(t + 1) * P, :], xf[t]).then_inc(S(f"rows_stored{t % 2}"), 16)
            for par in range(2):
                sp.wait_ge(S(f"rows_stored{par}"), 16 * NT // 2 + 24 * NT)
                sp.wait_ge(S(f"rows_stored{par}"), 16 * NT // 2 + 8 * NT)
                sp.wait_ge(S(f"rows_stored{par}"), 16 * NT // 2 + 16 * NT)
                sp.wait_ge(S(f"h3_stored{par}"), 16 * NT // 2)

        @block.gpsimd
        def _(pool):
            nc.gpsimd.memset(ident, 0.0)
            nc.gpsimd.memset(ones, 1.0)
            nc.gpsimd.memset(rows, 0.0)
            nc.gpsimd.memset(irows, 0)
            nc.gpsimd.memset(blockB.rearrange("p a b c -> p (a b c)"), 0.0)
            nc.gpsimd.memset(blockC.rearrange("p a b c -> p (a b c)"), 0.0).then_inc(once("zeroed"), 1)
            pool.wait_ge(once("zeroed"), nth("zeroed", 1))
            nc.gpsimd.affine_select(out=ident, in_=ident, compare_op=ALU.not_equal, fill=1.0, base=0,
                                    pattern=[[-1, P]], channel_multiplier=1).then_inc(once("ident_ready"), 1)
            for name, key in (("norm_mix", "norm_mix_2"), ("conv_b", "conv_b_2"), ("lru_ba", "lru_ba_2"),
                              ("lru_bx", "lru_bx_2"), ("lru_lambda", "lru_lambda_2"), ("norm_cx", "norm_cx_2"),
                              ("norm_mem", "norm_mem_2"), ("norm_ffn", "norm_ffn_2"), ("glu_b", "glu_b"),
                              ("ssm_d", "ssm_d"), ("cq_norm", "cq_norm_2"), ("ck_norm", "ck_norm_2"),
                              ("subln", "subln_2")):
                src = flat(I[key][0])
                pool.dma_start(rows[ROW[name]:ROW[name] + src.shape[0], :], src).then_inc(S("params_in"), 16)
            for name, key in (("lam_re", "ssm_lam_re"), ("lam_im", "ssm_lam_im")):
                pool.dma_start(rows[ROW[name]:ROW[name] + 8, :], I[key][0].rearrange("(s a) q -> s (a q)", a=2)
                               ).then_inc(S("params_in"), 16)
            pool.dma_start(rows[16:48, :], I["conv_w_2"][0].rearrange("j (r c) -> (j r) c", c=P)
                           ).then_inc(S("params_in"), 16)
            pool.dma_start(irows[96:104, :], flat(I["positions_2"][0])).then_inc(S("params_in"), 16)
            ls = I["ssm_log_step"][0].rearrange("(s a) -> a s", a=2)
            for a in range(2):
                pool.dma_start(lstep[64 * a:64 * a + 64, :], ls[a].partition_broadcast(64),
                               allow_slow_non_contiguous=True).then_inc(S("ssm_in"), 16)
            for m, key in enumerate(("ssm_b_re", "ssm_b_im")):
                pool.dma_start(b_raw[:, m], I[key][0].rearrange("(s a) q c -> (a q) s c", a=2)).then_inc(S("ssm_in"), 16)
            for m, key in enumerate(("ssm_c_re", "ssm_c_im")):
                src = I[key][0].rearrange("(f j a) c q -> j a c f q", j=4, a=2)
                for j in range(4):
                    for a in range(2):
                        pool.dma_start(blockC[32 * j + 16 * a:32 * j + 16 * a + 16, j:ST:4, m, 64 * a:64 * a + 64],
                                       src[j, a]).then_inc(S("ssm_c_in"), 16)
            pool.dma_start(wgm, I["gm_w_s"][0].rearrange("h t s -> t h s")).then_inc(S("wgm_in"), 16)
            pool.dma_start(gm_bs.rearrange("p h t -> p (h t)"), I["gm_b_s"][0].rearrange("h t -> (h t)").partition_broadcast(P)
                           ).then_inc(S("gm_in"), 16)
            pool.dma_start(glu_w, I["glu_w"][0].rearrange("(k p) n -> p k n", p=P)).then_inc(S("gm_in"), 16)
            pool.wait_ge(S("wgm_in"), 16)
            nc.gpsimd.affine_select(out=wgm, in_=wgm, compare_op=ALU.is_ge, fill=0.0, base=0,
                                    pattern=[[0, GM_HEADS], [-1, P]], channel_multiplier=1).then_inc(once("wgm_masked"), 1)
            pool.wait_ge(once("kv_ready"), nth("kv_ready", 1))
            for s in range(ST):
                pool.wait_ge(S("scanned"), s + 1)
                c, sn, re, im = wcos[s % 2], wsin[s % 2], gr[s % 2], gi[s % 2]
                for n, (tab, g) in enumerate(((c, re), (sn, im), (sn, re), (c, im))):
                    if s:
                        pool.wait_ge(S("h_used"), 4 * (s - 1) + n + 1)
                    nc.gpsimd.tensor_tensor(hbuf[n], tab, g, ALU.mult).then_inc(S("h_ready"), 1)

            pool.wait_ge(S("vectors_in"), 32 + 32)
            for t in range(NT):
                pool.wait_ge(S("xr_normed"), t + 1)
                nc.gpsimd.tensor_tensor(xr[t % 2], xr[t % 2], ln_g, ALU.mult)
                pool.drain()
                nc.gpsimd.tensor_tensor(xr[t % 2], xr[t % 2], ln_b, ALU.add).then_inc(S("rows_ready"), 1)

            pool.wait_ge(once("heads_done"), nth("heads_done", 1))
            nc.gpsimd.memset(zeros, 0.0)
            pool.drain()
            pool.dma_start(y_dram[EXPERTS * P:].rearrange("(p b) (q n) -> p (b q) n", p=P, n=256),
                           zeros.unsqueeze(1).broadcast_to([P, OVER * D // 256, 256])).then_inc(S("tok_moved"), 16)
            pool.wait_ge(S("co_taken"), 8)
            nc.gpsimd.iota(iota_i, pattern=[[1, EXPERTS]], base=0, channel_multiplier=0)
            nc.gpsimd.iota(tok_i, pattern=[[P, NT]], base=0, channel_multiplier=1)
            nc.gpsimd.memset(zero_i, 0)
            pool.drain()
            nc.gpsimd.tensor_copy(iota_f, iota_i)
            nc.gpsimd.affine_select(out=tri, in_=ones, compare_op=ALU.is_gt, fill=0.0, base=0,
                                    pattern=[[1, P]], channel_multiplier=-1).then_inc(once("route_consts"), 1)
            pool.wait_ge(once("route_consts"), nth("route_consts", 1))
            pool.dma_start(tok_dram.rearrange("(p b) o -> p (b o)", b=BLOCKS), zero_i).then_inc(S("tok_moved"), 16)
            pool.wait_ge(S("tok_moved"), 32)
            pool.wait_ge(once("dest_ready"), nth("dest_ready", 1))
            for t in range(NT):
                for n in range(2):
                    nc.gpsimd.indirect_dma_start(
                        out=tok_dram, out_offset=bass.IndirectOffsetOnAxis(ap=dest_i[n][:, t:t + 1], axis=0),
                        in_=tok_i[:, t:t + 1], in_offset=None).then_inc(S("tok_moved"), 16)
            pool.wait_ge(S("tok_moved"), 32 + 32 * NT)
            pool.dma_start(slot_tok, tok_dram.rearrange("(b p) o -> p (b o)", p=P), allow_slow_non_contiguous=True
                           ).then_inc(S("tok_moved"), 16)
            pool.wait_ge(S("tok_moved"), 48 + 32 * NT)
            for par in range(2):
                pool.wait_ge(S(f"h3_stored{par}"), 16 * NT // 2)
                pool.wait_ge(S(f"rows_stored{par}"), 16 * NT // 2 + 16 * NT)

            def gather_rows(e, par, waits):
                if waits:
                    pool.wait_ge(S("xg_turned"), e - 1)
                nc.gpsimd.tensor_copy(gidx[par][:, 0:1], slot_tok[:, bass.ds(e, 1)])
                pool.drain()
                nc.gpsimd.indirect_dma_start(
                    out=xg[par], out_offset=None, in_=h3_dram,
                    in_offset=bass.IndirectOffsetOnAxis(ap=gidx[par][:, 0:1], axis=0)).then_inc(S(f"xg_full{par}"), 16)

            gather_rows(0, 0, False)
            gather_rows(1, 1, False)
            with pool.Fori(1, EXPERTS // 2) as i:
                for par in range(2):
                    gather_rows(pool.snap(i * 2 + par), par, True)
            pool.wait_ge(S("xg_turned"), EXPERTS)
            pool.wait_ge(once("over_ready"), nth("over_ready", 1))
            n_over = pool.value_load(over_i[0:1, 16:17], min_val=0, max_val=OVER)
            with pool.Fori(0, OVER) as j:
                with pool.If(j < n_over):
                    pool.wait_ge(S("xg_turned"), j + EXPERTS)
                    nc.gpsimd.tensor_copy(gidx[0][:, 0:1], slot_tok[:, bass.ds(j + EXPERTS, 1)])
                    pool.drain()
                    nc.gpsimd.indirect_dma_start(
                        out=xg[0], out_offset=None, in_=h3_dram,
                        in_offset=bass.IndirectOffsetOnAxis(ap=gidx[0][:, 0:1], axis=0)).then_inc(S("xg_full0"), 16)
            pool.wait_ge(S("over_stored"), 1)
            for par in range(2):
                pool.wait_ge(S(f"y_stored{par}"), 16 * EXPERTS // 2)
            for t in range(NT):
                if t >= 4:
                    pool.wait_ge(S("out_ready"), t - 3)
                for n in range(2):
                    nc.gpsimd.indirect_dma_start(
                        out=yg[n][t % 4], out_offset=None, in_=y_dram,
                        in_offset=bass.IndirectOffsetOnAxis(ap=dest_i[n][:, t:t + 1], axis=0)
                    ).then_inc(S(f"yg_full{t % 4}"), 16)

        @block.tensor
        def _(pe):
            for name in ("o_ready", "ot_turned"):
                pe.sem_inc(S(name), 1)
            pe.wait_ge(once("ident_ready"), nth("ident_ready", 1))
            for t in range(NT + 2):
                pe.wait_ge(S(f"xin_full{t % 4}"), 16 * (t // 4 + 1))
                if t >= 2:
                    pe.wait_ge(S("xt_copied_v"), t - 1)
                    pe.wait_ge(S("xt_copied_a"), t - 1)
                for k in range(KT):
                    last = nc.tensor.transpose(pair[t % 2][:, k * P:(k + 1) * P], xin[t % 4][:, k * P:(k + 1) * P], ident)
                last.then_inc(S("xin_turned"), 1)
            pe.wait_ge(once("rows_filled"), nth("rows_filled", 1))
            nc.tensor.transpose(pair[3][:, 0:P], rows, ident).then_inc(once("cols_turned"), 1)
            slot_ready(pe, 0)
            pe.wait_ge(S("xt_copied_v"), NT + 2)
            pe.wait_ge(S("xt_copied_a"), NT + 2)
            for f in range(4):
                if f == 3:
                    pe.wait_ge(once("cols_ready"), nth("cols_ready", 1))
                for c in range(2):
                    last = products(pair[f][:, c * HALF:(c + 1) * HALF],
                                    [(ring[:, 0, k, f * P:(f + 1) * P], regA[:, k, c * HALF:(c + 1) * HALF])
                                     for k in range(KT)])
                last.then_inc(S("xs_ready"), 1)
            slot_done(pe, 0)
            slot_ready(pe, 1)
            pe.wait_ge(S("xs_taken"), 1)
            for f in range(2):
                last = products(pair[0][:, f * MEM:(f + 1) * MEM],
                                [(ring[:, 1, k, f * P:(f + 1) * P], memT[:, k]) for k in range(KT)])
            for f in range(2):
                last = products(pair[0][:, HALF + f * XA:HALF + (f + 1) * XA],
                                [(memT[:, k, f * P:(f + 1) * P], ring[:, 1, k, XA:2 * XA]) for k in range(KT)])
            last.then_inc(once("kv_ready"), 1)
            slot_done(pe, 1)
            pe.wait_ge(once("wgm_masked"), nth("wgm_masked", 1))
            pe.wait_ge(S("xs_taken"), 2)
            for h in range(GM_HEADS):
                last = nc.tensor.transpose(pair[1][:, h * P:(h + 1) * P], wgm[:, h], ident)
            last.then_inc(once("wgm_turned"), 1)
            pe.wait_ge(S("ssm_c_in"), 16 * 16)
            for m in range(2):
                pe.wait_ge(S("xs_taken"), 3 + m)
                for s in range(ST):
                    last = nc.tensor.transpose(pair[2 + m][:, s * P:(s + 1) * P], blockC[:, s, m], ident)
                last.then_inc(once("ct_turned"), 1)
            pe.wait_ge(once("bbar_placed"), nth("bbar_placed", 1))
            for m in range(2):
                pe.wait_ge(once("wt_taken"), nth("wt_taken", 1))
                for s in range(ST):
                    last = nc.tensor.transpose(pair[m][:, s * P:(s + 1) * P], blockB[:, s, m], ident)
                last.then_inc(once("bt_turned"), 1)
            def state_input(s):
                if s == 0:
                    pe.wait_ge(once("bt_ready"), nth("bt_ready", 2))
                    pe.wait_ge(once("ct_ready"), nth("ct_ready", 2))
                else:
                    pe.wait_ge(S("bx_taken"), s)
                for m in range(2):
                    for c in range(2):
                        last = nc.tensor.matmul(pair[m][:, c * HALF:(c + 1) * HALF], BT[:, s, m],
                                                xb[:, s // 4, c * HALF:(c + 1) * HALF], start=True, stop=True)
                last.then_inc(S("bx_ready"), 1)

            state_input(0)
            for s in range(ST):
                f = s // 4
                if s + 1 < ST:
                    state_input(s + 1)
                for n, w in enumerate((0, 1, 2, 2)):
                    pe.wait_ge(S("h_ready"), 4 * s + n + 1)
                    for c in range(2):
                        last = nc.tensor.matmul(pair[2 + f][:, c * HALF:(c + 1) * HALF], CT[:, s, w],
                                                hbuf[n][:, c * HALF:(c + 1) * HALF],
                                                start=(s % 4 == 0 and n == 0), stop=(s % 4 == 3 and n == 3))
                    last.then_inc(S("h_used"), 1)
            pe.wait_ge(S("yb_ready"), 2)
            pe.wait_ge(S("gm_in"), 32)
            for f in range(2):
                for c in range(2):
                    last = products(pair[f][:, c * HALF:(c + 1) * HALF],
                                    [(glu_w[:, k, f * P:(f + 1) * P], yb[:, k, c * HALF:(c + 1) * HALF]) for k in range(2)])
                last.then_inc(S("glu_ready"), 1)

            slot_ready(pe, 0)
            for t in range(NT):
                if t >= 2:
                    pe.wait_ge(S("vg_ready"), t - 1)
                else:
                    pe.wait_ge(S("glu_tanh"), t + 1)
                products(pair[t % 2][:, 0:HALF], [(regA[:, k, t * P:(t + 1) * P], ring[:, 0, k]) for k in range(KT)]
                         ).then_inc(S("v_ready"), 1)
            slot_done(pe, 0)
            slot_ready(pe, 1)
            slot_ready(pe, 2)
            for h in range(GM_HEADS):
                for j in range(3):
                    n = 3 * h + j
                    if n >= 4:
                        pe.wait_ge(S(("u_taken", "g_taken", "mix_taken")[(n - 4) % 3]), (n - 4) // 3 + 1)
                    elif n < 2:
                        pe.wait_ge(S("vg_ready"), NT)
                    elif n == 2:
                        pe.wait_ge(S("yd_ready"), 2)
                    o = pair[n % 4]
                    if j < 2:
                        for c in range(2):
                            last = products(o[:, c * HALF:(c + 1) * HALF],
                                            [(ring[:, 1 + j, k, h * P:(h + 1) * P], regA[:, k, c * HALF:(c + 1) * HALF])
                                             for k in range(KT)])
                    else:
                        pe.wait_ge(S("vh_ready"), NT)
                        for c in range(NT):
                            last = nc.tensor.matmul(o[:, c * P:(c + 1) * P], vh[:, c, h * P:(h + 1) * P], wT[:, h],
                                                    start=True, stop=True)
                    last.then_inc(S(("u_ready", "g_ready", "mix_ready")[j]), 1)
            slot_done(pe, 1)
            slot_done(pe, 2)
            slot_ready(pe, 3)
            pe.wait_ge(S("mix_taken"), GM_HEADS)
            for f in range(4):
                for c in range(2):
                    last = products(pair[f][:, c * HALF:(c + 1) * HALF],
                                    [(ring[:, 3, k, f * P:(f + 1) * P], regA[:, k, c * HALF:(c + 1) * HALF])
                                     for k in range(KT)])
                last.then_inc(S("qx_ready"), 1)
            slot_done(pe, 3)
            pe.wait_ge(S("qx_taken"), 4)

            def xa_scores(t):
                if t >= 2:
                    pe.wait_ge(S("mem_exp"), t - 1)
                for h in range(XA_HEADS):
                    r = XA_DIM * (h % 2)
                    b = 2 * (h % 2) + h // 2
                    last = nc.tensor.matmul(pair[t % 2][:, b * MEM:(b + 1) * MEM],
                                            qF[r:r + XA_DIM, h // 2, t * P:(t + 1) * P], kF[r:r + XA_DIM, h // 2],
                                            start=True, stop=True)
                last.then_inc(S("mem_scores"), 1)

            xa_scores(0)
            xa_scores(1)
            for t in range(NT):
                if t + 2 < NT:
                    xa_scores(t + 2)
                pe.wait_ge(S("mem_probs"), t + 1)
                if t >= 1:
                    pe.wait_ge(S("probs_t_taken"), t)
                for n in range(8):
                    last = nc.tensor.transpose(pair[2][:, n * P:(n + 1) * P], ex[t % 2][:, n * P:(n + 1) * P], ident)
                last.then_inc(S("mem_turned"), 1)
                if t % 4 == 3:
                    pe.wait_ge(S("probs_t_taken"), t + 1)
                    if t == 7:
                        pe.wait_ge(S("yx_ready"), 2)
                    for f in range(2):
                        for a in range(2):
                            h = 2 * f + a
                            for m in range(2):
                                last = nc.tensor.matmul(pair[3][XA_DIM * a:XA_DIM * a + XA_DIM, f * HALF:(f + 1) * HALF],
                                                        vM[:, m, h * XA_DIM:(h + 1) * XA_DIM], pT[:, 2 * (2 * a + f) + m],
                                                        start=(m == 0), stop=(m == 1))
                        last.then_inc(S("xa_out"), 1)
            slot_ready(pe, 0)
            slot_ready(pe, 1)
            pe.wait_ge(S("yx_ready"), 4)
            for t in range(NT + 1):
                if t < NT:
                    if t >= 2:
                        pe.wait_ge(S("xr_added"), t - 1)
                    for c in range(2):
                        last = products(pair[t % 2][:, c * HALF:(c + 1) * HALF],
                                        [(regB[:, k, t * P:(t + 1) * P], ring[:, c, k]) for k in range(KT)])
                    last.then_inc(S("o_rows_ready"), 1)
                if t >= 1:
                    pe.wait_ge(S("rows_normed"), t)
                    if t >= 3:
                        pe.wait_ge(S("rows_taken"), t - 2)
                    for k in range(KT):
                        last = nc.tensor.transpose(pair[2 + (t - 1) % 2][:, k * P:(k + 1) * P],
                                                   hx[(t - 1) % 2][:, k * P:(k + 1) * P], ident)
                    last.then_inc(S("rows_turned"), 1)
            slot_done(pe, 0)
            slot_done(pe, 1)

            with pe.Fori(0, KT // 2) as i:
                for par in range(2):
                    b = i * 2 + par
                    w = ring[:, 2 + par].rearrange("p k n -> p (k n)")
                    pe.wait_ge(slot_full[2 + par], LOADED * (used[2 + par] + 1) + i * LOADED)
                    pe.wait_ge(S("lru_w_full%d" % par), i * 32 + 32)
                    pe.wait_ge(S("rows_taken"), NT)
                    pe.wait_ge(S("lin_taken"), b + 1)
                    for m in range(2):
                        if m == 1:
                            pe.wait_ge(S("gate_taken"), b + 1)
                        for c in range(2):
                            last = products(pair[m][:, c * HALF:(c + 1) * HALF],
                                            [(w[:, m * 1024 + k * P:m * 1024 + (k + 1) * P],
                                              regA[:, k, c * HALF:(c + 1) * HALF]) for k in range(KT)])
                        last.then_inc(S(("lin_ready", "gate_ready")[m]), 1)
                    pe.wait_ge(S("xc_ready"), b + 2)
                    for m in range(2):
                        pe.wait_ge(S(("r_taken", "i_taken")[m]), b + 1)
                        for c in range(2):
                            last = nc.tensor.matmul(pair[2 + m][:, c * HALF:(c + 1) * HALF],
                                                    w[:, 2048 + m * P:2048 + (m + 1) * P],
                                                    xc[par][:, c * HALF:(c + 1) * HALF], start=True, stop=True)
                        last.then_inc(S(("r_ready", "i_ready")[m]), 1)
                    pe.drain()
                    pe.sem_inc(slot_free[2 + par], 1)
            for par in range(2):
                used[2 + par] += KT // 2

            def merge(count0, slots, before):
                for m in range(KT):
                    if m % 4 == 0:
                        sw, sg = slots[m // 4]
                        slot_ready(pe, sw)
                        slot_ready(pe, sg)
                    for j, src in ((1, regA), (0, regB)):
                        if m >= 2:
                            pe.wait_ge(S("merged"), count0 + m - 1)
                        elif m == 0:
                            before[j]()
                        for c in range(2):
                            last = products(pair[2 * (m % 2) + j][:, c * HALF:(c + 1) * HALF],
                                            [(ring[:, (sw, sg)[j], k, (m % 4) * P:(m % 4 + 1) * P],
                                              src[:, k, c * HALF:(c + 1) * HALF]) for k in range(KT)])
                        last.then_inc(S(("merge_y", "merge_g")[j]), 1)
                    if m % 4 == 3:
                        slot_done(pe, sw)
                        slot_done(pe, sg)

            merge(0, ((0, 1), (2, 3)), (lambda: pe.wait_ge(S("lru_done"), KT + 1),
                                         lambda: pe.wait_ge(S("i_taken"), KT + 1)))

            def project(h, t, par):
                if t == 0:
                    pe.wait_ge(S("head_full"), h * 48 + 48)
                pe.wait_ge(S("qkv_taken"), h * 8 + t + 1)
                products(pair[2][:, 0:384],
                         [(regA[:, k, t * P:(t + 1) * P], ring[:, par].rearrange("p k n -> p (k n)")[:, k * 384:(k + 1) * 384])
                          for k in range(KT)]).then_inc(S("qkv_ready"), 1)
                if t == NT - 1:
                    pe.drain()
                    pe.sem_inc(S("head_free"), 48)

            def turn_qk(h, par, g, copied):
                pe.wait_ge(S("qk_normed"), h + 1)
                pe.wait_ge(S("qkv_taken"), copied + 1)
                if g:
                    pe.wait_ge(S("qkt_taken"), h * 4 + g)
                for n in range(4):
                    t, m = 4 * (g % 2) + n, g // 2
                    last = nc.tensor.transpose(pair[2][:, n * P:(n + 1) * P], qkv[par][:, t, m * P:(m + 1) * P], ident)
                last.then_inc(S("qk_turned"), 1)

            def scores(h, j, par):
                if j == 0:
                    pe.wait_ge(S("qkt_taken"), h * 4 + 4)
                pe.wait_ge(S("exp_done"), h * 8 + j + 1)
                n = (j + 1) * P
                for m in range(2):
                    for c in range(0, n, HALF):
                        e = min(n, c + HALF)
                        last = nc.tensor.matmul(pair[m][:, c:e], qT[par][64 * m:64 * m + 64, j * P:(j + 1) * P],
                                                kT[par][64 * m:64 * m + 64, c:e], start=True, stop=True)
                last.then_inc(S("s_ready"), 1)

            def turn_weights(h, j):
                pe.wait_ge(S("w_ready"), h * 8 + j + 2)
                pe.wait_ge(S("wt_copied"), h * 8 + j + 1)
                if j == 0:
                    pe.wait_ge(S("ot_taken"), h + 1)
                for kb in range(j + 1):
                    last = nc.tensor.transpose(pair[3][:, kb * P:(kb + 1) * P], wmix[j % 2][:, kb * P:(kb + 1) * P], ident)
                last.then_inc(S("wt_turned"), 1)

            def values(h, j):
                pe.wait_ge(S("wt_copied"), h * 8 + j + 2)
                pe.wait_ge(S("o_taken"), h * 8 + j + 1)
                if j == 0:
                    pe.wait_ge(S("v_copied"), h + 1)
                products(pair[2][:, HALF:HALF + P],
                         [(wmT[:, kb * P:(kb + 1) * P], vv[:, kb]) for kb in range(j + 1)]).then_inc(S("o_ready"), 1)

            def turn_o(h):
                pe.wait_ge(S("o_normed"), h + 1)
                for t in range(NT):
                    last = nc.tensor.transpose(pair[3][:, t * P:(t + 1) * P], obuf[:, t], ident)
                last.then_inc(S("ot_turned"), 1)

            def attend(h, par, first=False, norms=True, projects=True):
                for j in range(NT):
                    scores(h, j, par)
                    if j:
                        turn_weights(h, j - 1)
                    if projects:
                        if j > 4:
                            pe.wait_ge(S("qkt_taken"), (h + 1) * 4 + j - 4)
                        project(h + 2, j, par)
                    if j == 0 and not first:
                        turn_o(h - 1)
                    if j:
                        values(h, j - 1)
                    if j >= 4 and norms:
                        turn_qk(h + 1, 1 - par, j - 4, (h + 2) * 8 + j + 1 if projects else 8 * HEADS)
                turn_weights(h, NT - 1)
                values(h, NT - 1)

            pe.wait_ge(S("merged"), KT)
            for h in range(2):
                for t in range(NT):
                    project(h, t, h)
            for g in range(4):
                turn_qk(0, 0, g, 16)
            attend(0, 0, first=True)
            with pe.Fori(0, (HEADS - 4) // 2) as i:
                for par in (1, 0):
                    attend(pe.snap(i * 2 + (2 - par)), par)
            attend(HEADS - 3, 1)
            attend(HEADS - 2, 0, projects=False)
            attend(HEADS - 1, 1, norms=False, projects=False)
            turn_o(HEADS - 1)
            merge(KT, ((0, 1), (2, 3)), (lambda: pe.wait_ge(S("ot_taken"), HEADS + 1),
                                          lambda: pe.wait_ge(S("exp_done"), 8 * HEADS + 1)))
            for t in range(2):
                pe.wait_ge(S("mrow_normed"), t + 1)
                pe.wait_ge(S("merged"), 2 * KT)
                for k in range(KT):
                    last = nc.tensor.transpose(pair[2 + t][:, k * P:(k + 1) * P], mrow[t][:, k * P:(k + 1) * P], ident)
                last.then_inc(S("m2_turned"), 1)
            slot_ready(pe, 0)
            slot_ready(pe, 1)
            pe.wait_ge(S("merged"), 2 * KT)
            for t in range(NT + 1):
                if t < NT:
                    if t >= 2:
                        pe.wait_ge(S("rows_ready"), t - 1 + NT)
                    for c in range(2):
                        last = products(pair[t % 2][:, c * HALF:(c + 1) * HALF],
                                        [(regC[:, k, t * P:(t + 1) * P], ring[:, c, k]) for k in range(KT)])
                    last.then_inc(S("o_rows_ready"), 1)
                if t >= 1:
                    if t == 1:
                        pe.wait_ge(S("m2_taken"), 2)
                    pe.wait_ge(S("rows_normed"), NT + t)
                    if t >= 3:
                        pe.wait_ge(S("rows_taken"), t - 2 + NT)
                    for k in range(KT):
                        last = nc.tensor.transpose(pair[2 + (t - 1) % 2][:, k * P:(k + 1) * P],
                                                   hx2[(t - 1) % 2][:, k * P:(k + 1) * P], ident)
                    last.then_inc(S("rows_turned"), 1)
            slot_done(pe, 0)
            slot_done(pe, 1)

            slot_ready(pe, 2)
            slot_ready(pe, 3)
            pe.wait_ge(S("rows_ready"), 2 * NT)
            for t in range(2):
                for c in range(2):
                    last = products(pair[t][:, c * HALF:(c + 1) * HALF],
                                    [(mT2[:, k, t * P:(t + 1) * P], ring[:, 2 + c, k]) for k in range(KT)])
                last.then_inc(S("kv2_ready"), 1)
            slot_done(pe, 2)
            slot_done(pe, 3)
            slot_ready(pe, 0)
            pe.wait_ge(S("rows_taken"), 2 * NT)
            for t in range(NT):
                if t >= 2:
                    pe.wait_ge(S("q2_taken"), t - 1)
                products(pair[2 + t % 2][:, 0:HALF], [(regA[:, k, t * P:(t + 1) * P], ring[:, 0, k]) for k in range(KT)]
                         ).then_inc(S("q2_ready"), 1)
            slot_done(pe, 0)
            pe.wait_ge(once("k2_normed"), nth("k2_normed", 1))
            pe.wait_ge(S("kv2_taken"), 2)
            for h in range(MH):
                for t in range(2):
                    last = nc.tensor.transpose(pair[0][:, (2 * h + t) * P:(2 * h + t + 1) * P],
                                               kvM[t][:, h * P:(h + 1) * P], ident)
            last.then_inc(once("k2_turned"), 1)
            pe.wait_ge(S("q2_taken"), NT)
            for t in range(NT):
                pe.wait_ge(S("q2_normed"), t + 1)
                if t >= 2:
                    pe.wait_ge(S("q2t_taken"), t - 1)
                for h in range(MH):
                    last = nc.tensor.transpose(pair[2 + t % 2][:, h * P:(h + 1) * P], qM[:, t, h * P:(h + 1) * P], ident)
                last.then_inc(S("q2_turned"), 1)
            pe.wait_ge(once("k2t_taken"), nth("k2t_taken", 1))
            pe.wait_ge(S("q2t_taken"), NT)

            def xb_scores(t):
                if t >= 2:
                    pe.wait_ge(S("mem_exp"), t - 1 + NT)
                for h in range(MH):
                    last = nc.tensor.matmul(pair[t % 2][:, h * MEM:(h + 1) * MEM], qF2[:, h, t * P:(t + 1) * P],
                                            kF2[:, h], start=True, stop=True)
                last.then_inc(S("mem_scores"), 1)

            xb_scores(0)
            xb_scores(1)
            for t in range(NT):
                if t + 2 < NT:
                    xb_scores(t + 2)
                pe.wait_ge(S("mem_probs"), NT + t + 1)
                if t >= 1:
                    pe.wait_ge(S("probs_t_taken"), NT + t)
                for n in range(8):
                    last = nc.tensor.transpose(pair[2][:, n * P:(n + 1) * P], ex2[t % 2][:, n * P:(n + 1) * P], ident)
                last.then_inc(S("mem_turned"), 1)
                if t % 4 == 3:
                    pe.wait_ge(S("probs_t_taken"), NT + t + 1)
                    for h in range(MH):
                        n = MH * (t // 4) + h
                        if n >= 2:
                            pe.wait_ge(S("co_taken"), n - 1)
                        products(pair[3][:, (h % 2) * HALF:(h % 2 + 1) * HALF],
                                 [(kvM[m][:, HALF + h * P:HALF + (h + 1) * P], pT2[:, 2 * h + m]) for m in range(2)]
                                 ).then_inc(S("co_ready"), 1)
            slot_ready(pe, 3)
            pe.wait_ge(S("co_taken"), 8)
            w_co = ring[:, 3].rearrange("p k n -> p (k n)").rearrange("p (k n) -> p k n", n=D)
            for t in range(NT + 1):
                if t < NT:
                    if t >= 2:
                        pe.wait_ge(S("rows_ready"), t - 1 + 2 * NT)
                    for c in range(2):
                        last = products(pair[t % 2][:, c * HALF:(c + 1) * HALF],
                                        [(oF2[:, k, t * P:(t + 1) * P], w_co[:, k, c * HALF:(c + 1) * HALF])
                                         for k in range(MH)])
                    last.then_inc(S("o_rows_ready"), 1)
                if t >= 1:
                    pe.wait_ge(S("rows_normed"), t + 2 * NT)
                    if t >= 3:
                        pe.wait_ge(S("rows_taken"), t - 2 + 2 * NT)
                    for k in range(KT):
                        last = nc.tensor.transpose(pair[2 + (t - 1) % 2][:, k * P:(k + 1) * P],
                                                   hx3[(t - 1) % 2][:, k * P:(k + 1) * P], ident)
                    last.then_inc(S("rows_turned"), 1)
            slot_done(pe, 3)
            pe.wait_ge(S("rows_taken"), 3 * NT)
            pe.wait_ge(S("rows_ready"), 3 * NT)
            pe.wait_ge(S("vectors_in"), 64 + 224)
            for t in range(NT):
                last = products(pair[0][:, t * 36:(t + 1) * 36],
                                [(regA[:, k, t * P:(t + 1) * P], w_r[:, k]) for k in range(KT)])
            last.then_inc(once("router_done"), 1)
            pe.wait_ge(once("chosen"), nth("chosen", 1))
            pe.wait_ge(once("route_consts"), nth("route_consts", 1))
            every = slice(0, NT * EXPERTS)
            products(pair[1][:, every], [(tri, Mb[:, 0:NT].rearrange("p t e -> p (t e)")),
                                         (ones, before[:, 0:NT].rearrange("p t e -> p (t e)"))])
            last = nc.tensor.matmul(pair[1][:, HALF:HALF + EXPERTS], ones, before[:, NT], start=True, stop=True)
            last.then_inc(once("ranked"), 1)

            def w_of(par, c):
                n = D if c == 2 else HALF
                return slots6[:, par, c].rearrange("p (k n) -> p k n", n=n)

            def up(e, par):
                n16 = (e // 2) * 16 + 16 if isinstance(e, int) else e * 8 + 16 - 8 * par
                pe.wait_ge(S("xgt_ready"), e + 1)
                for c in range(2):
                    pe.wait_ge(S(f"w_full{par}{c}"), n16)
                    products(pair[par][:, c * HALF:(c + 1) * HALF], [(xgT[par][:, k], w_of(par, c)[:, k]) for k in range(KT)]
                             ).then_inc(S(("gate_done", "up_done")[c]), 1)

            def turn_product(e):
                pe.wait_ge(S("a_made"), e + 1)
                pe.wait_ge(S("xgt_ready"), e + 2)
                for k in range(4):
                    last = nc.tensor.transpose(pair[3][:, k * P:(k + 1) * P], aa[:, k * P:(k + 1) * P], ident)
                last.then_inc(S("a_turned"), 1)

            def down(e, par):
                n16 = (e // 2) * 16 + 16 if isinstance(e, int) else e * 8 + 16 - 8 * par
                pe.wait_ge(S(f"w_full{par}2"), n16)
                pe.wait_ge(S("at_ready"), e + 1)
                pe.wait_ge(S("y_taken"), e + 1)
                for c in range(2):
                    last = products(pair[2][:, c * HALF:(c + 1) * HALF],
                                    [(aT[:, k], w_of(par, 2)[:, k, c * HALF:(c + 1) * HALF]) for k in range(4)])
                last.then_inc(S("down_done"), 1)

            pe.wait_ge(once("dest_ready"), nth("dest_ready", 1))
            pe.wait_ge(S("xg_full0"), 16)
            for k in range(KT):
                last = nc.tensor.transpose(pair[3][:, k * P:(k + 1) * P], xg[0][:, k * P:(k + 1) * P], ident)
            last.then_inc(S("xg_turned"), 1)
            up(0, 0)
            pe.wait_ge(S("xg_full1"), 16)
            for k in range(KT):
                last = nc.tensor.transpose(pair[3][:, k * P:(k + 1) * P], xg[1][:, k * P:(k + 1) * P], ident)
            last.then_inc(S("xg_turned"), 1)
            turn_product(0)
            with pe.Fori(0, EXPERTS // 2 - 1) as i:
                for m in range(2):
                    e, par = pe.snap(i * 2 + (1 + m)), 1 - m
                    up(e, par)
                    pe.wait_ge(S("at_ready"), e)
                    pe.wait_ge(S(f"xg_full{1 - par}"), i * 16 + 32)
                    for k in range(KT):
                        last = nc.tensor.transpose(pair[3][:, k * P:(k + 1) * P], xg[1 - par][:, k * P:(k + 1) * P], ident)
                    last.then_inc(S("xg_turned"), 1)
                    down(e - 1, 1 - par)
                    turn_product(e)
            up(EXPERTS - 1, 1)
            down(EXPERTS - 2, 0)
            pe.wait_ge(S("a_made"), EXPERTS)
            for k in range(4):
                last = nc.tensor.transpose(pair[3][:, k * P:(k + 1) * P], aa[:, k * P:(k + 1) * P], ident)
            last.then_inc(S("a_turned"), 1)
            down(EXPERTS - 1, 1)
            pe.wait_ge(once("over_ready"), nth("over_ready", 1))
            n_over = pe.value_load(over_i[0:1, 16:17], min_val=0, max_val=OVER)
            with pe.Fori(0, OVER) as j:
                with pe.If(j < n_over):
                    pe.wait_ge(S("xg_full0"), j * 16 + 16 + 8 * EXPERTS)
                    for k in range(KT):
                        last = nc.tensor.transpose(pair[3][:, k * P:(k + 1) * P], xg[0][:, k * P:(k + 1) * P], ident)
                    last.then_inc(S("xg_turned"), 1)
                    pe.wait_ge(S("o_w_full"), j * 48 + 48)
                    pe.wait_ge(S("xgt_ready"), j + 1 + EXPERTS)
                    for c in range(2):
                        last = products(pair[0][:, c * HALF:(c + 1) * HALF],
                                        [(xgT[0][:, k], w_of(0, c)[:, k]) for k in range(KT)])
                    last.then_inc(S("up_done"), 1)
                    pe.wait_ge(S("a_made"), j + 1 + EXPERTS)
                    for k in range(4):
                        last = nc.tensor.transpose(pair[3][:, k * P:(k + 1) * P], aa[:, k * P:(k + 1) * P], ident)
                    last.then_inc(S("a_turned"), 1)
                    pe.wait_ge(S("at_ready"), j + 1 + EXPERTS)
                    for c in range(2):
                        last = products(pair[2][:, c * HALF:(c + 1) * HALF],
                                        [(aT[:, k], w_of(0, 2)[:, k, c * HALF:(c + 1) * HALF]) for k in range(4)])
                    last.then_inc(S("down_done"), 1)

        @block.scalar
        def _(act):
            for name in ("lin_taken", "gate_taken", "r_taken", "i_taken", "qkv_taken", "exp_done", "wt_copied",
                         "o_taken", "y_taken"):
                act.sem_inc(S(name), 1)
            for t in range(NT + 2):
                act.wait_ge(S("xin_turned"), t + 1)
                dst = regA[:, 4:8, t * P:(t + 1) * P] if t < NT else memT[:, 4:8, (t - NT) * P:(t - NT + 1) * P]
                nc.scalar.copy(dst, pair[t % 2][:, HALF:].rearrange("p (k n) -> p k n", n=P)
                               ).then_inc(S("xt_copied_a"), 1)
            for f in range(2):
                act.wait_ge(S("xs_ready"), f + 1)
                nc.scalar.copy(xb[:, f], pair[f]).then_inc(S("xs_taken"), 1)
            for f in range(2):
                act.wait_ge(S("xs_ready"), 3 + f)
                nc.scalar.activation(gb[:, f], pair[2 + f], ACT.Tanh, scale=0.5).then_inc(S("gb_tanh"), 1)
            act.wait_ge(once("kv_ready"), nth("kv_ready", 1))
            nc.scalar.copy(kF.rearrange("p f n -> p (f n)"), pair[0][:, 0:HALF])
            nc.scalar.copy(vM.rearrange("p f n -> p (f n)"), pair[0][:, HALF:]).then_inc(once("kv_taken"), 1)
            act.wait_ge(once("wgm_turned"), nth("wgm_turned", 1))
            nc.scalar.copy(wT.rearrange("p h t -> p (h t)"), pair[1][:, 0:HALF]).then_inc(once("wt_taken"), 1)
            act.wait_ge(once("ct_turned"), nth("ct_turned", 1))
            cre = pair[2].rearrange("p (s n) -> p s n", n=P)
            nc.scalar.copy(CT[:, :, 0], cre)
            nc.scalar.mul(CT[:, :, 1], cre, -1.0).then_inc(once("ct_ready"), 1)
            act.wait_ge(once("ct_turned"), nth("ct_turned", 2))
            nc.scalar.mul(CT[:, :, 2], pair[3].rearrange("p (s n) -> p s n", n=P), -1.0).then_inc(once("ct_ready"), 1)
            for m in range(2):
                act.wait_ge(once("bt_turned"), nth("bt_turned", m + 1))
                nc.scalar.copy(BT[:, :, m], pair[m].rearrange("p (s n) -> p s n", n=P)).then_inc(once("bt_ready"), 1)
            for f in range(2):
                act.wait_ge(S("yd_ready"), f + 1)
                nc.scalar.activation(yb[:, f], yb[:, f], ACT.Gelu_apprx_tanh).then_inc(S("yb_ready"), 1)
            for f in range(2):
                act.wait_ge(S("glu_ready"), f + 1)
                act.wait_ge(once("half_glu_b"), nth("half_glu_b", 1))
                nc.scalar.activation(rot[f], pair[f], ACT.Tanh, bias=ssmp["t4"][:, f:f + 1], scale=0.5
                                     ).then_inc(S("glu_tanh"), 1)

            for t in range(NT):
                act.wait_ge(S("v_ready"), t + 1)
                nc.scalar.activation(vg[:, t], pair[t % 2][:, 0:HALF], ACT.Gelu_apprx_tanh).then_inc(S("vg_ready"), 1)
            for h in range(GM_HEADS):
                act.wait_ge(S("branch_b"), 2)
                if h >= 2:
                    act.wait_ge(S("ya_ready"), h - 1)
                act.wait_ge(S("u_ready"), h + 1)
                nc.scalar.activation(gu[h % 2], pair[3 * h % 4], ACT.Gelu_apprx_tanh).then_inc(S("u_taken"), 1)
                act.wait_ge(S("g_ready"), h + 1)
                nc.scalar.activation(th[h % 2], pair[(3 * h + 1) % 4], ACT.Tanh, scale=0.5).then_inc(S("ga_tanh"), 1)
            for f in range(2):
                act.wait_ge(S("qx_ready"), f + 1)
                nc.scalar.copy(qF[:, f], pair[f]).then_inc(S("qx_taken"), 1)
            for f in range(2):
                act.wait_ge(S("qx_ready"), 3 + f)
                nc.scalar.activation(regB[:, 6 + f], pair[2 + f], ACT.Tanh, scale=0.5).then_inc(S("gx_tanh"), 1)
            def mem_exp_xa(t):
                act.wait_ge(S("mem_max"), t + 1)
                if t >= 2:
                    act.wait_ge(S("mem_turned"), t - 1)
                    act.wait_ge(S("mem_probs"), t - 1)
                for h in range(XA_HEADS):
                    c = slice(h * MEM, (h + 1) * MEM)
                    last = nc.scalar.activation(ex[t % 2][:, c], pair[t % 2][:, c], ACT.Exp,
                                                bias=xa_nm[t % 2][:, h:h + 1], scale=XA_DIM ** -0.5,
                                                accum_out=xa_sum[t % 2][:, h:h + 1])
                last.then_inc(S("mem_exp"), 1)

            mem_exp_xa(0)
            for t in range(NT):
                if t + 1 < NT:
                    mem_exp_xa(t + 1)
                act.wait_ge(S("mem_turned"), t + 1)
                if t == 4:
                    act.wait_ge(S("xa_out"), 2)
                nc.scalar.copy(pT[:, :, (t % 4) * P:(t % 4 + 1) * P], pair[2].rearrange("p (n c) -> p n c", c=P)
                               ).then_inc(S("probs_t_taken"), 1)
            for t in range(NT):
                act.wait_ge(S("rows_ready"), t + 1)
                if t >= 1:
                    act.wait_ge(S("rows_rms"), t)
                nc.scalar.activation(sqj, xr[t % 2], ACT.Square, accum_out=sm["ss"][:, 0:1]).then_inc(S("rows_squared"), 1)
                act.drain()

            with act.Fori(0, KT // 2) as i:
                for par in range(2):
                    b = i * 2 + par
                    act.wait_ge(S("lin_ready"), b + 1)
                    act.wait_ge(S("xc_ready"), b + 1)
                    act.wait_ge(once("xp_zeroed"), nth("xp_zeroed", 1))
                    nc.scalar.copy(xp[par][:, 3:3 + SEQ], pair[0]).then_inc(S("lin_taken"), 1)
                    act.wait_ge(S("gate_ready"), b + 1)
                    act.wait_ge(S("lru_done"), b + 1)
                    nc.scalar.activation(gg, pair[1], ACT.Gelu_apprx_tanh).then_inc(S("gate_taken"), 1)
                    pc = pcol[par]
                    act.wait_ge(S("r_ready"), b + 1)
                    nc.scalar.activation(thr, pair[2], ACT.Tanh, bias=pc[:, 5:6], scale=0.5).then_inc(S("r_taken"), 1)
                    act.wait_ge(S("i_ready"), b + 1)
                    nc.scalar.activation(thi, pair[3], ACT.Tanh, bias=pc[:, 6:7], scale=0.5).then_inc(S("i_taken"), 1)
                    act.drain()
                    nc.scalar.activation(av, thr, ACT.Exp, bias=pc[:, 7:8], scale=pc[:, 7:8])
                    nc.scalar.activation(tl, thr, ACT.Tanh, bias=pc[:, 7:8], scale=pc[:, 7:8])
                    act.drain()
                    nc.scalar.activation(sq, av, ACT.Square).then_inc(S("a_ready"), 1)
                    act.wait_ge(S("one_less"), b + 1)
                    nc.scalar.activation(sq, sq, ACT.Sqrt, scale=-1.0).then_inc(S("root_ready"), 1)

            def merge_gates(count0):
                for m in range(KT):
                    act.wait_ge(S("merge_g"), count0 + m + 1)
                    if m >= 2:
                        act.wait_ge(S("merged"), count0 + m - 1)
                    nc.scalar.activation(mth[m % 2], pair[2 * (m % 2) + 1], ACT.Tanh, scale=0.5
                                         ).then_inc(S("merge_t"), 1)

            act.wait_ge(S("lru_done"), KT + 1)
            merge_gates(0)

            def project(h, t, par):
                act.wait_ge(S("qkv_ready"), h * 8 + t + 1)
                nc.scalar.copy(qkv[par][:, t], pair[2][:, 0:384]).then_inc(S("qkv_taken"), 1)

            def squares(h, par):
                act.drain()
                wait_unless_first(act, S("qk_normed"), h)
                nc.scalar.activation(sq8, qkv[par][:, :, 0:256], ACT.Square).then_inc(S("qk_squared"), 1)

            def copy_v(h, par):
                act.drain()
                act.wait_ge(S("o_ready"), h * 8 + 1)
                nc.scalar.copy(vv, qkv[par][:, :, 256:384]).then_inc(S("v_copied"), 1)

            def take_qk(h, par, g):
                act.wait_ge(S("qk_turned"), h * 4 + g + 1)
                nc.scalar.copy((qT, kT)[g // 2][par][:, (g % 2) * HALF:(g % 2 + 1) * HALF], pair[2][:, 0:HALF]
                               ).then_inc(S("qkt_taken"), 1)

            def take_weights(h, j):
                n = (j + 1) * P
                act.wait_ge(S("wt_turned"), h * 8 + j + 1)
                act.wait_ge(S("o_ready"), h * 8 + j + 1)
                nc.scalar.copy(wmT[:, 0:n], pair[3][:, 0:n]).then_inc(S("wt_copied"), 1)

            def take_values(h, j):
                act.drain()
                act.wait_ge(S("ot_turned"), h + 1)
                act.wait_ge(S("o_ready"), h * 8 + j + 2)
                nc.scalar.copy(obuf[:, j], pair[2][:, HALF:HALF + P])
                nc.scalar.activation(junk, pair[2][:, HALF:HALF + P], ACT.Square, accum_out=ho["ss"][:, j:j + 1]
                                     ).then_inc(S("o_taken"), 1)

            def attend(h, par, norms=True, projects=True):
                for j in range(NT):
                    n = (j + 1) * P
                    if j:
                        take_weights(h, j - 1)
                    act.wait_ge(S("nm_ready"), h * 8 + j + 1)
                    act.wait_ge(S("w_ready"), h * 8 + j + 1)
                    for m in range(2):
                        last = nc.scalar.activation(e2[:, m, 0:n], pair[m][:, 0:n], ACT.Exp, bias=ho["nm"][:, m:m + 1],
                                                    scale=0.125, accum_out=ho["sum"][:, m:m + 1])
                    last.then_inc(S("exp_done"), 1)
                    if j == 0:
                        copy_v(h, par)
                        act.drain()
                    if projects:
                        project(h + 2, j, par)
                    if j == 0 and norms:
                        squares(h + 1, 1 - par)
                    if j:
                        take_values(h, j - 1)
                    if j >= 4 and norms:
                        take_qk(h + 1, 1 - par, j - 4)
                take_weights(h, NT - 1)
                take_values(h, NT - 1)

            act.wait_ge(once("lam_sums"), nth("lam_sums", 1))
            nc.scalar.activation(ho["rc"][:, 0:2], ho["rl"][:, 0:2], ACT.Exp).then_inc(once("lam_exp"), 1)
            for h in range(2):
                for t in range(NT):
                    project(h, t, h)
                if h == 0:
                    squares(0, 0)
            for g in range(4):
                take_qk(0, 0, g)
            attend(0, 0)
            with act.Fori(0, (HEADS - 4) // 2) as i:
                for par in (1, 0):
                    attend(act.snap(i * 2 + (2 - par)), par)
            attend(HEADS - 3, 1)
            attend(HEADS - 2, 0, projects=False)
            attend(HEADS - 1, 1, norms=False, projects=False)
            for t in range(2):
                act.wait_ge(S("vectors_in"), 32 + 192)
                nc.scalar.activation(ex2[t], mrow[t], ACT.Square, accum_out=cs["ss"][:, t:t + 1])
            act.drain()
            act.sem_inc(once("mrow_squared"), 1)
            merge_gates(KT)
            for t in range(NT):
                act.wait_ge(S("rows_ready"), NT + t + 1)
                if t >= 1:
                    act.wait_ge(S("rows_rms"), NT + t)
                nc.scalar.activation(sqj2, xr2[t % 2], ACT.Square, accum_out=sm["ss"][:, 0:1]).then_inc(S("rows_squared"), 1)
                act.drain()

            for t in range(2):
                act.wait_ge(S("kv2_ready"), t + 1)
                nc.scalar.copy(kvM[t], pair[t]).then_inc(S("kv2_taken"), 1)
                act.wait_ge(S("mrow_normed"), 2)
                act.drain()
                for h in range(MH):
                    last = nc.scalar.activation(jk, kvM[t][:, h * P:(h + 1) * P], ACT.Square,
                                                accum_out=cs["ss"][:, 4 * t + h:4 * t + h + 1])
                    act.drain()
                act.sem_inc(once("k2_squared"), 1)
            for t in range(NT):
                act.wait_ge(S("q2_ready"), t + 1)
                if t == 0:
                    act.wait_ge(once("k2_normed"), nth("k2_normed", 1))
                    act.wait_ge(S("rows_taken"), 2 * NT)
                for h in range(MH):
                    act.drain()
                    nc.scalar.activation(jk, pair[2 + t % 2][:, h * P:(h + 1) * P], ACT.Square,
                                         accum_out=cs["ss"][:, 4 * t + h:4 * t + h + 1])
                nc.scalar.copy(qM[:, t], pair[2 + t % 2][:, 0:HALF]).then_inc(S("q2_taken"), 1)
            act.wait_ge(once("k2_turned"), nth("k2_turned", 1))
            nc.scalar.activation(kF2.rearrange("p h m -> p (h m)"), pair[0], ACT.Copy, scale=col("ck_norm", 1)
                                 ).then_inc(once("k2t_taken"), 1)
            def mem_exp_xb(t):
                act.wait_ge(S("mem_max"), NT + t + 1)
                if t >= 2:
                    act.wait_ge(S("mem_turned"), t - 1 + NT)
                    act.wait_ge(S("mem_probs"), t - 1 + NT)
                for h in range(MH):
                    c = slice(h * MEM, (h + 1) * MEM)
                    last = nc.scalar.activation(ex2[t % 2][:, c], pair[t % 2][:, c], ACT.Exp,
                                                bias=xa_nm[t % 2][:, h:h + 1], scale=P ** -0.5,
                                                accum_out=xa_sum[t % 2][:, h:h + 1])
                last.then_inc(S("mem_exp"), 1)

            mem_exp_xb(0)
            for t in range(NT):
                if t + 1 < NT:
                    mem_exp_xb(t + 1)
                act.wait_ge(S("mem_turned"), NT + t + 1)
                if t == 4:
                    act.wait_ge(S("co_ready"), 4)
                nc.scalar.copy(pT2[:, :, (t % 4) * P:(t % 4 + 1) * P], pair[2].rearrange("p (n c) -> p n c", c=P)
                               ).then_inc(S("probs_t_taken"), 1)
                if t % 4 == 3:
                    for h in range(MH):
                        act.wait_ge(S("co_ready"), MH * (t // 4) + h + 1)
                        nc.scalar.copy(oF2[:, h, (t // 4) * HALF:(t // 4 + 1) * HALF],
                                       pair[3][:, (h % 2) * HALF:(h % 2 + 1) * HALF]).then_inc(S("co_taken"), 1)
            for t in range(NT):
                act.wait_ge(S("rows_ready"), 2 * NT + t + 1)
                if t >= 1:
                    act.wait_ge(S("rows_rms"), t + 2 * NT)
                nc.scalar.activation(sqj3, xr3[t % 2], ACT.Square, accum_out=sm["ss"][:, 0:1]).then_inc(S("rows_squared"), 1)
                act.drain()
            act.wait_ge(once("group_less_max"), nth("group_less_max", 1))
            nc.scalar.activation(grp["e"], grp["e"], ACT.Exp).then_inc(once("group_exp"), 1)
            act.wait_ge(once("second_less_first"), nth("second_less_first", 1))
            nc.scalar.activation(r8["e2"], r8["e2"], ACT.Exp).then_inc(once("second_exp"), 1)

            def gate(e, par):
                wait_unless_first(act, S("a_made"), e)
                act.wait_ge(S("gate_done"), e + 1)
                nc.scalar.activation(ga, pair[par][:, 0:HALF], ACT.Tanh, scale=0.5).then_inc(S("ga_ready"), 1)

            def take_y(e, par, n16):
                if not (isinstance(n16, int) and n16 == 0):
                    act.wait_ge(S(f"y_stored{par}"), n16)
                act.wait_ge(S("down_done"), e + 1)
                nc.scalar.copy(ys[par], pair[2]).then_inc(S("y_taken"), 1)
                act.wait_ge(S("y_taken"), e + 2)
                rows0 = e * P
                act.dma_start(y_dram[bass.ds(rows0, P), :], ys[par]).then_inc(S(f"y_stored{par}"), 16)

            act.wait_ge(once("ranked"), nth("ranked", 1))
            act.wait_ge(S("xg_turned"), 1)
            gate(0, 0)
            gate(1, 1)
            take_y(0, 0, 0)
            gate(2, 0)
            take_y(1, 1, 0)
            with act.Fori(1, EXPERTS // 2 - 1) as i:
                for m in range(2):
                    e = act.snap(i * 2 + m)
                    gate(e + 1, 1 - m)
                    take_y(e, m, i * 16)
            gate(EXPERTS - 1, 1)
            take_y(EXPERTS - 2, 0, (EXPERTS // 2 - 1) * 16)
            take_y(EXPERTS - 1, 1, (EXPERTS // 2 - 1) * 16)
            act.wait_ge(once("over_ready"), nth("over_ready", 1))
            n_over = act.value_load(over_i[0:1, 16:17], min_val=0, max_val=OVER)
            with act.Fori(0, OVER) as j:
                with act.If(j < n_over):
                    act.wait_ge(S("up_done"), j + 1 + EXPERTS)
                    nc.scalar.activation(ga, pair[0][:, 0:HALF], ACT.Tanh, scale=0.5).then_inc(S("ga_ready"), 1)
                    act.wait_ge(S("y_stored0"), j * 16 + 8 * EXPERTS)
                    act.wait_ge(S("down_done"), j + 1 + EXPERTS)
                    nc.scalar.copy(ys[0], pair[2]).then_inc(S("y_taken"), 1)

        @block.vector
        def _(v):
            for name in ("xc_ready", "lru_done", "ot_taken", "w_ready"):
                v.sem_inc(S(name), 1)
            def after(op, *a, **k):
                v.drain()
                return op(*a, **k)

            tt, ts, stt = nc.vector.tensor_tensor, nc.vector.tensor_scalar, nc.vector.scalar_tensor_tensor

            def sincos(x, c, s, tmp):
                k, y, y2, m, pc_, ps_ = tmp
                after(ts, k, x, 4.0 / TWO_PI, ROUND, ALU.mult, ALU.add)
                after(ts, k, k, ROUND, None, ALU.subtract)
                after(stt, y, k, -PI_A / 4, x, ALU.mult, ALU.add)
                after(stt, y, k, -PI_B / 4, y, ALU.mult, ALU.add)
                after(stt, y, k, -PI_C / 4, y, ALU.mult, ALU.add)
                after(tt, y2, y, y, ALU.mult)
                after(ts, pc_, y2, -1.0 / 3628800, None, ALU.mult)
                ts(ps_, y2, 1.0 / 362880, None, ALU.mult)
                for a, b in ((1.0 / 40320, -1.0 / 5040), (-1.0 / 720, 1.0 / 120), (1.0 / 24, -1.0 / 6)):
                    after(stt, pc_, pc_, a, y2, ALU.add, ALU.mult)
                    stt(ps_, ps_, b, y2, ALU.add, ALU.mult)
                after(stt, pc_, pc_, -0.5, y2, ALU.add, ALU.mult)
                stt(ps_, ps_, 1.0, y, ALU.add, ALU.mult)
                after(ts, pc_, pc_, 1.0, None, ALU.add)
                after(ts, m, k, 0.25, ROUND, ALU.mult, ALU.add)
                after(ts, m, m, ROUND, None, ALU.subtract)
                after(stt, m, m, -4.0, k, ALU.mult, ALU.add)
                after(stt, k, m, -1.0, m, ALU.mult, ALU.max)
                after(ts, y, k, -1.0, 2.0, ALU.mult, ALU.add)
                after(tt, y, y, m, ALU.mult)
                ts(k, k, -1.0, 1.0, ALU.mult, ALU.add)
                after(tt, c, pc_, k, ALU.mult)
                tt(s, ps_, k, ALU.mult)
                tt(y2, ps_, y, ALU.mult)
                tt(m, pc_, y, ALU.mult)
                after(tt, c, c, y2, ALU.subtract)
                tt(s, s, m, ALU.add)

            def exponential(dst, x, tmp, itmp):
                k, y, p = tmp
                after(ts, y, x, 88.0, -87.0, ALU.min, ALU.max)
                after(ts, k, y, float(np.log2(np.e)), ROUND, ALU.mult, ALU.add)
                after(ts, k, k, ROUND, None, ALU.subtract)
                after(stt, y, k, -LN2_A, y, ALU.mult, ALU.add)
                after(stt, y, k, -LN2_B, y, ALU.mult, ALU.add)
                after(ts, p, y, 1.0 / 5040, None, ALU.mult)
                for c in (1.0 / 720, 1.0 / 120, 1.0 / 24, 1.0 / 6, 0.5, 1.0):
                    after(stt, p, p, c, y, ALU.add, ALU.mult)
                ts(itmp, k, 127.0, float(2 ** 23), ALU.add, ALU.mult)
                after(ts, p, p, 1.0, None, ALU.add)
                after(tt, dst, p, itmp.bitcast(F32), ALU.mult)

            def rsqrt(dst, x, n):
                r, h, i, hx_ = rs[0][:, 0:n], rs[1][:, 0:n], rs[2][:, 0:n], rs[3][:, 0:n]
                after(ts, i, x.bitcast(I32), 1, None, ALU.logical_shift_right)
                after(ts, i, i, -1.0, float(0x5f3759df), ALU.mult, ALU.add)
                v.drain()
                y = i.bitcast(F32)
                ts(hx_, x, -0.5, None, ALU.mult)
                v.drain()
                for step in range(3):
                    o = dst if step == 2 else r
                    if n == 1:
                        ts(h, y, y, hx_, ALU.mult, ALU.mult)
                    else:
                        tt(h, y, y, ALU.mult)
                        after(tt, h, h, hx_, ALU.mult)
                    after(stt, o, h, 1.5, y, ALU.add, ALU.mult)
                    v.drain()
                    y = o

            def turned_with_gain(t, count0, gain, dst):
                v.wait_ge(S("rows_turned"), count0 + t + 1)
                tt(dst[:, :, t * P:(t + 1) * P], pair[2 + t % 2].rearrange("p (k n) -> p k n", n=P),
                   col(gain).unsqueeze(2).broadcast_to([P, KT, P]), ALU.mult).then_inc(S("rows_taken"), 1)

            for t in range(NT + 2):
                v.wait_ge(S("xin_turned"), t + 1)
                dst = regA[:, 0:4, t * P:(t + 1) * P] if t < NT else memT[:, 0:4, (t - NT) * P:(t - NT + 1) * P]
                nc.vector.tensor_copy(dst, pair[t % 2][:, 0:HALF].rearrange("p (k n) -> p k n", n=P)
                                      ).then_inc(S("xt_copied_v"), 1)
            v.wait_ge(once("zeroed"), nth("zeroed", 1))
            v.wait_ge(S("params_in"), PARAMS)
            nc.vector.tensor_copy(rows[96:104, :], irows[96:104, :]).then_inc(once("rows_filled"), 1)
            v.wait_ge(once("cols_turned"), nth("cols_turned", 1))
            nc.vector.tensor_copy(cols, pair[3][:, 0:P]).then_inc(once("cols_ready"), 1)
            v.drain()
            c8 = cols[:, 8:64].rearrange("p (m b) -> p m b", b=8)
            nc.vector.tensor_copy(tab8[:, 0:5], c8[:, 0:5])
            ts(tab8[:, 5:7], c8[:, 5:7], 0.5, None, ALU.mult)
            lam = col("lru_lambda")
            x, e, z, z2, pz, mx_ = (tiny[n][:, 0:KT] for n in "abcdef")
            ts(mx_, lam, -1.0, 0.0, ALU.mult, ALU.max)
            after(stt, x, lam, -1.0, lam, ALU.mult, ALU.min)
            exponential(e, x, (z, z2, pz), rs[2][:, 0:KT])
            after(ts, z, e, 2.0, None, ALU.add)
            after(nc.vector.reciprocal, z, z)
            after(tt, z, z, e, ALU.mult)
            after(tt, z2, z, z, ALU.mult)
            after(ts, pz, z2, 1.0 / 17, None, ALU.mult)
            for n in (15, 13, 11, 9, 7, 5, 3):
                after(stt, pz, pz, 1.0 / n, z2, ALU.add, ALU.mult)
            after(stt, pz, pz, 1.0, z, ALU.add, ALU.mult)
            after(stt, pz, pz, 2.0, mx_, ALU.mult, ALU.add)
            after(ts, tab8[:, 7], pz, -4.0, None, ALU.mult)
            ts(subln, col("subln", 1), 0.8, None, ALU.mult)
            for n, f in enumerate(INV_FREQ):
                ts(tiny["g"].rearrange("p (t d) -> p t d", d=8)[:, :, n], col("positions"), f, None, ALU.mult)
            v.drain()
            sincos(tiny["g"], rope_c.rearrange("p t d -> p (t d)"), rope_s.rearrange("p t d -> p (t d)"),
                   [tiny[n] for n in "abcdef"])
            q = ssmp
            v.wait_ge(S("ssm_in"), 64)
            three = [tiny[n][:, 0:ST] for n in "abc"]
            exponential(q["step"], lstep, three, rs[2][:, 0:ST])
            after(tt, q["t1"], col("lam_re"), q["step"], ALU.mult)
            exponential(q["r"], q["t1"], three, rs[2][:, 0:ST])
            after(tt, q["ang"], col("lam_im"), q["step"], ALU.mult)
            sincos(q["ang"], q["c"], q["s"], [tiny[n][:, 0:ST] for n in "abcdef"])
            after(tt, q["lr"], q["r"], q["c"], ALU.mult)
            tt(q["li"], q["r"], q["s"], ALU.mult)
            after(ts, q["lr"], q["lr"], -1.0, None, ALU.add)
            lre, lim = col("lam_re"), col("lam_im")
            after(tt, q["t1"], lre, lre, ALU.mult)
            tt(q["t2"], lim, lim, ALU.mult)
            after(tt, q["den"], q["t1"], q["t2"], ALU.add)
            after(nc.vector.reciprocal, q["den"], q["den"])
            tt(q["t1"], q["lr"], lre, ALU.mult)
            tt(q["t2"], q["li"], lim, ALU.mult)
            tt(q["t3"], q["li"], lre, ALU.mult)
            tt(q["t4"], q["lr"], lim, ALU.mult)
            after(tt, q["t1"], q["t1"], q["t2"], ALU.add)
            tt(q["t3"], q["t3"], q["t4"], ALU.subtract)
            after(tt, q["br"], q["t1"], q["den"], ALU.mult)
            tt(q["bi"], q["t3"], q["den"], ALU.mult)
            wide16 = lambda a: a.unsqueeze(2).broadcast_to([P, ST, 16])
            after(tt, b_bar[:, 0], b_raw[:, 0], wide16(q["br"]), ALU.mult)
            tt(b_bar[:, 1], b_raw[:, 1], wide16(q["br"]), ALU.mult)
            tt(b_tmp, b_raw[:, 1], wide16(q["bi"]), ALU.mult)
            after(tt, b_bar[:, 0], b_bar[:, 0], b_tmp, ALU.subtract)
            after(tt, b_tmp, b_raw[:, 0], wide16(q["bi"]), ALU.mult)
            after(tt, b_bar[:, 1], b_bar[:, 1], b_tmp, ALU.add)
            v.drain()
            for m in range(2):
                for a in range(2):
                    for j in range(4):
                        last = nc.vector.tensor_copy(
                            blockB[64 * a:64 * a + 64, j:ST:4, m, 32 * j + 16 * a:32 * j + 16 * a + 16],
                            b_bar[64 * a:64 * a + 64, m, j:ST:4])
            last.then_inc(once("bbar_placed"), 1)
            for f in range(2):
                v.wait_ge(S("gb_tanh"), f + 1)
                stt(gb[:, f], gb[:, f], 1.0, pair[2 + f], ALU.add, ALU.mult).then_inc(S("xs_taken"), 1)
            nc.vector.tensor_copy(phase[1][0], q["c"])
            nc.vector.tensor_copy(phase[1][1], q["s"])
            n = 1
            while n < 512:
                c, s = phase[n]
                after(tt, q["t1"], c, c, ALU.mult)
                tt(q["t2"], s, s, ALU.mult)
                tt(q["t3"], c, s, ALU.mult)
                after(tt, phase[2 * n][0], q["t1"], q["t2"], ALU.subtract)
                ts(phase[2 * n][1], q["t3"], 2.0, None, ALU.mult)
                n *= 2
            after(nc.vector.memset, tabc[:, :, 0:1], 1.0)
            nc.vector.memset(tabs[:, :, 0:1], 0.0)
            n = 1
            t0, t1 = rot[0].rearrange("p (s n) -> p s n", n=P), rot[1].rearrange("p (s n) -> p s n", n=P)
            while n < P:
                c, s = (x.unsqueeze(2).broadcast_to([P, ST, n]) for x in phase[n])
                tc, tsn = tabc[:, :, 0:n], tabs[:, :, 0:n]
                after(tt, t0[:, :, 0:n], tsn, s, ALU.mult)
                tt(t1[:, :, 0:n], tc, s, ALU.mult)
                tt(tabc[:, :, n:2 * n], tc, c, ALU.mult)
                tt(tabs[:, :, n:2 * n], tsn, c, ALU.mult)
                after(tt, tabc[:, :, n:2 * n], tabc[:, :, n:2 * n], t0[:, :, 0:n], ALU.subtract)
                tt(tabs[:, :, n:2 * n], tabs[:, :, n:2 * n], t1[:, :, 0:n], ALU.add)
                n *= 2
            for s in range(ST):
                if s >= 2:
                    v.wait_ge(S("h_ready"), 4 * (s - 1))
                wc, ws = wcos[s % 2], wsin[s % 2]
                after(nc.vector.tensor_copy, wc[:, 0:P], tabc[:, s])
                nc.vector.tensor_copy(ws[:, 0:P], tabs[:, s])
                for n in (128, 256, 512):
                    pc_, ps_ = phase[n][0][:, s:s + 1], phase[n][1][:, s:s + 1]
                    after(ts, rot[0][:, 0:n], ws[:, 0:n], ps_, None, ALU.mult)
                    ts(rot[1][:, 0:n], wc[:, 0:n], ps_, None, ALU.mult)
                    after(stt, wc[:, n:2 * n], wc[:, 0:n], pc_, rot[0][:, 0:n], ALU.mult, ALU.subtract)
                    stt(ws[:, n:2 * n], ws[:, 0:n], pc_, rot[1][:, 0:n], ALU.mult, ALU.add)
                v.wait_ge(S("bx_ready"), s + 1)
                after(tt, rot[0], pair[0], wc, ALU.mult)
                tt(rot[1], pair[1], ws, ALU.mult)
                tt(rot[2], pair[1], wc, ALU.mult)
                tt(rot[3], pair[0], ws, ALU.mult).then_inc(S("bx_taken"), 1)
                after(tt, rot[0], rot[0], rot[1], ALU.add)
                tt(rot[2], rot[2], rot[3], ALU.subtract)
                r = q["r"][:, s:s + 1].broadcast_to([P, SEQ])
                after(nc.vector.tensor_tensor_scan, gr[s % 2], r, rot[0], 0.0, ALU.mult, ALU.add)
                nc.vector.tensor_tensor_scan(gi[s % 2], r, rot[2], 0.0, ALU.mult, ALU.add).then_inc(S("scanned"), 1)
                if s in (4, ST - 1):
                    f = s // 4 - (s == 4)
                    v.wait_ge(S("h_used"), 4 * (4 * f + 4))
                    stt(yb[:, f], xb[:, f], cols[:, ROW["ssm_d"] + f:ROW["ssm_d"] + f + 1], pair[2 + f],
                        ALU.mult, ALU.add).then_inc(S("yd_ready"), 1)
            ts(q["t4"][:, 0:2], col("glu_b", 2), 0.5, None, ALU.mult).then_inc(once("half_glu_b"), 1)
            for f in range(2):
                v.wait_ge(S("glu_tanh"), f + 1)
                after(stt, rot[2 + f], rot[f], 1.0, yb[:, f], ALU.add, ALU.mult)
                after(stt, regB[:, 4 + f], rot[2 + f], 0.25, gb[:, f], ALU.mult, ALU.mult).then_inc(S("branch_b"), 1)
            for t in range(NT):
                v.wait_ge(S("vg_ready"), t + 1)
                for h in range(GM_HEADS):
                    nc.vector.bn_stats(gm_st[:, 4 * t + h], vg[:, t, h * P:(h + 1) * P])
            v.drain()
            for n in range(32):
                nc.vector.bn_aggr(gm_mv[:, n], gm_st[:, n])
            after(ts, tiny["a"][:, 0:32], gm_mv[:, :, 1], LN_EPS, None, ALU.add)
            rsqrt(gm_r, tiny["a"][:, 0:32], 32)
            v.wait_ge(S("vectors_in"), 32)
            for t in range(NT):
                for h in range(GM_HEADS):
                    n = 4 * t + h
                    ts(vh[:, t, h * P:(h + 1) * P], vg[:, t, h * P:(h + 1) * P], gm_mv[:, n, 0:1], gm_r[:, n:n + 1],
                       ALU.subtract, ALU.mult)
                after(tt, vh[:, t], vh[:, t], gm_g, ALU.mult)
                after(tt, vh[:, t], vh[:, t], gm_b, ALU.add).then_inc(S("vh_ready"), 1)
            for h in range(GM_HEADS):
                v.wait_ge(S("ga_tanh"), h + 1)
                after(stt, th[h % 2], th[h % 2], 1.0, pair[(3 * h + 1) % 4], ALU.add, ALU.mult).then_inc(S("g_taken"), 1)
                v.wait_ge(S("mix_ready"), h + 1)
                after(tt, mb.rearrange("p (c t) -> p c t", t=P), pair[(3 * h + 2) % 4].rearrange("p (c t) -> p c t", t=P),
                      gm_bs[:, h].unsqueeze(1).broadcast_to([P, NT, P]), ALU.add).then_inc(S("mix_taken"), 1)
                v.wait_ge(S("u_taken"), h + 1)
                tt(gu[h % 2], gu[h % 2], th[h % 2], ALU.mult)
                after(stt, regB[:, h], mb, 0.5, gu[h % 2], ALU.mult, ALU.mult).then_inc(S("ya_ready"), 1)
            for f in range(2):
                v.wait_ge(S("gx_tanh"), f + 1)
                stt(regB[:, 6 + f], regB[:, 6 + f], 1.0, pair[2 + f], ALU.add, ALU.mult).then_inc(S("qx_taken"), 1)
            def mem_max(t, count0, scale):
                v.wait_ge(S("mem_scores"), count0 + t + 1)
                after(nc.vector.tensor_reduce, sm["mx"][:, 0:4], pair[t % 2].rearrange("p (h m) -> p h m", m=MEM),
                      AX.X, ALU.max)
                after(ts, xa_nm[t % 2], sm["mx"][:, 0:4], -scale, None, ALU.mult).then_inc(S("mem_max"), 1)

            mem_max(0, 0, XA_DIM ** -0.5)
            mem_max(1, 0, XA_DIM ** -0.5)
            for t in range(NT + 1):
                if t in (4, 8):
                    for f in range(2):
                        o = regB[:, 6 + f, (t // 4 - 1) * HALF:(t // 4) * HALF]
                        v.wait_ge(S("xa_out"), 2 * (t // 4 - 1) + f + 1)
                        stt(o, pair[3][:, f * HALF:(f + 1) * HALF], 0.5, o, ALU.mult, ALU.mult).then_inc(S("yx_ready"), 1)
                if t < NT:
                    v.wait_ge(S("mem_exp"), t + 1)
                    after(nc.vector.reciprocal, sm["rc"][:, 0:4], xa_sum[t % 2])
                    p3 = ex[t % 2].rearrange("p (h m) -> p h m", m=MEM)
                    after(tt, p3, p3, sm["rc"][:, 0:4].unsqueeze(2).broadcast_to([P, XA_HEADS, MEM]), ALU.mult
                          ).then_inc(S("mem_probs"), 1)
                    if t + 2 < NT:
                        mem_max(t + 2, 0, XA_DIM ** -0.5)
            for t in range(NT + 1):
                if t < NT:
                    x = xr[t % 2]
                    v.wait_ge(S("o_rows_ready"), t + 1)
                    v.wait_ge(S(f"rows_full{t % 2}"), 16 * (t // 2 + 1))
                    stt(x, x, DN_ALPHA, pair[t % 2], ALU.mult, ALU.add).then_inc(S("xr_added"), 1)
                    v.drain()
                    for c in range(2):
                        nc.vector.bn_stats(gm_st[:, c], x[:, c * HALF:(c + 1) * HALF])
                    after(nc.vector.bn_aggr, gm_mv[:, 0], gm_st[:, 0:2])
                    after(ts, sm["v1"][:, 0:1], gm_mv[:, 0, 1:2], LN_EPS, None, ALU.add)
                    rsqrt(sm["r1"][:, 0:1], sm["v1"][:, 0:1], 1)
                    after(ts, x, x, gm_mv[:, 0, 0:1], sm["r1"][:, 0:1], ALU.subtract, ALU.mult).then_inc(S("xr_normed"), 1)
                if t >= 1:
                    turned_with_gain(t - 1, 0, "norm_mix", regA)
                if t < NT:
                    v.wait_ge(S("rows_squared"), t + 1)
                    after(ts, sm["v1"][:, 0:1], sm["ss"][:, 0:1], 1.0 / D, EPS, ALU.mult, ALU.add).then_inc(S("rows_rms"), 1)
                    rsqrt(sm["r2"][:, 0:1], sm["v1"][:, 0:1], 1)
                    if t >= 2:
                        v.wait_ge(S("rows_turned"), t - 1)
                    after(ts, hx[t % 2], xr[t % 2], sm["r2"][:, 0:1], None, ALU.mult).then_inc(S("rows_normed"), 1)
            v.wait_ge(S("rows_turned"), NT)
            for par in range(2):
                v.wait_ge(S(f"rows_stored{par}"), 16 * NT // 2)
            for n in range(2):
                last = nc.vector.memset(xp[n][:, 0:3], 0.0)
            last.then_inc(once("xp_zeroed"), 1)
            with v.Fori(0, KT // 2) as i:
                for par in range(2):
                    b = i * 2 + par
                    pc = pcol[par]
                    x, o = xp[par], xc[par]
                    v.drain()
                    nc.vector.tensor_copy(pc, tab8[:, :, bass.ds(b, 1)].rearrange("p m o -> p (m o)"))
                    v.drain()
                    v.wait_ge(S("lin_taken"), b + 2)
                    ts(o, x[:, 0:SEQ], pc[:, 1:2], pc[:, 0:1], ALU.mult, ALU.add)
                    for j in range(1, 4):
                        last = after(stt, o, x[:, j:j + SEQ], pc[:, 1 + j:2 + j], o, ALU.mult, ALU.add)
                    last.then_inc(S("xc_ready"), 1)
                    v.drain()
                    v.wait_ge(S("a_ready"), b + 1)
                    stt(sq, sq, 1.0, tl, ALU.add, ALU.mult).then_inc(S("one_less"), 1)
                    stt(thi, thi, 1.0, o, ALU.add, ALU.mult)
                    v.drain()
                    v.wait_ge(S("root_ready"), b + 1)
                    stt(thi, thi, 0.5, sq, ALU.mult, ALU.mult)
                    after(nc.vector.tensor_tensor_scan, thr, av, thi, 0.0, ALU.mult, ALU.add)
                    after(tt, regB[:, bass.ds(b, 1)].rearrange("p o n -> p (o n)"), thr, gg, ALU.mult
                          ).then_inc(S("lru_done"), 1)
            for m in range(KT):
                v.wait_ge(S("merge_y"), m + 1)
                v.wait_ge(S("merge_t"), m + 1)
                after(stt, regC[:, m], mth[m % 2], 1.0, pair[2 * (m % 2)], ALU.add, ALU.mult).then_inc(S("merged"), 1)
            v.wait_ge(S("vectors_in"), 128 + 64)
            for n in range(2):
                tt(junk[:, 64 * n:64 * n + 64], lam4[:, 2 * n], lam4[:, 2 * n + 1], ALU.mult)
            after(nc.vector.tensor_reduce, ho["rl"][:, 0:2], junk.rearrange("p (n d) -> p n d", n=2), AX.X, ALU.add
                  ).then_inc(once("lam_sums"), 1)
            v.wait_ge(once("lam_exp"), nth("lam_exp", 1))
            after(tt, neg_lam, ho["rc"][:, 1:2], ho["rc"][:, 0:1], ALU.subtract)
            after(ts, neg_lam, neg_lam, -0.2, None, ALU.add)

            def norm_qk(h, par, part):
                qk = qkv[par][:, :, 0:256].rearrange("p t (m d) -> p t m d", d=64)
                v.drain()
                if part == 0:
                    v.wait_ge(S("qk_squared"), h + 1)
                    nc.vector.tensor_reduce(hs["ss"], sq8.rearrange("p t (m d) -> p (t m) d", d=64), AX.X, ALU.add)
                    after(ts, hs["v1"], hs["ss"], 1.0 / 64, EPS, ALU.mult, ALU.add)
                    rsqrt(hs["r"], hs["v1"], 32)
                elif part == 1:
                    tt(qk, qk, hs["r"].rearrange("p (t m) -> p t m", m=4).unsqueeze(3).broadcast_to([P, NT, 4, 64]),
                       ALU.mult)
                    after(tt, qkv[par][:, :, 0:256], qkv[par][:, :, 0:256],
                          qk_gain.rearrange("p m d -> p (m d)").unsqueeze(1).broadcast_to([P, NT, 256]), ALU.mult)
                else:
                    x1, x2 = qk[:, :, :, 0:8], qk[:, :, :, 8:16]
                    c, s = (x.unsqueeze(2).broadcast_to([P, NT, 4, 8]) for x in (rope_c, rope_s))
                    tt(rope_t[0], x1, c, ALU.mult)
                    tt(rope_t[1], x2, s, ALU.mult)
                    tt(rope_t[2], x2, c, ALU.mult)
                    tt(rope_t[3], x1, s, ALU.mult)
                    after(tt, x1, rope_t[0], rope_t[1], ALU.subtract)
                    tt(x2, rope_t[2], rope_t[3], ALU.add).then_inc(S("qk_normed"), 1)

            def attend(h, par, dst=None, norms=True):
                for j in range(NT):
                    n = (j + 1) * P
                    v.wait_ge(S("s_ready"), h * 8 + j + 1)
                    nc.vector.memset(psum[0:64, 0:2, j * P + 64:(j + 1) * P], -1e30)
                    after(nc.vector.tensor_reduce, ho["mx"][:, 0:2], psum[:, 0:2, 0:n], AX.X, ALU.max)
                    after(ts, ho["nm"][:, 0:2], ho["mx"][:, 0:2], -0.125, None, ALU.mult).then_inc(S("nm_ready"), 1)
                    v.drain()
                    v.wait_ge(S("exp_done"), h * 8 + j + 2)
                    nc.vector.reciprocal(ho["rc"][:, 0:2], ho["sum"][:, 0:2])
                    after(tt, ho["rl"][:, 0:1], ho["rc"][:, 1:2], neg_lam, ALU.mult)
                    v.drain()
                    if j >= 2:
                        v.wait_ge(S("wt_turned"), h * 8 + j - 1)
                    ts(wmix[j % 2][:, 0:n], e2[:, 0, 0:n], ho["rc"][:, 0:1], None, ALU.mult)
                    after(stt, wmix[j % 2][:, 0:n], e2[:, 1, 0:n], ho["rl"][:, 0:1], wmix[j % 2][:, 0:n],
                          ALU.mult, ALU.add).then_inc(S("w_ready"), 1)
                    if j == 0 and dst is not None:
                        norm_o(h - 1)
                        take_o(h - 1, dst)
                    if 1 <= j <= 3 and norms:
                        norm_qk(h + 1, 1 - par, j - 1)

            def norm_o(h):
                v.drain()
                v.wait_ge(S("o_taken"), h * 8 + 9)
                ts(ho["v1"], ho["ss"], 1.0 / P, EPS, ALU.mult, ALU.add)
                rsqrt(ho["r"], ho["v1"], 8)
                after(tt, obuf, obuf, ho["r"].unsqueeze(2).broadcast_to([P, NT, P]), ALU.mult).then_inc(S("o_normed"), 1)

            def take_o(h, dst):
                v.wait_ge(S("ot_turned"), h + 2)
                ts(dst, pair[3], subln[:, 0:1], None, ALU.mult).then_inc(S("ot_taken"), 1)

            for part in range(3):
                norm_qk(0, 0, part)
            attend(0, 0)
            with v.Fori(0, (HEADS - 4) // 2) as i:
                for par in (1, 0):
                    h = v.snap(i * 2 + (2 - par))
                    attend(h, par, regB[:, bass.ds(v.snap(h - 1), 1)].rearrange("p o n -> p (o n)"))
            attend(HEADS - 3, 1, regB[:, HEADS - 4])
            attend(HEADS - 2, 0, regB[:, HEADS - 3])
            attend(HEADS - 1, 1, regB[:, HEADS - 2], norms=False)
            norm_o(HEADS - 1)
            take_o(HEADS - 1, regB[:, HEADS - 1])
            v.wait_ge(S("ot_turned"), HEADS + 1)
            v.drain()
            v.sem_inc(once("heads_done"), 1)
            v.wait_ge(once("mrow_squared"), nth("mrow_squared", 1))
            ts(cs["v1"][:, 0:2], cs["ss"][:, 0:2], 1.0 / D, EPS, ALU.mult, ALU.add)
            rsqrt(cs["r"][:, 0:2], cs["v1"][:, 0:2], 2)
            for t in range(2):
                after(ts, mrow[t], mrow[t], cs["r"][:, t:t + 1], None, ALU.mult).then_inc(S("mrow_normed"), 1)
            for m in range(KT):
                v.wait_ge(S("merge_y"), m + 1 + KT)
                v.wait_ge(S("merge_t"), m + 1 + KT)
                after(stt, mtmp, mth[m % 2], 1.0, pair[2 * (m % 2)], ALU.add, ALU.mult)
                after(tt, regC[:, m], regC[:, m], mtmp, ALU.add).then_inc(S("merged"), 1)
            for t in range(2):
                v.wait_ge(S("m2_turned"), t + 1)
                tt(mT2[:, :, t * P:(t + 1) * P], pair[2 + t].rearrange("p (k n) -> p k n", n=P),
                   col("norm_mem").unsqueeze(2).broadcast_to([P, KT, P]), ALU.mult).then_inc(S("m2_taken"), 1)
            for t in range(NT + 1):
                if t < NT:
                    x = xr2[t % 2]
                    v.wait_ge(S("o_rows_ready"), NT + t + 1)
                    v.wait_ge(S(f"rows_full{t % 2}"), 16 * (t // 2 + 1) + 8 * NT)
                    stt(x, pair[t % 2], 0.5, x, ALU.mult, ALU.add).then_inc(S("rows_ready"), 1)
                if t >= 1:
                    turned_with_gain(t - 1, 1 * NT, "norm_cx", regA)
                if t < NT:
                    v.wait_ge(S("rows_squared"), NT + t + 1)
                    after(ts, sm["v1"][:, 0:1], sm["ss"][:, 0:1], 1.0 / D, EPS, ALU.mult, ALU.add).then_inc(S("rows_rms"), 1)
                    rsqrt(sm["r2"][:, 0:1], sm["v1"][:, 0:1], 1)
                    if t >= 2:
                        v.wait_ge(S("rows_turned"), t - 1 + NT)
                    after(ts, hx2[t % 2], xr2[t % 2], sm["r2"][:, 0:1], None, ALU.mult).then_inc(S("rows_normed"), 1)
            v.wait_ge(once("k2_squared"), nth("k2_squared", 2))
            after(ts, cs["v1"][:, 0:8], cs["ss"][:, 0:8], 1.0 / P, EPS, ALU.mult, ALU.add)
            rsqrt(cs["r"][:, 0:8], cs["v1"][:, 0:8], 8)
            for t in range(2):
                k3 = kvM[t][:, 0:HALF].rearrange("p (h d) -> p h d", d=P)
                last = after(tt, k3, k3, cs["r"][:, 4 * t:4 * t + 4].unsqueeze(2).broadcast_to([P, MH, P]), ALU.mult)
            last.then_inc(once("k2_normed"), 1)
            v.wait_ge(S("q2_taken"), NT)
            after(ts, cs["v1"], cs["ss"], 1.0 / P, EPS, ALU.mult, ALU.add)
            rsqrt(cs["r"], cs["v1"], 32)
            for t in range(NT + 1):
                if t < NT:
                    q3 = qM[:, t].rearrange("p (h d) -> p h d", d=P)
                    after(tt, q3, q3, cs["r"][:, 4 * t:4 * t + 4].unsqueeze(2).broadcast_to([P, MH, P]), ALU.mult
                          ).then_inc(S("q2_normed"), 1)
                if t >= 1:
                    v.wait_ge(S("q2_turned"), t)
                    ts(qF2[:, :, (t - 1) * P:t * P], pair[2 + (t - 1) % 2][:, 0:HALF].rearrange("p (h n) -> p h n", n=P),
                       col("cq_norm", 1), None, ALU.mult).then_inc(S("q2t_taken"), 1)
            mem_max(0, NT, P ** -0.5)
            mem_max(1, NT, P ** -0.5)
            for t in range(NT):
                v.wait_ge(S("mem_exp"), NT + t + 1)
                after(nc.vector.reciprocal, sm["rc"][:, 0:4], xa_sum[t % 2])
                p3 = ex2[t % 2].rearrange("p (h m) -> p h m", m=MEM)
                after(tt, p3, p3, sm["rc"][:, 0:4].unsqueeze(2).broadcast_to([P, MH, MEM]), ALU.mult
                      ).then_inc(S("mem_probs"), 1)
                if t + 2 < NT:
                    mem_max(t + 2, NT, P ** -0.5)
            for t in range(NT + 1):
                if t < NT:
                    x = xr3[t % 2]
                    v.wait_ge(S("o_rows_ready"), 2 * NT + t + 1)
                    v.wait_ge(S(f"rows_full{t % 2}"), 16 * (t // 2 + 1) + 16 * NT)
                    tt(x, pair[t % 2], x, ALU.add).then_inc(S("rows_ready"), 1)
                if t >= 1:
                    turned_with_gain(t - 1, 2 * NT, "norm_ffn", regA)
                if t < NT:
                    v.wait_ge(S("rows_squared"), 2 * NT + t + 1)
                    after(ts, sm["v1"][:, 0:1], sm["ss"][:, 0:1], 1.0 / D, EPS, ALU.mult, ALU.add).then_inc(S("rows_rms"), 1)
                    rsqrt(sm["r2"][:, 0:1], sm["v1"][:, 0:1], 1)
                    if t >= 2:
                        v.wait_ge(S("rows_turned"), t - 1 + 2 * NT)
                        v.wait_ge(S(f"h3_stored{t % 2}"), 16 * (t // 2))
                    after(ts, hx3[t % 2], xr3[t % 2], sm["r2"][:, 0:1], None, ALU.mult).then_inc(S("rows_normed"), 1)
            v.wait_ge(once("router_done"), nth("router_done", 1))
            v.wait_ge(once("route_consts"), nth("route_consts", 1))
            b3 = lambda a, n: a.unsqueeze(2).broadcast_to([P, NT, n])
            after(tt, logit, pair[0][:, 0:NT * 36].rearrange("p (t n) -> p t n", n=36),
                  b_r.unsqueeze(1).broadcast_to([P, NT, 36]), ALU.add)
            gl = logit[:, :, 0:4]
            iota4 = iota_f[:, 0:4].unsqueeze(1).broadcast_to([P, NT, 4])
            iota8 = iota_f[:, 0:8].unsqueeze(1).broadcast_to([P, NT, 8])

            def first_of_max(x, mx_, eq, idx, one, iota, n):
                after(nc.vector.tensor_reduce, mx_, x, AX.X, ALU.max)
                after(tt, eq, x, b3(mx_, n), ALU.is_equal)
                after(stt, eq, eq, -100.0, iota, ALU.mult, ALU.add)
                after(nc.vector.tensor_reduce, idx, eq, AX.X, ALU.min)
                after(ts, idx, idx, 100.0, None, ALU.add)
                after(tt, one, iota, b3(idx, n), ALU.is_equal)

            first_of_max(gl, r8["gm"], grp["eq"], r8["gi"], grp["sel"], iota4, 4)
            after(tt, grp["e"], gl, b3(r8["gm"], 4), ALU.subtract).then_inc(once("group_less_max"), 1)
            v.wait_ge(once("group_exp"), nth("group_exp", 1))
            after(nc.vector.tensor_reduce, r8["gv"], grp["e"], AX.X, ALU.add)
            after(nc.vector.reciprocal, r8["gv"], r8["gv"])
            sel4 = grp["sel"].unsqueeze(3).broadcast_to([P, NT, 4, 8])
            after(tt, big, logit[:, :, 4:36].rearrange("p t (g e) -> p t g e", e=8), sel4, ALU.mult)
            after(nc.vector.tensor_reduce, el["v"], big.rearrange("p t g e -> p t e g"), AX.X, ALU.add)
            first_of_max(el["v"], r8["m1"], el["eq"], r8["i1"], el["one"], iota8, 8)
            after(stt, el["v2"], el["one"], -1e38, el["v"], ALU.mult, ALU.add)
            first_of_max(el["v2"], r8["m2"], el["eq"], r8["i1"], el["two"], iota8, 8)
            after(tt, r8["e2"], r8["m2"], r8["m1"], ALU.subtract).then_inc(once("second_less_first"), 1)
            for n, one in enumerate((el["one"], el["two"])):
                tt(M[n].rearrange("p t (g e) -> p t g e", e=8), sel4,
                   one.unsqueeze(2).broadcast_to([P, NT, 4, 8]), ALU.mult)
            after(tt, Mb, M[0], M[1], ALU.add)
            nc.vector.memset(before[:, 0], 0.0)
            for t in range(NT):
                last = after(tt, before[:, t + 1], before[:, t], Mb[:, t], ALU.add)
            last.then_inc(once("chosen"), 1)
            v.wait_ge(once("second_exp"), nth("second_exp", 1))
            after(ts, r8["w1"], r8["e2"], 1.0, None, ALU.add)
            after(nc.vector.reciprocal, r8["w1"], r8["w1"])
            after(tt, r8["t"], r8["w1"], r8["e2"], ALU.mult)
            after(tt, gate_w[:, :, 0], r8["w1"], r8["gv"], ALU.mult)
            tt(gate_w[:, :, 1], r8["t"], r8["gv"], ALU.mult)
            v.wait_ge(once("ranked"), nth("ranked", 1))
            after(nc.vector.tensor_copy, ce["n"], pair[1][:, HALF:HALF + EXPERTS])
            nc.vector.tensor_copy(rank.rearrange("p t e -> p (t e)"), pair[1][:, 0:NT * EXPERTS])
            after(ts, ce["ov"], ce["n"], float(P), None, ALU.is_gt)
            for n in range(2, SEQ // P):
                after(stt, ce["ov"], ce["n"], float(n * P), ce["ov"], ALU.is_gt, ALU.add)
            after(nc.vector.tensor_tensor_scan, ce["end"], ones[:, 0:EXPERTS], ce["ov"], 0.0, ALU.mult, ALU.add)
            after(tt, ce["off"], ce["end"], ce["ov"], ALU.subtract)
            after(ts, ce["off"], ce["off"], float(P), float(P * (EXPERTS - 1)), ALU.mult, ALU.add)
            after(stt, ce["off"], iota_f, -float(P), ce["off"], ALU.mult, ALU.add)
            after(ts, rt, rank, float(P), None, ALU.is_ge)
            after(tt, rt, rt, ce["off"].unsqueeze(1).broadcast_to([P, NT, EXPERTS]), ALU.mult)
            after(tt, rt, rt, rank, ALU.add)
            after(stt, ce["t"], iota_f, float(P), ones[:, 0:EXPERTS], ALU.mult, ALU.mult)
            after(tt, rt, rt, ce["t"].unsqueeze(1).broadcast_to([P, NT, EXPERTS]), ALU.add)
            for n in range(2):
                after(tt, M[n], M[n], rt, ALU.mult)
                after(nc.vector.tensor_reduce, r8["t"], M[n], AX.X, ALU.add)
                after(nc.vector.tensor_copy, dest_i[n], r8["t"])
            v.drain()
            v.sem_inc(once("dest_ready"), 1)
            tt(oj, ce["end"].unsqueeze(1).broadcast_to([P, OVER + 1, EXPERTS]),
               iota_f[:, 0:OVER + 1].unsqueeze(2).broadcast_to([P, OVER + 1, EXPERTS]), ALU.is_le)
            after(nc.vector.tensor_reduce, of[:, 0:16], oj, AX.X, ALU.add)
            nc.vector.tensor_copy(of[:, 16:17], ce["end"][:, EXPERTS - 1:EXPERTS])
            nc.vector.memset(of[:, 17:32], 0.0)
            after(ts, of[:, 0:16], of[:, 0:16], float(EXPERTS - 1), None, ALU.min)
            after(nc.vector.tensor_copy, over_i, of).then_inc(once("over_ready"), 1)

            gain = col("norm_ffn").unsqueeze(2).broadcast_to([P, KT, P])

            def take_rows(e, par):
                v.wait_ge(S("xg_turned"), e + 1)
                tt(xgT[par], pair[3].rearrange("p (k n) -> p k n", n=P), gain, ALU.mult).then_inc(S("xgt_ready"), 1)

            def make_product(e, par):
                v.drain()
                v.wait_ge(S("ga_ready"), e + 1)
                stt(ga, ga, 1.0, pair[par][:, 0:HALF], ALU.add, ALU.mult)
                v.drain()
                wait_unless_first(v, S("a_turned"), e)
                v.wait_ge(S("up_done"), e + 1)
                stt(aa, ga, 0.5, pair[par][:, HALF:], ALU.mult, ALU.mult).then_inc(S("a_made"), 1)

            def take_product(e):
                wait_unless_first(v, S("down_done"), e)
                v.wait_ge(S("a_turned"), e + 1)
                nc.vector.tensor_copy(aT.rearrange("p k n -> p (k n)"), pair[3][:, 0:HALF]).then_inc(S("at_ready"), 1)

            for par in range(2):
                v.wait_ge(S(f"h3_stored{par}"), 16 * NT // 2)
                v.wait_ge(S(f"rows_stored{par}"), 16 * NT // 2 + 16 * NT)
            take_rows(0, 0)
            take_rows(1, 1)
            make_product(0, 0)
            take_product(0)
            with v.Fori(0, EXPERTS // 2 - 1) as i:
                for m in range(2):
                    e, par = v.snap(i * 2 + (1 + m)), 1 - m
                    take_rows(e + 1, 1 - par)
                    make_product(e, par)
                    take_product(e)
            make_product(EXPERTS - 1, 1)
            take_product(EXPERTS - 1)
            n_over = v.value_load(over_i[0:1, 16:17], min_val=0, max_val=OVER)
            with v.Fori(0, OVER) as j:
                with v.If(j < n_over):
                    v.wait_ge(S("xg_turned"), j + 1 + EXPERTS)
                    tt(xgT[0], pair[3].rearrange("p (k n) -> p k n", n=P), gain, ALU.mult).then_inc(S("xgt_ready"), 1)
                    v.wait_ge(S("ga_ready"), j + 1 + EXPERTS)
                    stt(ga, ga, 1.0, pair[0][:, 0:HALF], ALU.add, ALU.mult)
                    after(stt, aa, ga, 0.5, pair[0][:, HALF:], ALU.mult, ALU.mult).then_inc(S("a_made"), 1)
                    v.wait_ge(S("a_turned"), j + 1 + EXPERTS)
                    nc.vector.tensor_copy(aT.rearrange("p k n -> p (k n)"), pair[3][:, 0:HALF]).then_inc(S("at_ready"), 1)
            for par in range(2):
                v.wait_ge(S(f"rows_full{par}"), 32 * NT)
            for t in range(NT):
                v.wait_ge(S(f"yg_full{t % 4}"), 32 * (t // 4 + 1))
                stt(xf[t], yg[0][t % 4], gate_w[:, t, 0:1], xf[t], ALU.mult, ALU.add)
                after(stt, xf[t], yg[1][t % 4], gate_w[:, t, 1:2], xf[t], ALU.mult, ALU.add
                      ).then_inc(S("out_ready"), 1)


def kernel(**inputs):
    import concourse.bacc as bacc
    from concourse.bass_utils import run_bass_kernel_spmd

    nc = bacc.Bacc("TRN2", target_bir_lowering=False, num_devices=1)
    arrays, tensors = {}, {}
    for name, a in inputs.items():
        a = np.ascontiguousarray(a)
        arrays[f"in_{name}_dram"] = a
        tensors[name] = nc.dram_tensor(f"in_{name}_dram", a.shape, mybir.dt.from_np(a.dtype), kind="ExternalInput").ap()
    out = nc.dram_tensor("out_0_dram", [1, SEQ, D], F32, kind="ExternalOutput").ap()
    program(nc, tensors, out)
    result = run_bass_kernel_spmd(nc, [arrays], core_ids=[0])
    return result.results[0]["out_0_dram"]
```
